# Optimizing a Trainium2 kernel written in Bass

```python
import jax, jax.numpy as jnp
from jax import lax
import numpy as np

D_MODEL = 1024
BATCH = 1
SEQ = 512
DEPTH = 2

GRID_W = 64
CTX_LEN = 256
EPS = 1e-6
F32 = jnp.float32

A_HEADS = 4
A_HEAD_DIM = 64
A_WIDTH = A_HEADS * A_HEAD_DIM
A_CHUNK = 128

B_HEADS = 8
B_NOPE = 64
B_ROPE = 32
B_QK = B_NOPE + B_ROPE
B_V = 64
B_WIDTH = B_HEADS * B_V
B_Q_RANK = 256
B_KV_RANK = 128
B_QBLOCK = 128
ROPE_THETA = 10000.0

C_HEADS = 4
C_DK = 64
C_DV = 64
C_KWIDTH = C_HEADS * C_DK
C_WIDTH = C_HEADS * C_DV
C_CHUNK = 64

D_MIX = A_WIDTH + B_WIDTH + C_WIDTH
IN_SPLITS = (A_WIDTH, A_WIDTH, B_Q_RANK, B_KV_RANK, B_ROPE, C_KWIDTH, C_KWIDTH, C_KWIDTH, C_WIDTH, C_WIDTH)
D_IN = sum(IN_SPLITS)
SPLIT_IDX = tuple(sum(IN_SPLITS[:i + 1]) for i in range(len(IN_SPLITS) - 1))

P_HEADS = 8
P_KEY_DIM = 256
P_N_KEYS = 128
P_N_EXPERTS = P_N_KEYS * P_N_KEYS
P_TOPK = 16
P_TOKEN_BLOCK = 128

kernel_name = 'hybrid_dit_gmlp_mla_hgrn2_peer'

def rmsnorm(x, w):
    xf = x.astype(F32)
    y = xf * lax.rsqrt(jnp.mean(xf * xf, axis=-1, keepdims=True) + EPS)
    return (y * w.astype(F32)).astype(x.dtype)

def modulate(x, shift, scale):
    return x * (1 + scale) + shift

def axial_rope_angles(rows):
    n_freq = B_ROPE // 4
    row = jnp.repeat(jnp.arange(rows, dtype=F32), GRID_W)
    col = jnp.tile(jnp.arange(GRID_W, dtype=F32), rows)
    inv_freq = ROPE_THETA ** (-jnp.arange(n_freq, dtype=F32) / n_freq)
    ang = jnp.stack([row[:, None] * inv_freq, col[:, None] * inv_freq], axis=1)
    return jnp.cos(ang), jnp.sin(ang)

def apply_rope(x, cos, sin):
    shp = x.shape
    xr = x.astype(F32).reshape(shp[:-1] + (2, 2, B_ROPE // 4))
    x1, x2 = xr[..., 0, :], xr[..., 1, :]
    c, s = cos[:, None], sin[:, None]
    out = jnp.stack([x1 * c - x2 * s, x2 * c + x1 * s], axis=-2)
    return out.reshape(shp).astype(x.dtype)

def chunk_gating_mlp(u, v, norm_w, w_s, b_s):
    bsz, n, _ = v.shape
    vn = rmsnorm(v.reshape(bsz, n, A_HEADS, A_HEAD_DIM), norm_w.reshape(A_HEADS, A_HEAD_DIM))
    vn = vn.reshape(bsz, n // A_CHUNK, A_CHUNK, A_HEADS, A_HEAD_DIM)
    mixed = jnp.einsum('hpq,bnqhc->bnphc', w_s, vn) + b_s.T[:, :, None]
    return u * mixed.reshape(bsz, n, A_WIDTH)

def mla_project(c_q, c_kv, k_rope, q_norm_w, w_uq, kv_norm_w, w_ukv, qn_w, kn_w, rope):
    bsz, n, _ = c_q.shape
    q = (rmsnorm(c_q, q_norm_w) @ w_uq).reshape(bsz, n, B_HEADS, B_QK)
    kv = (rmsnorm(c_kv, kv_norm_w) @ w_ukv).reshape(bsz, n, B_HEADS, B_NOPE + B_V)
    k_nope, v = kv[..., :B_NOPE], kv[..., B_NOPE:]
    k = jnp.concatenate([k_nope, jnp.broadcast_to(k_rope[:, :, None, :], (bsz, n, B_HEADS, B_ROPE))], axis=-1)
    q, k = rmsnorm(q, qn_w), rmsnorm(k, kn_w)
    if rope is not None:
        cos, sin = rope
        q = jnp.concatenate([q[..., :B_NOPE], apply_rope(q[..., B_NOPE:], cos, sin)], axis=-1)
        k = jnp.concatenate([k[..., :B_NOPE], apply_rope(k[..., B_NOPE:], cos, sin)], axis=-1)
    return q, k, v

def attend(q, k, v):
    s = jnp.einsum('bhqd,bhkd->bhqk', q.astype(F32), k.astype(F32)) * (B_QK ** -0.5)
    p = jax.nn.softmax(s, axis=-1)
    return jnp.einsum('bhqk,bhkd->bhqd', p, v.astype(F32)).astype(v.dtype)

def mla_latent(q, k, v, k_ctx, v_ctx):
    bsz, n, _, _ = q.shape
    kt = jnp.concatenate([k_ctx, k], axis=1).transpose(0, 2, 1, 3)
    vt = jnp.concatenate([v_ctx, v], axis=1).transpose(0, 2, 1, 3)
    nb = n // B_QBLOCK
    qb = q.reshape(bsz, nb, B_QBLOCK, B_HEADS, B_QK).transpose(1, 0, 3, 2, 4)
    ob = lax.map(lambda qi: attend(qi, kt, vt), qb)
    return ob.transpose(1, 0, 3, 2, 4).reshape(bsz, n, B_WIDTH)

def mla_context(q, k, v):
    bsz, n, _, _ = q.shape
    o = attend(q.transpose(0, 2, 1, 3), k.transpose(0, 2, 1, 3), v.transpose(0, 2, 1, 3))
    return o.transpose(0, 2, 1, 3).reshape(bsz, n, B_WIDTH)

def to_heads(t):
    bsz, n, _ = t.shape
    return t.reshape(bsz, n, C_HEADS, -1).transpose(0, 2, 1, 3)

def hgrn2_gates(z, lb):
    z = z.astype(F32)
    lb = lb.astype(F32)
    logf = jnp.logaddexp(jnp.log(lb), jnp.log1p(-lb) + jax.nn.log_sigmoid(z))
    k = (1.0 - lb) * jax.nn.sigmoid(-z)
    return to_heads(logf), to_heads(k)

def gla_scan(q, k, v, logf, s0):
    bsz, h, n, _ = q.shape
    nc = n // C_CHUNK

    def to_chunks(t):
        return jnp.moveaxis(t.reshape(bsz, h, nc, C_CHUNK, t.shape[-1]), 2, 0)

    incl = jnp.tril(jnp.ones((C_CHUNK, C_CHUNK), dtype=bool))

    def step(state, inp):
        qc, kc, vc, lf = inp
        b = jnp.cumsum(lf, axis=2)
        o_inter = jnp.einsum('bhtk,bhkv->bhtv', qc * jnp.exp(b), state)
        diff = jnp.where(incl[:, :, None], b[:, :, :, None, :] - b[:, :, None, :, :], -jnp.inf)
        att = jnp.einsum('bhtk,bhsk,bhtsk->bhts', qc, kc, jnp.exp(diff))
        o = o_inter + jnp.einsum('bhts,bhsv->bhtv', att, vc)
        b_last = b[:, :, -1:, :]
        state = jnp.exp(b_last[:, :, 0, :, None]) * state + jnp.einsum('bhsk,bhsv->bhkv', kc * jnp.exp(b_last - b), vc)
        return state, o

    s_final, o = lax.scan(step, s0, (to_chunks(q), to_chunks(k), to_chunks(v), to_chunks(logf)))
    return jnp.moveaxis(o, 0, 2).reshape(bsz, h, n, v.shape[-1]), s_final

def hgrn2_scan(cq, zf, zb, ci, lb_f, lb_b, s0_f, s0_b):
    dt = cq.dtype
    q = to_heads(cq.astype(F32)) * (C_DK ** -0.5)
    v = to_heads(ci.astype(F32))
    logf_f, k_f = hgrn2_gates(zf, lb_f)
    logf_b, k_b = hgrn2_gates(zb, lb_b)
    flip = lambda t: jnp.flip(t, axis=2)
    o_f, s_f = gla_scan(q, k_f, v, logf_f, s0_f)
    o_b, s_b = gla_scan(flip(q), flip(k_b), flip(v), flip(logf_b), s0_b)
    return (o_f + flip(o_b)).astype(dt), s_f, s_b

def hgrn2_readout(o, g, norm_w):
    bsz, _, n, _ = o.shape
    o = o.transpose(0, 2, 1, 3)
    g = g.reshape(bsz, n, C_HEADS, C_DV)
    return (rmsnorm(o, norm_w) * jax.nn.silu(g)).reshape(bsz, n, C_WIDTH)

def peer_route(h, w_q, sub_keys):
    t = h.shape[0]
    q = (h @ w_q).reshape(t, P_HEADS, 2, P_KEY_DIM // 2).astype(F32)
    s = jnp.einsum('thpd,hpnd->thpn', q, sub_keys.astype(F32))
    sv, si = lax.top_k(s, P_TOPK)
    cand = sv[:, :, 0, :, None] + sv[:, :, 1, None, :]
    best, ci = lax.top_k(cand.reshape(t, P_HEADS, P_TOPK * P_TOPK), P_TOPK)
    i1 = jnp.take_along_axis(si[:, :, 0], ci // P_TOPK, axis=-1)
    i2 = jnp.take_along_axis(si[:, :, 1], ci % P_TOPK, axis=-1)
    experts = (i1 * P_N_KEYS + i2).reshape(t, P_HEADS * P_TOPK)
    gates = jax.nn.softmax(best, axis=-1).reshape(t, P_HEADS * P_TOPK)
    return experts, gates

def peer(h, w_q, sub_keys, u_tab, v_tab):
    bsz, n, d = h.shape
    t = bsz * n
    hf = h.reshape(t, d)
    experts, gates = peer_route(hf, w_q, sub_keys)
    nb = t // P_TOKEN_BLOCK

    def block(args):
        hb, eb, gb = args
        a = jnp.einsum('td,tkd->tk', hb, u_tab[eb])
        w = gb.astype(hb.dtype) * jax.nn.gelu(a, approximate=False)
        return jnp.einsum('tk,tkd->td', w, v_tab[eb])

    y = lax.map(block, (hf.reshape(nb, P_TOKEN_BLOCK, d),
                        experts.reshape(nb, P_TOKEN_BLOCK, P_HEADS * P_TOPK),
                        gates.reshape(nb, P_TOKEN_BLOCK, P_HEADS * P_TOPK)))
    return y.reshape(bsz, n, d)

def setup_inputs(seed: int = 0) -> dict:
    key = jax.random.key(seed)
    ks = jax.random.split(key, 26)

    def nrm(k, shape, scale=1.0):
        return jax.random.normal(k, shape, dtype=F32) * scale

    def gain(k, shape):
        return 1.0 + 0.02 * jax.random.normal(k, shape, dtype=F32)

    return {
        'x': nrm(ks[0], (BATCH, SEQ, D_MODEL)),
        'c': nrm(ks[1], (BATCH, D_MODEL)),
        'ctx': nrm(ks[2], (BATCH, CTX_LEN, D_MODEL)),
        'c_ctx': nrm(ks[3], (D_MODEL,)),
        'ln1_w': gain(ks[4], (DEPTH, D_MODEL)),
        'ln2_w': gain(ks[5], (DEPTH, D_MODEL)),
        'w_mod': nrm(ks[6], (DEPTH, D_MODEL, 6 * D_MODEL), 0.5 * D_MODEL ** -0.5),
        'b_mod': nrm(ks[7], (DEPTH, 6 * D_MODEL), 0.02),
        'w_in': nrm(ks[8], (DEPTH, D_MODEL, D_IN), D_MODEL ** -0.5),
        'w_out': nrm(ks[9], (DEPTH, D_MIX, D_MODEL), D_MIX ** -0.5),
        'a_norm_w': gain(ks[10], (DEPTH, A_WIDTH)),
        'a_w_s': nrm(ks[11], (DEPTH, A_HEADS, A_CHUNK, A_CHUNK), A_CHUNK ** -0.5),
        'a_b_s': gain(ks[12], (DEPTH, A_HEADS, A_CHUNK)),
        'b_q_norm_w': gain(ks[13], (DEPTH, B_Q_RANK)),
        'b_w_uq': nrm(ks[14], (DEPTH, B_Q_RANK, B_HEADS * B_QK), B_Q_RANK ** -0.5),
        'b_kv_norm_w': gain(ks[15], (DEPTH, B_KV_RANK)),
        'b_w_ukv': nrm(ks[16], (DEPTH, B_KV_RANK, B_HEADS * (B_NOPE + B_V)), B_KV_RANK ** -0.5),
        'b_q_head_norm_w': gain(ks[17], (DEPTH, B_QK)),
        'b_k_head_norm_w': gain(ks[18], (DEPTH, B_QK)),
        'c_lb_logits': nrm(ks[19], (DEPTH, 2, C_KWIDTH)),
        'c_out_norm_w': gain(ks[20], (DEPTH, C_DV)),
        'p_w_q': nrm(ks[21], (DEPTH, D_MODEL, P_HEADS * P_KEY_DIM), D_MODEL ** -0.5),
        'p_sub_keys': nrm(ks[22], (DEPTH, P_HEADS, 2, P_N_KEYS, P_KEY_DIM // 2), (P_KEY_DIM // 2) ** -0.5),
        'p_u': nrm(ks[23], (DEPTH, P_N_EXPERTS, D_MODEL), D_MODEL ** -0.5),
        'p_v': nrm(ks[24], (DEPTH, P_N_EXPERTS, D_MODEL), 1.0),
    }

def reference(x, c, ctx, c_ctx, ln1_w, ln2_w, w_mod, b_mod, w_in, w_out,
              a_norm_w, a_w_s, a_b_s,
              b_q_norm_w, b_w_uq, b_kv_norm_w, b_w_ukv, b_q_head_norm_w, b_k_head_norm_w,
              c_lb_logits, c_out_norm_w,
              p_w_q, p_sub_keys, p_u, p_v):
    bsz, n_lat, _ = x.shape
    rows = n_lat // GRID_W
    rope = axial_rope_angles(rows)
    lb = jnp.cumsum(jax.nn.softmax(c_lb_logits.astype(F32), axis=0), axis=0)
    lb = lb - lb[0:1]
    silu_c = jax.nn.silu(c)
    silu_cc = jax.nn.silu(c_ctx)

    for layer in range(DEPTH):
        last = layer == DEPTH - 1
        mod = jnp.split((silu_c @ w_mod[layer] + b_mod[layer])[:, None, :], 6, axis=-1)
        mod_c = jnp.split((silu_cc @ w_mod[layer] + b_mod[layer])[None, None, :], 6, axis=-1)

        h = modulate(rmsnorm(x, ln1_w[layer]), mod[0], mod[1])
        hc = modulate(rmsnorm(ctx, ln1_w[layer]), mod_c[0], mod_c[1])
        au, av, bq, bkv, bkr, cq, cff, cfb, ci, cg = jnp.split(h @ w_in[layer], SPLIT_IDX, axis=-1)
        au_c, av_c, bq_c, bkv_c, bkr_c, cq_c, cff_c, cfb_c, ci_c, cg_c = jnp.split(hc @ w_in[layer], SPLIT_IDX, axis=-1)

        a_out = chunk_gating_mlp(au, av, a_norm_w[layer], a_w_s[layer], a_b_s[layer])

        mla_w = (b_q_norm_w[layer], b_w_uq[layer], b_kv_norm_w[layer], b_w_ukv[layer],
                 b_q_head_norm_w[layer], b_k_head_norm_w[layer])
        q_l, k_l, v_l = mla_project(bq, bkv, bkr, *mla_w, rope=rope)
        q_c, k_c, v_c = mla_project(bq_c, bkv_c, bkr_c, *mla_w, rope=None)
        b_out = mla_latent(q_l, k_l, v_l, k_c, v_c)

        zeros = jnp.zeros((bsz, C_HEADS, C_DK, C_DV), F32)
        o_c, s_f, s_b = hgrn2_scan(cq_c, cff_c, cfb_c, ci_c, lb[layer, 0], lb[layer, 1], zeros, zeros)
        o_l, _, _ = hgrn2_scan(cq, cff, cfb, ci, lb[layer, 0], lb[layer, 1], s_f, s_b)
        c_out = hgrn2_readout(o_l, cg, c_out_norm_w[layer])

        x = x + mod[2] * (jnp.concatenate([a_out, b_out, c_out], axis=-1) @ w_out[layer])
        if not last:
            a_out_c = chunk_gating_mlp(au_c, av_c, a_norm_w[layer], a_w_s[layer], a_b_s[layer])
            b_out_c = mla_context(q_c, k_c, v_c)
            c_out_c = hgrn2_readout(o_c, cg_c, c_out_norm_w[layer])
            ctx = ctx + mod_c[2] * (jnp.concatenate([a_out_c, b_out_c, c_out_c], axis=-1) @ w_out[layer])

        x = x + mod[5] * peer(modulate(rmsnorm(x, ln2_w[layer]), mod[3], mod[4]),
                              p_w_q[layer], p_sub_keys[layer], p_u[layer], p_v[layer])
        if not last:
            ctx = ctx + mod_c[5] * peer(modulate(rmsnorm(ctx, ln2_w[layer]), mod_c[3], mod_c[4]),
                                        p_w_q[layer], p_sub_keys[layer], p_u[layer], p_v[layer])
    return x


_drawn_inputs = setup_inputs


def setup_inputs(seed=0):
    import zlib

    import numpy as np

    out = dict(_drawn_inputs(seed))
    spreads = {}
    factors = {'a_norm_w': 2.968,
     'a_b_s': 3.076,
     'b_q_norm_w': 7.634,
     'b_kv_norm_w': 4.848,
     'b_q_head_norm_w': 7.867,
     'b_k_head_norm_w': 6.51,
     'c_out_norm_w': 3.658}
    for name, (base, spread) in spreads.items():
        noise = np.random.default_rng([zlib.crc32(name.encode()), seed]).standard_normal(out[name].shape)
        drawn = base * np.exp(spread * noise) if base else spread * noise
        out[name] = __import__('jax').numpy.asarray(drawn.astype(out[name].dtype))
    for name, factor in factors.items():
        out[name] = (out[name] * factor).astype(out[name].dtype)
    return out
```

```python
from collections import defaultdict
from contextlib import ExitStack

import numpy as np

import concourse.bass as bass
from concourse import mybir

P = 128
DEPTH = 2
D = 1024
KD = D // P
NCTX, NLAT = 256, 512
T = NCTX + NLAT
NTT = T // P
EPS = 1e-6
F32 = mybir.dt.float32
F32R = mybir.dt.float32r
U32 = mybir.dt.uint32
ALU = mybir.AluOpType
ACT = mybir.ActivationFunctionType
AX = mybir.AxisListType

LAT, CTX = (NCTX, NLAT, 0), (0, NCTX, 1)
BH, BN, BR, BV = 8, 64, 32, 64
BQK = BN + BR
PH, NK, TOPK = 8, 128, 16
LEVELS = (64, 32, 16, 8, 4, 2, 1)
NLB = 7
TB = 32
NTB = T // TB

MOD_TILES = DEPTH * 6 * KD
IN_TILES, OUT_TILES, WQ_TILES, EXPERT_TILES = 18, 8, 16, 256
LAYER_TILES = IN_TILES + OUT_TILES + WQ_TILES + EXPERT_TILES
N_TILES = MOD_TILES + DEPTH * LAYER_TILES
NSUPER = NK // 2
RAW, SPLIT = 2, 4
GROUPS = TB // 4

PAR = {"ln1": 0, "ln2": 8, "bqn": 16, "bkvn": 18, "qhw": 19, "khw": 20, "qrw": 21, "krw": 22, "conorm": 23}
NPAR = 24


def segs_of(layer, context_too):
    return (LAT, CTX) if context_too or layer < DEPTH - 1 else (LAT,)


class Counts:

    def __init__(self):
        self.n = defaultdict(int)
        self.i, self.rate, self.entry = None, {}, {}

    def at(self, sem, count):
        return count if self.i is None else self.i * self.rate[sem] + count

    def upto(self, sem, k=1):
        self.n[sem] += k
        return self.at(sem, self.n[sem])

    def bank(self, sem):
        return self.n[sem] % 4

    def enter(self, i, rate):
        self.i, self.rate, self.entry = i, rate, dict(self.n)

    def leave(self, count):
        for sem in list(self.n):
            gained = self.n[sem] - self.entry.get(sem, 0)
            assert not gained or gained == self.rate.get(sem), (sem, gained, self.rate.get(sem))
            self.n[sem] = self.entry.get(sem, 0) + count * gained
        self.i = None


def build_program(nc, tiles, x_in, consts, params, bmod, cond, arow, aws, bw, keys, lblog, gates, out):
    sem_ctx = ExitStack()

    def semaphore(name):
        return sem_ctx.enter_context(nc.semaphore(name))

    raw_landed = (semaphore("raw_landed0"), semaphore("raw_landed1"))
    g_stored = (semaphore("g_stored0"), semaphore("g_stored1"))
    g_landed = (semaphore("g_landed0"), semaphore("g_landed1"))
    hi_done = semaphore("hi_done")
    lo_done = semaphore("lo_done")
    tile_passed = semaphore("tile_passed")
    psum_V_full = semaphore("psum_V_full")
    psum_V_free = semaphore("psum_V_free")
    psum_A_full = semaphore("psum_A_full")
    psum_A_free = semaphore("psum_A_free")
    inputs_landed = semaphore("inputs_landed")
    act_chain = semaphore("act_chain")
    dve_chain = semaphore("dve_chain")
    cond_ready = semaphore("cond_ready")
    cond_hi = semaphore("cond_hi")
    cond_split = semaphore("cond_split")
    mod_ready = semaphore("mod_ready")
    sq_ready = semaphore("sq_ready")
    sq_used = semaphore("sq_used")
    root_ready = semaphore("root_ready")
    tmp_ready = semaphore("tmp_ready")
    hhi_ready = semaphore("hhi_ready")
    h_ready = semaphore("h_ready")
    proj_ready = semaphore("proj_ready")
    aw_landed = semaphore("aw_landed")
    av_squared = semaphore("av_squared")
    a_sums = semaphore("a_sums")
    vn_ready = semaphore("vn_ready")
    a_root = semaphore("a_root")
    f_ready = semaphore("f_ready")
    logf_ready = semaphore("logf_ready")
    e_raw = semaphore("e_raw")
    e_exp = semaphore("e_exp")
    khat_ready = semaphore("khat_ready")
    gx_exp = semaphore("gx_exp")
    khT_ready = semaphore("khT_ready")
    states_zero = semaphore("states_zero")
    state_ready = semaphore("state_ready")
    qexp_ready = semaphore("qexp_ready")
    lvl_raw = semaphore("lvl_raw")
    lvl_exp = semaphore("lvl_exp")
    qk_ready = semaphore("qk_ready")
    att_ready = semaphore("att_ready")
    att_used = semaphore("att_used")
    unit_passed = semaphore("unit_passed")
    o_raw = semaphore("o_raw")
    osq_ready = semaphore("osq_ready")
    o_root = semaphore("o_root")
    a_done = semaphore("a_done")
    c_done = semaphore("c_done")
    bw_landed = semaphore("bw_landed")
    bsq_ready = semaphore("bsq_ready")
    b_root = semaphore("b_root")
    bn_ready = semaphore("bn_ready")
    v_ready = semaphore("v_ready")
    kr_squared = semaphore("kr_squared")
    headsq = semaphore("headsq")
    head_root = semaphore("head_root")
    head_ready = semaphore("head_ready")
    scores_ready = semaphore("scores_ready")
    negmax_ready = semaphore("negmax_ready")
    exp_done = semaphore("exp_done")
    probs_ready = semaphore("probs_ready")
    pt_ready = semaphore("pt_ready")
    mix_lo = semaphore("mix_lo")
    mix_ready = semaphore("mix_ready")
    x_ready = semaphore("x_ready")
    keys_landed = semaphore("keys_landed")
    q_ready = semaphore("q_ready")
    cand_raw = semaphore("cand_raw")
    cand_exp = semaphore("cand_exp")
    sel_ready = semaphore("sel_ready")
    sel_copied = semaphore("sel_copied")
    oh_ready = semaphore("oh_ready")
    oh_passed = semaphore("oh_passed")
    gates_full = semaphore("gates_full")
    gelu_ready = semaphore("gelu_ready")
    w_ready = semaphore("w_ready")
    out_stored = semaphore("out_stored")

    at = [((nc.sbuf_base + 31) // 32) * 32]

    def place(name, shape, dt=F32, offset=None):
        size = int(np.prod(shape[1:])) * 4
        if offset is None:
            offset = at[0]
            at[0] += (size + 31) // 32 * 32
        return nc.alloc_sbuf_tensor_at(name, shape, dt, offset=offset)

    xT = place("xT", [P, KD, T])
    raw = place("raw", [P, RAW, D])
    split_hi = place("split_hi", [P, SPLIT, KD, P], F32R)
    split_lo = place("split_lo", [P, SPLIT, KD, P], F32R)
    HB = at[0]
    h_hi = place("h_hi", [P, KD, T], F32R)
    h_lo = place("h_lo", [P, KD, T], F32R)
    CW = consts.shape[1]
    cst = place("cst", [P, CW])
    mod = place("mod", [P, MOD_TILES, 2])
    modA = place("modA", [P, DEPTH, 2, KD, 2])
    par = place("par", [P, DEPTH, NPAR])
    bm = place("bm", [P, MOD_TILES])
    lb = place("lb", [P, 8, 4])
    c_raw = place("c_raw", [P, KD, 2])
    c_hi = place("c_hi", [P, KD, 2], F32R)
    c_lo = place("c_lo", [P, KD, 2], F32R)
    a_wsT = place("a_wsT", [P, 4, P])
    a_bias = place("a_bias", [P, 2, P])
    a_norm = place("a_norm", [P, 256])
    small = place("small", [P, 160])
    RB = at[0]
    assert RB + 75520 <= nc.sbuf_usable_end, (RB + 75520, nc.sbuf_usable_end)

    def in_r(name, offset, shape, dt=F32):
        assert offset + int(np.prod(shape[1:])) * 4 <= nc.sbuf_usable_end - RB, name
        return place(name, shape, dt, RB + offset)

    o = [0]

    def const(w):
        o[0] += w
        return cst[:, o[0] - w:o[0]]

    ident, ones, bones, iota = const(P), const(P), const(P), const(P)
    iota16 = const(TOPK)
    masks = const(2 * NLB * 64).rearrange("p (d l t) -> p d l t", d=2, l=NLB)
    resets = const(T + 1)
    rope_c, rope_s = const(T), const(T)
    assert o[0] == CW

    sq = in_r("sq", 0, [P, 2, T])
    root = in_r("root", 6144, [P, T])
    tmp = in_r("tmp", 9216, [P, 2, T])
    au = in_r("au", 0, [P, 2, T])
    av = in_r("av", 6144, [P, NTT, 256])
    bq = in_r("bq", 12288, [P, 2, T])
    bkv = in_r("bkv", 18432, [P, T])
    krx = in_r("krx", 21504, [P, 2, T])
    ci = in_r("ci", 27648, [P, NTT, 256])
    cq = in_r("cq", 33792, [P, 2, T])
    lf = in_r("lf", 39936, [P, 4, T])
    kk = in_r("kk", 52224, [P, 4, T])
    cg = in_r("cg", 64512, [P, 2, T])
    attm = in_r("attm", 70656, [P, 2, NLB, 64])
    attF = in_r("attF", 74240, [P, 2, P])
    attR = in_r("attR", 75264, [P, 64])
    mixF = place("mixF", [P, KD, T], F32, HB)
    HL = HB + KD * T * 4
    av_sq = place("av_sq", [P, NTT, 256], F32, HL)
    vn = place("vn", [P, NTT, 256], F32, HL + 6144)
    cb = place("cb", [P, 4, T], F32, HB + 6144)
    states = place("states", [P, 4, NTT, P], F32, HL)
    khT = place("khT", [P, NTT, 4, P], F32, HL + 12288)
    lvl_q = place("lvl_q", [P, 7, 2, P], F32, HL + 12288)
    lvl_k = in_r("lvl_k", 0, [P, 7, 2, P])
    o_sq = in_r("o_sq", 0, [P, T])
    o_rt = in_r("o_rt", 3072, [P, T])
    w_uq = in_r("w_uq", 0, [P, 2048 + 1024])
    bc = in_r("bc", 27648, [P, 4, T])
    vt = in_r("vt", 39936, [P, NTT, BH * BV])
    qn = in_r("qn", 52224, [P, 2, T])
    kn = in_r("kn", 58368, [P, 2, T])
    q_sq = in_r("q_sq", 64512, [P, T])
    k_sq = in_r("k_sq", 67584, [P, 2, T])
    b_sq = in_r("b_sq", 64512, [P, 3, T])
    q_raw = place("q_raw", [P, T], F32, HL)
    q_rot = place("q_rot", [P, T], F32, HL + 3072)
    k_raw = place("k_raw", [P, T], F32, HL + 6144)
    h_rt = place("h_rt", [P, 2, T], F32, HL + 9216)
    b_rt = place("b_rt", [P, 2, T], F32, HL + 9216)
    probs = place("probs", [P, 2, T], F32, HL + 15360)
    ptA = place("ptA", [P, T], F32, HL + 21504)
    ptB = in_r("ptB", 24576, [P, T])
    pts = (ptA, ptB)
    mix_r = in_r("mix_r", 0, [P, 2, T], F32R)
    keysT = in_r("keysT", 67328, [P, WQ_TILES, P])
    q_hp = in_r("q_hp", 8192, [P, 2, T])
    s_work = in_r("s_work", 14336, [P, NTT, P])
    sv = in_r("sv", 17408, [P, NTT, WQ_TILES, TOPK])
    si = in_r("si", 23552, [P, NTT, WQ_TILES, TOPK], U32)
    si_f = in_r("si_f", 29696, [P, NTT, WQ_TILES, TOPK])
    cand = in_r("cand", 35840, [P, PH, TOPK * TOPK])
    eq = in_r("eq", 44032, [P, P, TOPK])
    cand2 = in_r("cand2", 52224, [P, 256])
    best = in_r("best", 53248, [P, PH, TOPK])
    best_i = in_r("best_i", 53760, [P, PH, TOPK], U32)
    ab_i = in_r("ab_i", 54272, [P, 2, PH * TOPK], U32)
    ab_f = in_r("ab_f", 55296, [P, 2, PH * TOPK])
    sel = in_r("sel", 56320, [P, 3, P])
    idxT = in_r("idxT", 58112, [P, 3, T])
    onehot = in_r("onehot", 0, [P, 4, 2, 4, P])
    g_buf = in_r("g_buf", 16384, [P, 2, P, TB])
    W_hi = in_r("W_hi", 0, [P, 2, 2, T], F32R)
    W_lo = in_r("W_lo", 12288, [P, 2, 2, T], F32R)
    gel = in_r("gel", 24576, [P, 2, T])
    g_in = in_r("g_in", 30720, [P, 2, NTB, 2 * TB])

    psV = nc.alloc_psum_tensor("psV", [P, 4, 512], F32)
    psA = nc.alloc_psum_tensor("psA", [P, 4, 512], F32)

    IN0 = [MOD_TILES + l * LAYER_TILES for l in range(DEPTH)]
    OUT0 = [n + IN_TILES for n in IN0]
    WQ0 = [n + OUT_TILES for n in OUT0]
    EX0 = [n + WQ_TILES for n in WQ0]
    uq = w_uq[:, 0:1536].rearrange("p (k n) -> p k n", k=2)
    uqr = w_uq[:, 1536:2048].rearrange("p (k n) -> p k n", k=2)
    ukv = w_uq[:, 2048:3072]
    chunk_f = list(range(NTT))
    chunk_b = [1, 0] + list(range(NTT - 1, 1, -1))

    block = sem_ctx.enter_context(nc.Block())

    score_bank = [[] for _ in range(DEPTH)]

    @block.tensor
    def _(pe):
        seen = Counts()
        tile_n = [0]
        passed = [0]

        def mm(out_, lhsT, rhs, start, stop, last=False):
            ins = nc.tensor.matmul(out_, lhsT, rhs, start=start, stop=stop)
            if passed[0] and not last:
                ins.then_inc(tile_passed, passed[0])
                passed[0] = 0
            return ins

        def next_tile():
            n = tile_n[0]
            tile_n[0] += 1
            pe.wait_ge(hi_done, seen.upto(hi_done))
            pe.wait_ge(lo_done, seen.upto(lo_done))
            return n % SPLIT

        def three(out_, a_hi, a_lo, b_hi, b_lo, start, stop):
            mm(out_, a_hi, b_hi, start, False)
            mm(out_, a_hi, b_lo, False, False)
            return mm(out_, a_lo, b_hi, False, stop, last=stop)

        def feature_tile(ring, segs, banks=2):
            w = next_tile()
            ps, full, free = (psA, psum_A_full, psum_A_free) if ring == "A" else (psV, psum_V_full, psum_V_free)
            f = seen.bank(free)
            pe.wait_ge(free, seen.upto(free, banks))
            for b, (s, n, _) in enumerate(segs):
                for c in range(KD):
                    ins = three(ps[:, f + b, 0:n], split_hi[:, w, c], split_lo[:, w, c],
                                h_hi[:, c, s:s + n], h_lo[:, c, s:s + n], c == 0, c == KD - 1)
            ins.then_inc(full, banks)
            passed[0] += 1

        def token_tile(segs):
            w = next_tile()
            f = seen.bank(psum_A_free)
            pe.wait_ge(psum_A_free, seen.upto(psum_A_free, 2))
            for b, (s, n, _) in enumerate(segs):
                for t in range(n // P):
                    tok = slice(s + t * P, s + (t + 1) * P)
                    for c in range(KD):
                        ins = three(psA[:, f + b, t * P:(t + 1) * P], h_hi[:, c, tok], h_lo[:, c, tok],
                                    split_hi[:, w, c], split_lo[:, w, c], c == 0, c == KD - 1)
            ins.then_inc(psum_A_full, 2)
            passed[0] += 1

        def sum_rows(segs, matrix, src, steps=1, rows=P):
            f = seen.bank(psum_A_free)
            pe.wait_ge(psum_A_free, seen.upto(psum_A_free, 2))
            for b, (s, n, _) in enumerate(segs):
                for k in range(steps):
                    ins = mm(psA[0:rows, f + b, 0:n], matrix, src(k)[:, s:s + n], k == 0, k == steps - 1,
                             last=k == steps - 1)
            ins.then_inc(psum_A_full, 2)

        def modulation(n0):
            f = seen.bank(psum_V_free)
            pe.wait_ge(psum_V_free, seen.upto(psum_V_free, 4))
            for j in range(8):
                w = next_tile()
                for c in range(KD):
                    ins = three(psV[:, f, 2 * j:2 * j + 2], split_hi[:, w, c], split_lo[:, w, c],
                                c_hi[:, c], c_lo[:, c], c == 0, c == KD - 1)
                passed[0] += 1
            ins.then_inc(psum_V_full, 4)

        def norm(l, which):
            segs = segs_of(l, which == 0)
            f = seen.bank(psum_A_free)
            pe.wait_ge(psum_A_free, seen.upto(psum_A_free, 2))
            for k in range(KD):
                pe.wait_ge(sq_ready, seen.upto(sq_ready))
                for b, (s, n, _) in enumerate(segs):
                    ins = mm(psA[:, f + b, 0:n], ones, sq[:, k % 2, s:s + n], k == 0, k == KD - 1,
                             last=b == len(segs) - 1)
                if k < KD - 2:
                    ins.then_inc(sq_used, 1)
            ins.then_inc(psum_A_full, 2)
            pe.wait_ge(h_ready, seen.upto(h_ready, KD))

        def in_projection(l):
            own, both = segs_of(l, False), segs_of(l, True)
            for t in range(IN_TILES):
                if t < 14:
                    feature_tile("A", both if t in (4, 5) or 8 <= t < 12 else own)
                else:
                    token_tile(own if t < 16 else both)

        def gated_mlp(l):
            segs = segs_of(l, False)
            pe.wait_ge(vn_ready, seen.upto(vn_ready))
            pe.wait_ge(aw_landed, seen.upto(aw_landed, 48))
            for hp in range(2):
                f = seen.bank(psum_V_free)
                pe.wait_ge(psum_V_free, seen.upto(psum_V_free, 2))
                for b, (s, n, _) in enumerate(segs):
                    for t in range(n // P):
                        tt = s // P + t
                        for hd in range(2):
                            h = 2 * hp + hd
                            ins = mm(psV[64 * hd:64 * hd + 64, f + b, t * P:(t + 1) * P], vn[:, tt, 64 * h:64 * h + 64],
                                     a_wsT[:, h], True, True, last=hd == 1)
                ins.then_inc(psum_V_full, 2)

        def hgrn(l):
            own = segs_of(l, False)
            pe.wait_ge(khat_ready, seen.upto(khat_ready))
            for tt in range(NTT):
                f = seen.bank(psum_A_free)
                pe.wait_ge(psum_A_free, seen.upto(psum_A_free, 2))
                for dt in range(4):
                    ins = nc.tensor.transpose(psA[:, f, dt * P:(dt + 1) * P], lf[:, dt, tt * P:(tt + 1) * P], ident)
                ins.then_inc(psum_A_full, 2)
            pe.wait_ge(khT_ready, seen.upto(khT_ready))
            for i in range(NTT - 1):
                f = seen.bank(psum_V_free)
                pe.wait_ge(psum_V_free, seen.upto(psum_V_free, 2))
                for d in range(2):
                    c = (chunk_f, chunk_b)[d][i]
                    for t in range(2):
                        dt = 2 * d + t
                        ins = mm(psV[:, f, dt * P:(dt + 1) * P], khT[:, c, dt], ci[:, c, t * P:(t + 1) * P],
                                 True, True, last=dt == 3)
                ins.then_inc(psum_V_full, 2)
            pe.wait_ge(qexp_ready, seen.upto(qexp_ready))
            pe.wait_ge(state_ready, seen.upto(state_ready))
            for hp in range(2):
                for s, n, _ in own:
                    fo = seen.bank(psum_A_free)
                    pe.wait_ge(psum_A_free, seen.upto(psum_A_free, 2))
                    for t in range(n // P):
                        tt = s // P + t
                        c0 = tt * P
                        pe.wait_ge(qk_ready, seen.upto(qk_ready))
                        for hd in range(2):
                            r = slice(64 * hd, 64 * hd + 64)
                            f = seen.bank(psum_V_free)
                            pe.wait_ge(psum_V_free, seen.upto(psum_V_free, 2))
                            for d in range(2):
                                for half in range(2):
                                    hs = slice(64 * half, 64 * half + 64)
                                    cs = slice(c0 + 64 * half, c0 + 64 * half + 64)
                                    for li in range(1, NLB):
                                        mm(psV[hs, f + d, (li - 1) * 64:li * 64], lvl_k[r, li, d, hs],
                                           lvl_q[r, li, d, hs], True, True)
                                    mm(psV[hs, f + d, 384:448], kk[r, 2 * d + hp, cs], cq[r, hp, cs], True, True)
                                a, b = (slice(0, 64), slice(64, 128)) if d == 0 else (slice(64, 128), slice(0, 64))
                                ins = mm(psV[a, f + d, 448:512], lvl_k[r, 0, d, a], lvl_q[r, 0, d, b], True, True,
                                         last=d == 1)
                            ins.then_inc(psum_V_full, 2)
                        o_ = psA[:, fo, t * P:(t + 1) * P]
                        mm(o_, states[:, hp, tt], lf[:, hp, c0:c0 + P], True, False)
                        mm(o_, states[:, 2 + hp, tt], lf[:, 2 + hp, c0:c0 + P], False, False, last=True)\
                            .then_inc(unit_passed, 1)
                        for hd in range(2):
                            pe.wait_ge(att_ready, seen.upto(att_ready))
                            h = 2 * hp + hd
                            end = hd == 1 and t == n // P - 1
                            ins = mm(psA[64 * hd:64 * hd + 64, fo, t * P:(t + 1) * P], ci[:, tt, h * 64:(h + 1) * 64],
                                     attF[:, hd], False, True, last=True)
                            if end:
                                ins.then_inc(psum_A_full, 2)
                                pe.wait_ge(psum_A_full, seen.n[psum_A_free])
                                pe.sem_inc(att_used, 1)
                            else:
                                ins.then_inc(att_used, 1)
            for hp in range(2):
                pe.wait_ge(osq_ready, seen.upto(osq_ready))
                sum_rows(own, bones, lambda k: o_sq)

        def attention(l):
            own, both = segs_of(l, False), segs_of(l, True)
            pe.wait_ge(c_done, seen.upto(c_done))
            pe.wait_ge(bw_landed, seen.upto(bw_landed, 16))
            pe.wait_ge(bsq_ready, seen.upto(bsq_ready, 2))
            sum_rows(own, ones, lambda k: b_sq[:, k], 2)
            sum_rows(both, ones, lambda k: b_sq[:, 2])
            pe.wait_ge(bn_ready, seen.upto(bn_ready))
            for tt in range(NTT):
                f = seen.bank(psum_A_free)
                pe.wait_ge(psum_A_free, seen.upto(psum_A_free, 1))
                mm(psA[:, f, :], bkv[:, tt * P:(tt + 1) * P], ukv[:, 512:1024], True, True, last=True)\
                    .then_inc(psum_A_full, 1)
            pe.wait_ge(v_ready, seen.upto(v_ready))

            def project(h):
                for s, n, _ in own:
                    f = seen.bank(psum_A_free)
                    pe.wait_ge(psum_A_free, seen.upto(psum_A_free, 2))
                    for k in range(2):
                        mm(psA[0:BQK, f, 0:n], uq[:, k, h * BQK:(h + 1) * BQK], bq[:, k, s:s + n], k == 0, k == 1)
                    for k in range(2):
                        ins = mm(psA[64:96, f + 1, 0:n], uqr[:, k, h * BR:(h + 1) * BR], bq[:, k, s:s + n],
                                 k == 0, k == 1, last=k == 1)
                    ins.then_inc(psum_A_full, 2)
                f = seen.bank(psum_A_free)
                pe.wait_ge(psum_A_free, seen.upto(psum_A_free, 2))
                for b, (s, n, _) in enumerate(both):
                    ins = mm(psA[0:BN, f + b, 0:n], ukv[:, h * BN:(h + 1) * BN], bkv[:, s:s + n], True, True, last=b == 1)
                ins.then_inc(psum_A_full, 2)
                pe.wait_ge(headsq, seen.upto(headsq))
                sum_rows(own, ones[0:BQK, 0:BQK], lambda k: q_sq[0:BQK], rows=BQK)
                sum_rows(both, ones[0:BQK, 0:BQK], lambda k: k_sq[0:BQK, h % 2], rows=BQK)

            def scores(h, s, q):
                f = seen.bank(psum_A_free)
                pe.wait_ge(psum_A_free, seen.upto(psum_A_free, 2))
                score_bank[l].append(f)
                lhsT = qn[0:BQK, h % 2, s + q * P:s + (q + 1) * P]
                cuts = ((0, 512), (512, T)) if s else ((0, P), (P, NCTX))
                for b, (a, e) in enumerate(cuts):
                    ins = mm(psA[:, f + b, 0:e - a], lhsT, kn[0:BQK, h % 2, a:e], True, True, last=True)
                    if b == 0:
                        ins.then_inc(psum_A_full, 2)
                    else:
                        ins.then_inc(scores_ready, 1)

            def transpose(u, s):
                pe.wait_ge(probs_ready, seen.upto(probs_ready))
                f = seen.bank(psum_A_free)
                pe.wait_ge(psum_A_free, seen.upto(psum_A_free, 2))
                for j in range(NTT if s else NCTX // P):
                    ins = nc.tensor.transpose(psA[:, f + j // 4, (j % 4) * P:(j % 4 + 1) * P],
                                              probs[:, u % 2, j * P:(j + 1) * P], ident)
                ins.then_inc(psum_A_full, 2)

            def values(h, u, s, n, q, fo):
                pe.wait_ge(pt_ready, seen.upto(pt_ready))
                nt = NTT if s else NCTX // P
                end = (q + 1) * P == n
                for j in range(nt):
                    ins = mm(psV[64 * (h % 2):64 * (h % 2) + 64, fo, q * P:(q + 1) * P], vt[:, j, h * BV:(h + 1) * BV],
                             pts[u % 2][:, j * P:(j + 1) * P], j == 0, j == nt - 1, last=end and j == nt - 1)
                if end:
                    ins.then_inc(psum_V_full, 1)

            units = [(s, n, q) for s, n, _ in own for q in range(n // P)]
            u = [0]

            def attend(h):
                fo = {}
                for s, n, _ in own:
                    fo[s] = seen.bank(psum_V_free)
                    pe.wait_ge(psum_V_free, seen.upto(psum_V_free, 1))
                scores(h, units[0][0], units[0][2])
                for i, (s, n, q) in enumerate(units):
                    if i + 1 < len(units):
                        scores(h, units[i + 1][0], units[i + 1][2])
                    if i:
                        s1, n1, q1 = units[i - 1]
                        values(h, u[0] - 1, s1, n1, q1, fo[s1])
                    transpose(u[0], s)
                    u[0] += 1
                values(h, u[0] - 1, s, n, q, fo[s])

            project(0)
            for h in range(BH):
                pe.wait_ge(head_ready, seen.upto(head_ready))
                if h + 1 < BH:
                    project(h + 1)
                attend(h)

        def out_projection(l):
            pe.wait_ge(mix_ready, seen.upto(mix_ready))
            for t in range(OUT_TILES):
                feature_tile("V", segs_of(l, False))

        def route(l):
            segs = segs_of(l, False)
            pe.wait_ge(keys_landed, seen.upto(keys_landed, 16))

            def score(t):
                pe.wait_ge(q_ready, seen.upto(q_ready))
                f = seen.bank(psum_V_free)
                pe.wait_ge(psum_V_free, seen.upto(psum_V_free, 2))
                for b, (s, n, _) in enumerate(segs):
                    for j in range(n // P):
                        ins = mm(psV[:, f + b, j * P:(j + 1) * P], q_hp[:, t % 2, s + j * P:s + (j + 1) * P],
                                 keysT[:, t], True, True, last=(j + 1) * P == n)
                ins.then_inc(psum_V_full, 2)

            for t in range(WQ_TILES):
                feature_tile("A", segs)
                if t:
                    score(t - 1)
            score(WQ_TILES - 1)
            for tt in range(segs[-1][0] // P, NTT):
                pe.wait_ge(sel_ready, seen.upto(sel_ready))
                f = seen.bank(psum_A_free)
                pe.wait_ge(psum_A_free, seen.upto(psum_A_free, 1))
                for j in range(3):
                    ins = nc.tensor.transpose(psA[:, f, j * P:(j + 1) * P], sel[:, j], ident)
                ins.then_inc(psum_A_full, 1)

        def build_gates(l):
            tb0 = 0 if l < DEPTH - 1 else NCTX // TB
            assert not passed[0]
            with pe.Fori(0, (NTB - tb0) // 2) as i:
                seen.enter(i, {oh_ready: 2 * GROUPS, psum_A_free: 2 * GROUPS})
                for g in range(2 * GROUPS):
                    pe.wait_ge(oh_ready, seen.upto(oh_ready))
                    f = seen.bank(psum_A_free)
                    pe.wait_ge(psum_A_free, seen.upto(psum_A_free, 1))
                    for j in range(4):
                        ins = mm(psA[:, f, j * P:(j + 1) * P], onehot[:, g % 4, 1, j], onehot[:, g % 4, 0, j], True, True,
                                 last=True)
                        if j == 1:
                            ins.then_inc(oh_passed, 1)
                    ins.then_inc(psum_A_full, 1)
            seen.leave((NTB - tb0) // 2)

        def experts(l):
            segs = segs_of(l, False)
            banks = len(segs)

            def apply_u():
                for c in range(2):
                    feature_tile("A", segs, banks)

            def apply_v(parity):
                w = [next_tile(), next_tile()]
                for k in range(KD):
                    f = seen.bank(psum_V_free)
                    pe.wait_ge(psum_V_free, seen.upto(psum_V_free, banks))
                    for b, (s, n, _) in enumerate(segs):
                        for c in range(2):
                            ins = three(psV[:, f + b, 0:n], split_hi[:, w[c], k], split_lo[:, w[c], k],
                                        W_hi[:, parity, c, s:s + n], W_lo[:, parity, c, s:s + n], c == 0, c == 1)
                    ins.then_inc(psum_V_full, banks)
                passed[0] += 2

            apply_u()
            apply_u()
            pe.wait_ge(w_ready, seen.upto(w_ready, 2))
            apply_v(0)
            rate = {hi_done: 8, lo_done: 8, psum_A_free: 4 * banks, psum_V_free: 16 * banks, w_ready: 4}
            with pe.Fori(0, (NSUPER - 2) // 2) as i:
                seen.enter(i, rate)
                for parity in (1, 0):
                    apply_u()
                    pe.wait_ge(w_ready, seen.upto(w_ready, 2))
                    apply_v(parity)
            seen.leave((NSUPER - 2) // 2)
            tile_n[0] = EX0[l] + EXPERT_TILES - 2
            pe.wait_ge(w_ready, seen.upto(w_ready, 2))
            apply_v(1)

        pe.wait_ge(inputs_landed, seen.upto(inputs_landed, 16 * 13))
        pe.wait_ge(cond_split, seen.upto(cond_split))
        pe.sem_inc(oh_passed, 3)
        pe.sem_inc(psum_V_free, 4)
        pe.sem_inc(psum_A_free, 4)
        modulation(0)
        with pe.Fori(0, MOD_TILES // 8 - 1) as i:
            seen.enter(i, {hi_done: 8, lo_done: 8, psum_V_free: 4})
            modulation(8)
        seen.leave(MOD_TILES // 8 - 1)
        tile_n[0] = MOD_TILES
        for l in range(DEPTH):
            norm(l, 0)
            in_projection(l)
            pe.wait_ge(proj_ready, seen.upto(proj_ready))
            gated_mlp(l)
            hgrn(l)
            attention(l)
            out_projection(l)
            norm(l, 1)
            route(l)
            build_gates(l)
            experts(l)
        pe.wait_ge(psum_V_full, seen.n[psum_V_free])

    @block.sync
    def _(sp):
        seen = Counts()

        def load(n, where=None):
            if n >= RAW:
                sp.wait_ge(hi_done, seen.at(hi_done, n - RAW + 1))
                sp.wait_ge(lo_done, seen.at(lo_done, n - RAW + 1))
            sp.dma_start(raw[:, n % RAW, :], tiles[n if where is None else where])\
               .then_inc(raw_landed[n % RAW], 16)

        def load_many(n, end):
            while n % 2 or n < RAW:
                load(n)
                n += 1
            pairs = (end - n) // 2
            with sp.Fori(0, pairs) as i:
                seen.enter(i, {hi_done: 2, lo_done: 2})
                load(n, i * 2 + n)
                load(n + 1, i * 2 + (n + 1))
            seen.leave(pairs)
            for m in range(n + 2 * pairs, end):
                load(m)

        done = 0
        for l in range(DEPTH):
            load_many(done, EX0[l] + 2 + RAW)
            done = EX0[l] + 2 + RAW
            tb0 = 0 if l < DEPTH - 1 else NCTX // TB
            with sp.Fori(0, (NTB - tb0) // 2) as i:
                seen.enter(i, {gates_full: 2})
                for b in range(2):
                    sp.wait_ge(gates_full, seen.upto(gates_full))
                    sp.dma_start(gates[i * 2 + (tb0 + b)], g_buf[:, b]).then_inc(g_stored[b], 16)
            seen.leave((NTB - tb0) // 2)
        load_many(done, N_TILES)

    @block.gpsimd
    def _(pool):
        seen = Counts()
        for k in range(KD):
            pool.dma_start(xT[:, k, :], x_in[:, k, :]).then_inc(inputs_landed, 16)
        for dst, src in ((cst[:], consts), (par[:], params), (bm[:], bmod), (c_raw[:], cond), (lb[:, 0:2, :], lblog)):
            pool.dma_start(dst, src).then_inc(inputs_landed, 16)

        def a_weights(l):
            pool.dma_start(a_wsT[:], aws[l]).then_inc(aw_landed, 16)
            pool.dma_start(a_bias[:], arow[l, :, 0:256]).then_inc(aw_landed, 16)
            pool.dma_start(a_norm[:], arow[l, :, 256:512]).then_inc(aw_landed, 16)

        a_weights(0)
        for b in range(2):
            seen.n[g_stored[b]] = 16
        for l in range(DEPTH):
            pool.wait_ge(a_done, seen.upto(a_done))
            pool.memset(states[:], 0.0).then_inc(states_zero, 1)
            if l + 1 < DEPTH:
                a_weights(l + 1)
            pool.wait_ge(c_done, seen.upto(c_done))
            pool.dma_start(w_uq[:], bw[l]).then_inc(bw_landed, 16)
            pool.wait_ge(mix_ready, seen.upto(mix_ready))
            pool.dma_start(keysT[:], keys[l]).then_inc(keys_landed, 16)
            tb0 = 0 if l < DEPTH - 1 else NCTX // TB
            for b in range(2):
                pool.wait_ge(g_stored[b], seen.upto(g_stored[b], 16 * (NTB - tb0) // 2))

            def load_gates(s, slot):
                return pool.dma_start(g_in[:, slot, tb0:NTB, :].rearrange("p b (i t) -> p b i t", i=2),
                                     gates[tb0:NTB].rearrange("b p (s i) t -> s p b i t", i=2)[s])\
                    .then_inc(g_landed[slot], 16)

            load_gates(0, 0)
            load_gates(1, 1)
            with pool.Fori(0, NSUPER // 2 - 1) as i:
                seen.enter(i, {w_ready: 4})
                for b in range(2):
                    pool.wait_ge(w_ready, seen.upto(w_ready, 2))
                    load_gates(i * 2 + (2 + b), b)
            seen.leave(NSUPER // 2 - 1)
            pool.wait_ge(w_ready, seen.upto(w_ready, 4))
        pool.wait_ge(x_ready, seen.upto(x_ready, 1 + 2 * DEPTH))
        pool.dma_start(out, xT[:, :, NCTX:T]).then_inc(out_stored, 16)
        pool.wait_ge(out_stored, 16)

    @block.scalar
    def _(act):
        seen = Counts()
        seen.n[psum_A_free] = 4
        A = nc.scalar.activation
        splits = [0]

        def split_to(end):
            while splits[0] < end:
                n = splits[0]
                splits[0] += 1
                act.wait_ge(raw_landed[n % RAW], seen.upto(raw_landed[n % RAW], 16))
                if n >= SPLIT:
                    act.wait_ge(tile_passed, seen.at(tile_passed, n - SPLIT + 1))
                A(split_hi[:, n % SPLIT].rearrange("p k n -> p (k n)"), raw[:, n % RAW, :], ACT.Copy).then_inc(hi_done, 1)
                act.wait_ge(hi_done, seen.upto(hi_done))

        def pair(f):
            return psA[:, f:f + 2, :].rearrange("p b n -> p (b n)")

        def norm(l, which):
            segs = segs_of(l, which == 0)
            t0 = segs[-1][0]
            for k in range(KD):
                if k >= 2:
                    act.wait_ge(sq_used, seen.upto(sq_used))
                A(sq[:, k % 2, t0:T], xT[:, k, t0:T], ACT.Square).then_inc(sq_ready, 1)
                act.wait_ge(sq_ready, seen.upto(sq_ready))
            f = seen.bank(psum_A_full)
            act.wait_ge(psum_A_full, seen.upto(psum_A_full, 2))
            for b, (s, n, _) in enumerate(segs):
                ins = A(root[:, s:s + n], psA[:, f + b, 0:n], ACT.Sqrt, bias=EPS_COL, scale=1.0 / D)
            ins.then_inc(psum_A_free, 2)
            act.wait_ge(psum_A_free, seen.upto(psum_A_free, 2))
            act.sem_inc(root_ready, 1)
            for k in range(KD):
                act.wait_ge(tmp_ready, seen.upto(tmp_ready))
                for s, n, j in segs:
                    shift = mod[:, l * 48 + which * 24 + k, j:j + 1]
                    ins = A(h_hi[:, k, s:s + n], tmp[:, k % 2, s:s + n], ACT.Identity, bias=shift)
                ins.then_inc(hhi_ready, 1)
                act.wait_ge(hhi_ready, seen.upto(hhi_ready))

        def copy_pair(f, segs, fn, dst, rows=slice(0, P), src_rows=None, **kw):
            src_rows = src_rows or rows
            for b, (s, n, _) in enumerate(segs):
                ins = A(dst[rows, s:s + n], psA[src_rows, f + b, 0:n], fn, **kw)
            return ins

        def in_projection(l):
            own = segs_of(l, False)
            both = segs_of(l, True)
            for t in range(IN_TILES):
                split_to(IN0[l] + t + 3)
                f = seen.bank(psum_A_full)
                act.wait_ge(psum_A_full, seen.upto(psum_A_full, 2))
                if t < 2:
                    ins = copy_pair(f, own, ACT.Copy, au[:, t])
                elif t < 4:
                    ins = copy_pair(f, own, ACT.Copy, bq[:, t - 2])
                elif t == 4:
                    ins = copy_pair(f, both, ACT.Copy, bkv[:])
                elif t == 5:
                    copy_pair(f, both, ACT.Copy, krx[:, 0], slice(64, 96))
                    ins = copy_pair(f, both, ACT.Copy, krx[:, 1], slice(64, 96), slice(96, 128))
                elif t < 8:
                    ins = copy_pair(f, own, ACT.Copy, cq[:, t - 6], scale=0.125)
                elif t < 12:
                    copy_pair(f, both, ACT.Sigmoid, lf[:, t - 8])
                    ins = copy_pair(f, both, ACT.Sigmoid, kk[:, t - 8], scale=-1.0)
                elif t < 14:
                    ins = copy_pair(f, own, ACT.Silu, cg[:, t - 12])
                else:
                    dst = (av, ci)[(t - 14) // 2]
                    c0 = (t % 2) * P
                    segs = own if t < 16 else both
                    for b, (s, n, _) in enumerate(segs):
                        ins = A(dst[:, s // P:(s + n) // P, c0:c0 + P],
                                psA[:, f + b, 0:n].rearrange("p (t c) -> p t c", c=P), ACT.Copy)
                ins.then_inc(psum_A_free, 2)
                act.wait_ge(psum_A_free, seen.upto(psum_A_free, 2))
            act.sem_inc(proj_ready, 1)

        def gated_mlp(l):
            t0 = 0 if l < DEPTH - 1 else NCTX // P
            A(av_sq[:, t0:], av[:, t0:], ACT.Square).then_inc(av_squared, 1)
            act.wait_ge(av_squared, seen.upto(av_squared))
            act.wait_ge(a_sums, seen.upto(a_sums))
            A(small[:, 24:48], small[:, 0:24], ACT.Sqrt, bias=EPS_COL, scale=1.0 / 64).then_inc(a_root, 1)
            act.wait_ge(a_root, seen.upto(a_root))

        def hgrn(l):
            own = segs_of(l, False)
            act.wait_ge(f_ready, seen.upto(f_ready))
            A(lf[:], lf[:], ACT.Ln).then_inc(logf_ready, 1)
            act.wait_ge(logf_ready, seen.upto(logf_ready))
            act.wait_ge(e_raw, seen.upto(e_raw))
            A(lf[:], lf[:], ACT.Exp, scale=-1.0).then_inc(e_exp, 1)
            act.wait_ge(e_exp, seen.upto(e_exp))
            for tt in range(NTT):
                f = seen.bank(psum_A_full)
                act.wait_ge(psum_A_full, seen.upto(psum_A_full, 2))
                A(khT[:, tt].rearrange("p d n -> p (d n)"), psA[:, f, :], ACT.Copy).then_inc(psum_A_free, 2)
                act.wait_ge(psum_A_free, seen.upto(psum_A_free, 2))
            act.sem_inc(khT_ready, 1)
            A(lf[:], cb[:], ACT.Exp).then_inc(gx_exp, 1)
            act.wait_ge(gx_exp, seen.upto(gx_exp))
            for hp in range(2):
                for s, n, _ in own:
                    for tt in range(s // P, (s + n) // P):
                        act.wait_ge(lvl_raw, seen.upto(lvl_raw))
                        A(lvl_q[:], lvl_q[:], ACT.Abs).then_inc(act_chain, 1)
                        act.wait_ge(act_chain, seen.upto(act_chain))
                        A(lvl_q[:], lvl_q[:], ACT.Exp, scale=-1.0).then_inc(lvl_exp, 1)
                        act.wait_ge(lvl_exp, seen.upto(lvl_exp))
                    f = seen.bank(psum_A_full)
                    act.wait_ge(psum_A_full, seen.upto(psum_A_full, 2))
                    A(mixF[:, 6 + hp, s:s + n], psA[:, f, 0:n], ACT.Copy).then_inc(psum_A_free, 2)
                    act.wait_ge(psum_A_free, seen.upto(psum_A_free, 2))
            t0 = own[-1][0]
            for hp in range(2):
                if hp:
                    act.wait_ge(o_raw, seen.upto(o_raw))
                A(o_sq[:, t0:T], mixF[:, 6 + hp, t0:T], ACT.Square).then_inc(osq_ready, 1)
                act.wait_ge(osq_ready, seen.upto(osq_ready))
                f = seen.bank(psum_A_full)
                act.wait_ge(psum_A_full, seen.upto(psum_A_full, 2))
                for b, (s, n, _) in enumerate(own):
                    ins = A(o_rt[:, s:s + n], psA[:, f + b, 0:n], ACT.Sqrt, bias=EPS_COL, scale=1.0 / 64)
                ins.then_inc(psum_A_free, 2)
                act.wait_ge(psum_A_free, seen.upto(psum_A_free, 2))
                act.sem_inc(o_root, 1)

        def attention(l):
            own, both = segs_of(l, False), segs_of(l, True)
            t0 = own[-1][0]
            act.wait_ge(c_done, seen.upto(c_done))
            A(b_sq[:, 0:2, t0:T], bq[:, :, t0:T], ACT.Square).then_inc(bsq_ready, 1)
            act.wait_ge(bsq_ready, seen.upto(bsq_ready))
            A(b_sq[:, 2, :], bkv[:], ACT.Square).then_inc(bsq_ready, 1)
            act.wait_ge(bsq_ready, seen.upto(bsq_ready))
            for j, (segs, width) in enumerate(((own, 256), (both, 128))):
                f = seen.bank(psum_A_full)
                act.wait_ge(psum_A_full, seen.upto(psum_A_full, 2))
                for b, (s, n, _) in enumerate(segs):
                    ins = A(b_rt[:, j, s:s + n], psA[:, f + b, 0:n], ACT.Sqrt, bias=EPS_COL, scale=1.0 / width)
                ins.then_inc(psum_A_free, 2)
                act.wait_ge(psum_A_free, seen.upto(psum_A_free, 2))
            act.sem_inc(b_root, 1)
            for tt in range(NTT):
                f = seen.bank(psum_A_full)
                act.wait_ge(psum_A_full, seen.upto(psum_A_full, 1))
                A(vt[:, tt, :], psA[:, f, :], ACT.Copy).then_inc(psum_A_free, 1)
                act.wait_ge(psum_A_free, seen.upto(psum_A_free, 1))
            act.sem_inc(v_ready, 1)
            for j in range(2):
                ins = A(k_sq[64:96, j, :], krx[64:96, 0, :], ACT.Square)
            ins.then_inc(kr_squared, 1)
            act.wait_ge(kr_squared, seen.upto(kr_squared))

            def project(h):
                if h:
                    act.wait_ge(head_ready, seen.upto(head_ready))
                for s, n, _ in own:
                    f = seen.bank(psum_A_full)
                    act.wait_ge(psum_A_full, seen.upto(psum_A_full, 2))
                    A(q_raw[0:BQK, s:s + n], psA[0:BQK, f, 0:n], ACT.Copy)
                    A(q_sq[0:BQK, s:s + n], psA[0:BQK, f, 0:n], ACT.Square)
                    A(q_rot[64:96, s:s + n], psA[64:96, f + 1, 0:n], ACT.Copy).then_inc(psum_A_free, 2)
                    act.wait_ge(psum_A_free, seen.upto(psum_A_free, 2))
                for b, (s, n, _) in enumerate(both):
                    if b == 0:
                        f = seen.bank(psum_A_full)
                        act.wait_ge(psum_A_full, seen.upto(psum_A_full, 2))
                    A(k_raw[0:BN, s:s + n], psA[0:BN, f + b, 0:n], ACT.Copy)
                    ins = A(k_sq[0:BN, h % 2, s:s + n], psA[0:BN, f + b, 0:n], ACT.Square)
                ins.then_inc(psum_A_free, 2)
                act.wait_ge(psum_A_free, seen.upto(psum_A_free, 2))
                act.sem_inc(headsq, 1)
                f = seen.bank(psum_A_full)
                act.wait_ge(psum_A_full, seen.upto(psum_A_full, 2))
                for b, (s, n, _) in enumerate(own):
                    ins = A(h_rt[0:BQK, 0, s:s + n], psA[0:BQK, f + b, 0:n], ACT.Sqrt, bias=EPS96_COL[0:BQK], scale=1.0)
                ins.then_inc(psum_A_free, 2)
                act.wait_ge(psum_A_free, seen.upto(psum_A_free, 2))
                f = seen.bank(psum_A_full)
                act.wait_ge(psum_A_full, seen.upto(psum_A_full, 2))
                for b, (s, n, _) in enumerate(both):
                    ins = A(h_rt[0:BQK, 1, s:s + n], psA[0:BQK, f + b, 0:n], ACT.Sqrt, bias=EPS_COL[0:BQK], scale=1.0 / BQK)
                ins.then_inc(psum_A_free, 2)
                act.wait_ge(psum_A_free, seen.upto(psum_A_free, 2))
                act.sem_inc(head_root, 1)

            units = [(s, n, q) for s, n, _ in own for q in range(n // P)]

            def evacuate(u, nkeys):
                f = seen.bank(psum_A_full)
                act.wait_ge(psum_A_full, seen.upto(psum_A_full, 2))
                A(pts[u % 2][:, 0:nkeys], pair(f)[:, 0:nkeys], ACT.Copy).then_inc(psum_A_free, 2)
                act.wait_ge(psum_A_free, seen.upto(psum_A_free, 2))
                act.sem_inc(pt_ready, 1)

            u = [0]

            def exponent(i):
                s, n, q = units[i]
                f = seen.bank(psum_A_full)
                act.wait_ge(psum_A_full, seen.upto(psum_A_full, 2))
                act.wait_ge(negmax_ready, seen.upto(negmax_ready))
                b = (u[0] + i) % 2
                if s:
                    src, dst = pair(f)[:, 0:T], probs[:, b, :]
                else:
                    src, dst = psA[:, f:f + 2, 0:P], probs[:, b, 0:NCTX].rearrange("p (b n) -> p b n", b=2)
                A(dst, src, ACT.Exp, bias=small[:, 48 + b:49 + b], accum_out=small[:, 50 + b:51 + b]).then_inc(psum_A_free, 2)
                act.wait_ge(psum_A_free, seen.upto(psum_A_free, 2))
                act.sem_inc(exp_done, 1)

            def attend(h):
                exponent(0)
                for i, (s, n, q) in enumerate(units):
                    if i + 1 < len(units):
                        exponent(i + 1)
                    evacuate(u[0] + i, T if s else NCTX)
                u[0] += len(units)

            project(0)
            for h in range(BH):
                if h + 1 < BH:
                    project(h + 1)
                attend(h)
            act.wait_ge(head_ready, seen.upto(head_ready))

        def mix_split():
            for k in range(KD):
                act.wait_ge(mix_lo, seen.upto(mix_lo))
                ins = A(h_hi[:, k, T0[0]:T], mixF[:, k, T0[0]:T], ACT.Copy)
            ins.then_inc(mix_ready, 1)
            act.wait_ge(mix_ready, seen.upto(mix_ready))

        def route(l):
            segs = segs_of(l, False)
            for t in range(WQ_TILES):
                split_to(min(WQ0[l] + t + 3, EX0[l] + 2))
                f = seen.bank(psum_A_full)
                act.wait_ge(psum_A_full, seen.upto(psum_A_full, 2))
                copy_pair(f, segs, ACT.Copy, q_hp[:, t % 2]).then_inc(psum_A_free, 2)
                act.wait_ge(psum_A_free, seen.upto(psum_A_free, 2))
                act.sem_inc(q_ready, 1)
            for tt in range(segs[-1][0] // P, NTT):
                act.wait_ge(cand_raw, seen.upto(cand_raw))
                A(best[:], best[:], ACT.Exp).then_inc(cand_exp, 1)
                act.wait_ge(cand_exp, seen.upto(cand_exp))
                f = seen.bank(psum_A_full)
                act.wait_ge(psum_A_full, seen.upto(psum_A_full, 1))
                A(idxT[:, :, tt * P:(tt + 1) * P],
                                psA[:, f, 0:384].rearrange("p (j t) -> p j t", j=3), ACT.Copy).then_inc(psum_A_free, 1)
                act.wait_ge(psum_A_free, seen.upto(psum_A_free, 1))
                act.sem_inc(sel_copied, 1)

        def build_gates(l):
            tb0 = 0 if l < DEPTH - 1 else NCTX // TB
            with act.Fori(0, (NTB - tb0) // 2) as i:
                seen.enter(i, {psum_A_full: 2 * GROUPS, psum_A_free: 2 * GROUPS, g_stored[0]: 16, g_stored[1]: 16})
                for b in range(2):
                    act.wait_ge(g_stored[b], seen.at(g_stored[b], seen.n[g_stored[b]]))
                    seen.n[g_stored[b]] += 16
                    for g in range(GROUPS):
                        f = seen.bank(psum_A_full)
                        act.wait_ge(psum_A_full, seen.upto(psum_A_full, 1))
                        A(g_buf[:, b, :, 4 * g:4 * g + 4],
                                        psA[:, f, :].rearrange("p (t i) -> p i t", t=4), ACT.Copy).then_inc(psum_A_free, 1)
                        act.wait_ge(psum_A_free, seen.upto(psum_A_free, 1))
                    act.sem_inc(gates_full, 1)
            seen.leave((NTB - tb0) // 2)

        def experts(l):
            segs = segs_of(l, False)
            banks = len(segs)

            def gelus():
                for c in range(2):
                    f = seen.bank(psum_A_full)
                    act.wait_ge(psum_A_full, seen.upto(psum_A_full, banks))
                    act.wait_ge(w_ready, seen.at(w_ready, seen.n[w_ready]))
                    seen.n[w_ready] += 1
                    copy_pair(f, segs, ACT.Gelu, gel[:, c]).then_inc(psum_A_free, banks)
                    act.wait_ge(psum_A_free, seen.upto(psum_A_free, banks))
                    act.sem_inc(gelu_ready, 1)

            def body(gelu=True):
                base = splits[0]
                split_to(base + 2)
                if gelu:
                    gelus()
                split_to(base + 4 if gelu else base + 2)

            for b in range(2):
                act.wait_ge(g_stored[b], seen.at(g_stored[b], seen.n[g_stored[b]]))
            for c in range(2):
                f = seen.bank(psum_A_full)
                act.wait_ge(psum_A_full, seen.upto(psum_A_full, banks))
                copy_pair(f, segs, ACT.Gelu, gel[:, c]).then_inc(psum_A_free, banks)
                act.wait_ge(psum_A_free, seen.upto(psum_A_free, banks))
                act.sem_inc(gelu_ready, 1)
            seen.n[w_ready] = l * 2 * NSUPER + 1
            split_to(EX0[l] + 4)
            body()
            rate = {raw_landed[0]: 64, raw_landed[1]: 64, tile_passed: 8, hi_done: 8, psum_A_full: 4 * banks,
                    psum_A_free: 4 * banks, w_ready: 4}
            first = splits[0]
            with act.Fori(0, (NSUPER - 2) // 2) as i:
                seen.enter(i, rate)
                body()
                body()
            seen.leave((NSUPER - 2) // 2)
            splits[0] = first + 4 * (NSUPER - 2)
            split_to(min(EX0[l] + EXPERT_TILES + 2, N_TILES))

        for b in range(2):
            act.sem_inc(g_stored[b], 16)
            seen.n[g_stored[b]] = 16
        EPS_COL, EPS96_COL = small[:, 150:151], small[:, 151:152]
        act.wait_ge(inputs_landed, seen.upto(inputs_landed, 16 * 13))
        A(c_raw[:], c_raw[:], ACT.Silu).then_inc(cond_ready, 1)
        act.wait_ge(cond_ready, seen.upto(cond_ready))
        A(c_hi[:], c_raw[:], ACT.Copy).then_inc(cond_hi, 1)
        act.wait_ge(cond_hi, seen.upto(cond_hi))
        split_to(10)
        first = splits[0]
        with act.Fori(0, MOD_TILES // 8 - 1) as i:
            seen.enter(i, {hi_done: 8, raw_landed[0]: 64, raw_landed[1]: 64, tile_passed: 8})
            split_to(splits[0] + 8)
        seen.leave(MOD_TILES // 8 - 1)
        splits[0] = first + MOD_TILES - 8
        act.wait_ge(mod_ready, seen.upto(mod_ready))
        A(lb[:, 3:5, :], lb[:, 3:5, :], ACT.Exp).then_inc(cond_hi, 1)
        act.wait_ge(cond_hi, seen.upto(cond_hi))
        T0 = [0]
        for l in range(DEPTH):
            T0[0] = segs_of(l, False)[-1][0]
            act.wait_ge(x_ready, seen.upto(x_ready))
            norm(l, 0)
            in_projection(l)
            gated_mlp(l)
            hgrn(l)
            attention(l)
            mix_split()
            for t in range(OUT_TILES):
                split_to(OUT0[l] + t + 3)
            act.wait_ge(x_ready, seen.upto(x_ready))
            norm(l, 1)
            route(l)
            build_gates(l)
            experts(l)

    @block.vector
    def _(dve):
        seen = Counts()
        seen.n[psum_V_free] = 4
        V = nc.vector
        splits = [0]

        def split_one():
            n = splits[0]
            splits[0] += 1
            dve.wait_ge(raw_landed[n % RAW], seen.upto(raw_landed[n % RAW], 16))
            if n >= SPLIT:
                dve.wait_ge(tile_passed, seen.at(tile_passed, n - SPLIT + 1))
            dve.wait_ge(hi_done, seen.upto(hi_done))
            V.tensor_tensor(split_lo[:, n % SPLIT].rearrange("p k n -> p (k n)"), raw[:, n % RAW, :],
                            split_hi[:, n % SPLIT].rearrange("p k n -> p (k n)").bitcast(F32), ALU.subtract).then_inc(lo_done, 1)
            dve.wait_ge(lo_done, seen.upto(lo_done))

        def split_to(end):
            while splits[0] < end:
                split_one()

        def norm(l, which):
            segs = segs_of(l, which == 0)
            t0 = segs[-1][0]
            dve.wait_ge(root_ready, seen.upto(root_ready))
            V.reciprocal(root[:, t0:T], root[:, t0:T]).then_inc(dve_chain, 1)
            dve.wait_ge(dve_chain, seen.upto(dve_chain))

            def lo(k):
                dve.wait_ge(hhi_ready, seen.upto(hhi_ready))
                for s, n, j in segs:
                    shift = mod[:, l * 48 + which * 24 + k, j:j + 1]
                    ins = V.scalar_tensor_tensor(h_lo[:, k, s:s + n], tmp[:, k % 2, s:s + n], shift,
                                                 h_hi[:, k, s:s + n].bitcast(F32), ALU.add, ALU.subtract)
                ins.then_inc(h_ready, 1)
                dve.wait_ge(h_ready, seen.upto(h_ready))

            for k in range(KD):
                for s, n, j in segs:
                    ins = V.scalar_tensor_tensor(tmp[:, k % 2, s:s + n], xT[:, k, s:s + n],
                                                 modA[:, l, which, k, j:j + 1], root[:, s:s + n], ALU.mult, ALU.mult)
                ins.then_inc(tmp_ready, 1)
                dve.wait_ge(tmp_ready, seen.upto(tmp_ready))
                if k:
                    lo(k - 1)
            lo(KD - 1)

        def gated_mlp(l):
            t0 = 0 if l < DEPTH - 1 else NCTX // P
            dve.wait_ge(av_squared, seen.upto(av_squared))
            V.tensor_reduce(small[:, 4 * t0:24], av_sq[:, t0:].rearrange("p t (h c) -> p (t h) c", c=64), AX.X, ALU.add).then_inc(a_sums, 1)
            dve.wait_ge(a_sums, seen.upto(a_sums))
            dve.wait_ge(a_root, seen.upto(a_root))
            V.reciprocal(small[:, 24:48], small[:, 24:48]).then_inc(dve_chain, 1)
            dve.wait_ge(dve_chain, seen.upto(dve_chain))
            v4 = vn[:, t0:].rearrange("p t (h c) -> p (t h) c", c=64)
            V.tensor_tensor(v4, av[:, t0:].rearrange("p t (h c) -> p (t h) c", c=64),
                                     small[:, 24 + 4 * t0:48].unsqueeze(2).broadcast_to([P, 24 - 4 * t0, 64]), ALU.mult).then_inc(dve_chain, 1)
            dve.wait_ge(dve_chain, seen.upto(dve_chain))
            dve.wait_ge(aw_landed, seen.upto(aw_landed, 48))
            V.tensor_tensor(vn[:, t0:], vn[:, t0:], a_norm[:].unsqueeze(1).broadcast_to([P, NTT - t0, 256]), ALU.mult).then_inc(vn_ready, 1)
            dve.wait_ge(vn_ready, seen.upto(vn_ready))
            segs = segs_of(l, False)
            for hp in range(2):
                f = seen.bank(psum_V_full)
                dve.wait_ge(psum_V_full, seen.upto(psum_V_full, 2))
                for b, (s, n, _) in enumerate(segs):
                    ins = V.tensor_tensor(mixF[:, hp, s:s + n].rearrange("p (t c) -> p t c", c=P),
                                          psV[:, f + b, 0:n].rearrange("p (t c) -> p t c", c=P),
                                          a_bias[:, hp].unsqueeze(1).broadcast_to([P, n // P, P]), ALU.add)
                ins.then_inc(psum_V_free, 2)
                dve.wait_ge(psum_V_free, seen.upto(psum_V_free, 2))
            t0 = t0 * P
            V.tensor_tensor(mixF[:, 0:2, t0:T], mixF[:, 0:2, t0:T], au[:, :, t0:T], ALU.mult).then_inc(dve_chain, 1)
            dve.wait_ge(dve_chain, seen.upto(dve_chain))
            dve.sem_inc(a_done, 1)

        def hgrn(l):
            own = segs_of(l, False)
            if l == DEPTH - 1:
                for dt in range(4):
                    V.tensor_scalar(lf[:, dt], lf[:, dt], lb[:, 6, dt:dt + 1], lb[:, 5, dt:dt + 1], ALU.mult, ALU.add)
                    ins = V.tensor_scalar(kk[:, dt], kk[:, dt], lb[:, 6, dt:dt + 1], None, ALU.mult)
                ins.then_inc(dve_chain, 1)
                dve.wait_ge(dve_chain, seen.upto(dve_chain))
            V.tensor_scalar(lf[:], lf[:], 2.0 ** -64, None, ALU.max).then_inc(f_ready, 1)
            dve.wait_ge(f_ready, seen.upto(f_ready))
            dve.wait_ge(logf_ready, seen.upto(logf_ready))
            for dt in range(4):
                if dt < 2:
                    ins = V.tensor_tensor_scan(cb[:, dt], resets[:, 0:T], lf[:, dt], 0.0, ALU.mult, ALU.add)
                else:
                    ins = V.tensor_tensor_scan(cb[:, dt, ::-1], resets[:, 1:T + 1][:, ::-1], lf[:, dt, ::-1], 0.0,
                                               ALU.mult, ALU.add)
            ins.then_inc(dve_chain, 1)
            dve.wait_ge(dve_chain, seen.upto(dve_chain))
            for dt in range(4):
                b4 = cb[:, dt].rearrange("p (c t) -> p c t", t=P)
                end = b4[:, :, P - 1:P] if dt < 2 else b4[:, :, 0:1]
                ins = V.tensor_tensor(lf[:, dt].rearrange("p (c t) -> p c t", t=P), b4,
                                      end.broadcast_to([P, NTT, P]), ALU.subtract)
            ins.then_inc(e_raw, 1)
            dve.wait_ge(e_raw, seen.upto(e_raw))
            dve.wait_ge(e_exp, seen.upto(e_exp))
            V.tensor_tensor(lf[:], lf[:], kk[:], ALU.mult).then_inc(khat_ready, 1)
            dve.wait_ge(khat_ready, seen.upto(khat_ready))
            dve.wait_ge(khT_ready, seen.upto(khT_ready))
            dve.wait_ge(gx_exp, seen.upto(gx_exp))
            for d in range(2):
                col = P - 1 if d == 0 else 0
                ins = V.tensor_copy(small[:, 52 + 12 * d:64 + 12 * d].rearrange("p (a c) -> p a c", a=2),
                                    lf[:, 2 * d:2 * d + 2, col::P])
            ins.then_inc(dve_chain, 1)
            dve.wait_ge(dve_chain, seen.upto(dve_chain))
            t0 = own[-1][0]
            for d in range(2):
                ins = V.tensor_tensor(lf[:, 2 * d:2 * d + 2, t0:T], lf[:, 2 * d:2 * d + 2, t0:T], cq[:, :, t0:T], ALU.mult)
            ins.then_inc(qexp_ready, 1)
            dve.wait_ge(qexp_ready, seen.upto(qexp_ready))
            dve.wait_ge(states_zero, seen.upto(states_zero))
            for i in range(NTT - 1):
                f = seen.bank(psum_V_full)
                dve.wait_ge(psum_V_full, seen.upto(psum_V_full, 2))
                for d in range(2):
                    order = chunk_f if d == 0 else chunk_b
                    c, nxt = order[i], order[i + 1]
                    for t in range(2):
                        dt = 2 * d + t
                        for r in (slice(0, 64), slice(64, 128)):
                            ins = V.scalar_tensor_tensor(
                                states[r, dt, nxt, r], states[r, dt, c, r], small[r, 52 + 6 * dt + c:53 + 6 * dt + c],
                                psV[r, f, dt * P + r.start:dt * P + r.stop], ALU.mult, ALU.add)
                ins.then_inc(psum_V_free, 2)
                dve.wait_ge(psum_V_free, seen.upto(psum_V_free, 2))
            dve.sem_inc(state_ready, 1)
            n_att = 0
            for hp in range(2):
                for s, n, _ in own:
                    for tt in range(s // P, (s + n) // P):
                        c0 = tt * P
                        if hp or tt != own[0][0] // P:
                            dve.wait_ge(unit_passed, seen.upto(unit_passed))
                        for li, m in enumerate(LEVELS):
                            for d in range(2):
                                b3 = cb[:, 2 * d + hp, c0:c0 + P].rearrange("p (b t) -> p b t", t=2 * m)
                                ref = b3[:, :, m - 1:m] if d == 0 else b3[:, :, m:m + 1]
                                ins = V.tensor_tensor(lvl_q[:, li, d].rearrange("p (b t) -> p b t", t=2 * m), b3,
                                                      ref.broadcast_to([P, P // (2 * m), 2 * m]), ALU.subtract)
                        ins.then_inc(lvl_raw, 1)
                        dve.wait_ge(lvl_raw, seen.upto(lvl_raw))
                        dve.wait_ge(lvl_exp, seen.upto(lvl_exp))
                        V.tensor_tensor(lvl_k[:], lvl_q[:],
                                        kk[:, hp:4:2, c0:c0 + P].unsqueeze(1).broadcast_to([P, 7, 2, P]), ALU.mult)
                        V.tensor_tensor(lvl_q[:].rearrange("p l d t -> p (l d) t"), lvl_q[:].rearrange("p l d t -> p (l d) t"),
                                        cq[:, hp, c0:c0 + P].unsqueeze(1).broadcast_to([P, 14, P]), ALU.mult).then_inc(qk_ready, 1)
                        dve.wait_ge(qk_ready, seen.upto(qk_ready))
                        for hd in range(2):
                            f = seen.bank(psum_V_full)
                            dve.wait_ge(psum_V_full, seen.upto(psum_V_full, 2))
                            if n_att >= 2:
                                dve.wait_ge(att_used, seen.upto(att_used))
                            V.tensor_tensor(attm[:], psV[:, f:f + 2, 0:448].rearrange("p d (l t) -> p d l t", l=NLB),
                                                     masks, ALU.mult).then_inc(dve_chain, 1)
                            dve.wait_ge(dve_chain, seen.upto(dve_chain))
                            V.tensor_reduce(attR[:], attm[:].rearrange("p d l t -> p t (d l)"), AX.X, ALU.add).then_inc(dve_chain, 1)
                            dve.wait_ge(dve_chain, seen.upto(dve_chain))
                            F = attF[:, hd]
                            V.tensor_copy(F[0:64, 0:64], attR[0:64, :])
                            V.tensor_copy(F[64:128, 64:128], attR[64:128, :])
                            V.tensor_copy(F[0:64, 64:128], psV[0:64, f, 448:512])
                            V.tensor_copy(F[64:128, 0:64], psV[64:128, f + 1, 448:512]).then_inc(psum_V_free, 2)
                            dve.wait_ge(psum_V_free, seen.upto(psum_V_free, 2))
                            dve.sem_inc(att_ready, 1)
                            n_att += 1
            dve.wait_ge(att_used, seen.upto(att_used, 2))
            dve.wait_ge(unit_passed, seen.upto(unit_passed))
            for hp in range(2):
                dve.wait_ge(o_root, seen.upto(o_root))
                V.reciprocal(o_rt[:, t0:T], o_rt[:, t0:T]).then_inc(dve_chain, 1)
                dve.wait_ge(dve_chain, seen.upto(dve_chain))
                V.scalar_tensor_tensor(mixF[:, 6 + hp, t0:T], mixF[:, 6 + hp, t0:T],
                                                par[:, l, PAR["conorm"]:PAR["conorm"] + 1], o_rt[:, t0:T], ALU.mult, ALU.mult).then_inc(dve_chain, 1)
                dve.wait_ge(dve_chain, seen.upto(dve_chain))
                V.tensor_tensor(mixF[:, 6 + hp, t0:T], mixF[:, 6 + hp, t0:T], cg[:, hp, t0:T], ALU.mult).then_inc(dve_chain, 1)
                dve.wait_ge(dve_chain, seen.upto(dve_chain))
                if hp == 0:
                    dve.sem_inc(o_raw, 1)
            dve.sem_inc(c_done, 1)

        def attention(l):
            own, both = segs_of(l, False), segs_of(l, True)
            t0 = own[-1][0]

            def pcol(name, rows=slice(0, P), i=0):
                return par[rows, l, PAR[name] + i:PAR[name] + i + 1]

            R = slice(64, 96)
            for j, (tab, w) in enumerate(((rope_c, "qhw"), (rope_s, "qrw"), (rope_c, "khw"), (rope_s, "krw"))):
                ins = V.tensor_scalar(bc[R, j], tab[R, :], pcol(w, R), None, ALU.mult)
            dve.wait_ge(b_root, seen.upto(b_root))
            V.reciprocal(b_rt[:, 0, t0:T], b_rt[:, 0, t0:T])
            V.reciprocal(b_rt[:, 1], b_rt[:, 1]).then_inc(dve_chain, 1)
            dve.wait_ge(dve_chain, seen.upto(dve_chain))
            for k in range(2):
                V.scalar_tensor_tensor(bq[:, k, t0:T], bq[:, k, t0:T], pcol("bqn", i=k), b_rt[:, 0, t0:T], ALU.mult, ALU.mult)
            V.scalar_tensor_tensor(bkv[:], bkv[:], pcol("bkvn"), b_rt[:, 1], ALU.mult, ALU.mult).then_inc(bn_ready, 1)
            dve.wait_ge(bn_ready, seen.upto(bn_ready))
            dve.wait_ge(kr_squared, seen.upto(kr_squared))
            V.tensor_tensor(krx[R, 0], krx[R, 0], bc[R, 2], ALU.mult)
            V.tensor_tensor(krx[R, 1], krx[R, 1], bc[R, 3], ALU.mult).then_inc(dve_chain, 1)
            dve.wait_ge(dve_chain, seen.upto(dve_chain))
            V.tensor_tensor(krx[R, 0], krx[R, 0], krx[R, 1], ALU.add).then_inc(dve_chain, 1)
            dve.wait_ge(dve_chain, seen.upto(dve_chain))
            N = slice(0, 64)

            def project(h):
                dve.wait_ge(head_root, seen.upto(head_root))
                V.reciprocal(h_rt[0:BQK, 0, t0:T], h_rt[0:BQK, 0, t0:T])
                V.reciprocal(h_rt[0:BQK, 1], h_rt[0:BQK, 1]).then_inc(dve_chain, 1)
                dve.wait_ge(dve_chain, seen.upto(dve_chain))
                q, k = qn[:, h % 2], kn[:, h % 2]
                V.scalar_tensor_tensor(q[N, t0:T], q_raw[N, t0:T], pcol("qhw", N), h_rt[N, 0, t0:T], ALU.mult, ALU.mult)
                V.scalar_tensor_tensor(k[N, :], k_raw[N, :], pcol("khw", N), h_rt[N, 1], ALU.mult, ALU.mult)
                V.tensor_tensor(q_raw[R, t0:T], q_raw[R, t0:T], bc[R, 0, t0:T], ALU.mult)
                V.tensor_tensor(q_rot[R, t0:T], q_rot[R, t0:T], bc[R, 1, t0:T], ALU.mult).then_inc(dve_chain, 1)
                dve.wait_ge(dve_chain, seen.upto(dve_chain))
                V.tensor_tensor(k[R, :], krx[R, 0], h_rt[R, 1], ALU.mult)
                V.tensor_tensor(q_raw[R, t0:T], q_raw[R, t0:T], q_rot[R, t0:T], ALU.add).then_inc(dve_chain, 1)
                dve.wait_ge(dve_chain, seen.upto(dve_chain))
                V.tensor_tensor(q[R, t0:T], q_raw[R, t0:T], h_rt[R, 0, t0:T], ALU.mult).then_inc(dve_chain, 1)
                dve.wait_ge(dve_chain, seen.upto(dve_chain))
                dve.sem_inc(head_ready, 1)

            units = [(s, n, q) for s, n, _ in own for q in range(n // P)]
            u = [0]

            def row_max(i):
                dve.wait_ge(scores_ready, seen.upto(scores_ready))
                s, f, b = units[i][0], score_bank[l][u[0] + i], (u[0] + i) % 2
                src = psA[:, f:f + 2, :].rearrange("p b n -> p (b n)")[:, 0:T] if s else psA[:, f:f + 2, 0:P]
                V.tensor_reduce(small[:, 48 + b:49 + b], src, AX.X if s else AX.XY, ALU.max, negate=True).then_inc(negmax_ready, 1)
                dve.wait_ge(negmax_ready, seen.upto(negmax_ready))

            def normalise(i, nkeys):
                dve.wait_ge(exp_done, seen.upto(exp_done))
                r = small[:, 50 + i % 2:51 + i % 2]
                V.reciprocal(r, r).then_inc(dve_chain, 1)
                dve.wait_ge(dve_chain, seen.upto(dve_chain))
                V.tensor_scalar(probs[:, i % 2, 0:nkeys], probs[:, i % 2, 0:nkeys], r, None, ALU.mult).then_inc(probs_ready, 1)
                dve.wait_ge(probs_ready, seen.upto(probs_ready))

            def attend(h):
                row_max(0)
                for i, (s, n, q) in enumerate(units):
                    if i + 1 < len(units):
                        row_max(i + 1)
                    normalise(u[0] + i, T if s else NCTX)
                u[0] += len(units)
                for s, n, _ in own:
                    f = seen.bank(psum_V_full)
                    dve.wait_ge(psum_V_full, seen.upto(psum_V_full, 1))
                    r = slice(64 * (h % 2), 64 * (h % 2) + 64)
                    V.tensor_copy(mixF[r, 2 + h // 2, s:s + n], psV[r, f, 0:n]).then_inc(psum_V_free, 1)
                    dve.wait_ge(psum_V_free, seen.upto(psum_V_free, 1))

            project(0)
            for h in range(BH):
                if h + 1 < BH:
                    project(h + 1)
                attend(h)

        def mix_split(l):
            t0 = segs_of(l, False)[-1][0]
            for k in range(KD):
                V.tensor_copy(mix_r[:, k % 2, t0:T], mixF[:, k, t0:T]).then_inc(dve_chain, 1)
                dve.wait_ge(dve_chain, seen.upto(dve_chain))
                V.tensor_tensor(h_lo[:, k, t0:T], mixF[:, k, t0:T], mix_r[:, k % 2, t0:T].bitcast(F32), ALU.subtract).then_inc(mix_lo, 1)
                dve.wait_ge(mix_lo, seen.upto(mix_lo))

        def add_gated(l, part, k, f, segs, banks=2):
            for b, (s, n, j) in enumerate(segs):
                ins = V.scalar_tensor_tensor(xT[:, k, s:s + n], psV[:, f + b, 0:n], mod[:, l * 48 + part * 8 + k, j:j + 1],
                                             xT[:, k, s:s + n], ALU.mult, ALU.add)
            ins.then_inc(psum_V_free, banks)
            dve.wait_ge(psum_V_free, seen.upto(psum_V_free, banks))

        def x_signal():
            dve.sem_inc(x_ready, 1)

        def top16(values, work, v16, i16):
            V.max(v16[:, 0:8], values).then_inc(dve_chain, 1)
            dve.wait_ge(dve_chain, seen.upto(dve_chain))
            V.max_index(i16[:, 0:8], v16[:, 0:8], values)
            ins = V.match_replace(work, v16[:, 0:8], values, -3.0e38)
            ins.then_inc(dve_chain, 1)
            dve.wait_ge(dve_chain, seen.upto(dve_chain))
            V.max(v16[:, 8:16], work).then_inc(dve_chain, 1)
            dve.wait_ge(dve_chain, seen.upto(dve_chain))
            return V.max_index(i16[:, 8:16], v16[:, 8:16], work)

        def route(l):
            segs = segs_of(l, False)
            tts = [(b, tt, tt - s // P) for b, (s, n, _) in enumerate(segs) for tt in range(s // P, (s + n) // P)]
            for t in range(WQ_TILES):
                split_to(min(WQ0[l] + t + 3, EX0[l] + 2))
                f = seen.bank(psum_V_full)
                dve.wait_ge(psum_V_full, seen.upto(psum_V_full, 2))

                def s_of(b, j):
                    return psV[:, f + b, j * P:(j + 1) * P]

                for b, tt, j in tts:
                    ins = V.max(sv[:, tt, t, 0:8], s_of(b, j))
                ins.then_inc(dve_chain, 1)
                dve.wait_ge(dve_chain, seen.upto(dve_chain))
                for b, tt, j in tts:
                    V.max_index(si[:, tt, t, 0:8], sv[:, tt, t, 0:8], s_of(b, j))
                    ins = V.match_replace(s_work[:, tt], sv[:, tt, t, 0:8], s_of(b, j), -3.0e38)
                ins.then_inc(psum_V_free, 2)
                dve.wait_ge(psum_V_free, seen.upto(psum_V_free, 2))
                for b, tt, j in tts:
                    ins = V.max(sv[:, tt, t, 8:16], s_work[:, tt])
                ins.then_inc(dve_chain, 1)
                dve.wait_ge(dve_chain, seen.upto(dve_chain))
                for b, tt, j in tts:
                    ins = V.max_index(si[:, tt, t, 8:16], sv[:, tt, t, 8:16], s_work[:, tt])
            ins.then_inc(dve_chain, 1)
            dve.wait_ge(dve_chain, seen.upto(dve_chain))
            tt0 = segs[-1][0] // P
            V.tensor_copy(si_f[:, tt0:], si[:, tt0:]).then_inc(dve_chain, 1)
            dve.wait_ge(dve_chain, seen.upto(dve_chain))
            for tt in range(tt0, NTT):
                svt = sv[:, tt].rearrange("p (h two) a -> p h two a", two=2)
                sit = si_f[:, tt].rearrange("p (h two) a -> p h two a", two=2)
                V.tensor_tensor(cand[:].rearrange("p h (a b) -> p h a b", b=TOPK),
                                         svt[:, :, 0, :].unsqueeze(3).broadcast_to([P, PH, TOPK, TOPK]),
                                         svt[:, :, 1, :].unsqueeze(2).broadcast_to([P, PH, TOPK, TOPK]), ALU.add).then_inc(dve_chain, 1)
                dve.wait_ge(dve_chain, seen.upto(dve_chain))
                for h in range(PH):
                    ins = top16(cand[:, h], cand2[:], best[:, h], best_i[:, h])
                ins.then_inc(dve_chain, 1)
                dve.wait_ge(dve_chain, seen.upto(dve_chain))
                if tt > tt0:
                    dve.wait_ge(sel_copied, seen.upto(sel_copied))
                bi = best_i[:].rearrange("p h k -> p (h k)")
                V.tensor_scalar(ab_i[:, 0], bi, 4, None, ALU.logical_shift_right)
                V.tensor_scalar(ab_i[:, 1], bi, 15, None, ALU.bitwise_and).then_inc(dve_chain, 1)
                dve.wait_ge(dve_chain, seen.upto(dve_chain))
                V.tensor_copy(ab_f[:], ab_i[:]).then_inc(dve_chain, 1)
                dve.wait_ge(dve_chain, seen.upto(dve_chain))
                V.tensor_copy(small[:, 128:136], best[:, :, 0]).then_inc(dve_chain, 1)
                dve.wait_ge(dve_chain, seen.upto(dve_chain))
                V.tensor_tensor(best[:], best[:], small[:, 128:136].unsqueeze(2).broadcast_to([P, PH, TOPK]), ALU.subtract).then_inc(cand_raw, 1)
                dve.wait_ge(cand_raw, seen.upto(cand_raw))
                for two in range(2):
                    V.tensor_tensor(eq[:], ab_f[:, two].unsqueeze(2).broadcast_to([P, P, TOPK]),
                                             iota16.unsqueeze(1).broadcast_to([P, P, TOPK]), ALU.is_equal).then_inc(dve_chain, 1)
                    dve.wait_ge(dve_chain, seen.upto(dve_chain))
                    e4 = eq[:].rearrange("p (h k) a -> p h k a", h=PH)
                    V.tensor_tensor(e4, e4, sit[:, :, two, :].unsqueeze(2).broadcast_to([P, PH, TOPK, TOPK]), ALU.mult).then_inc(dve_chain, 1)
                    dve.wait_ge(dve_chain, seen.upto(dve_chain))
                    V.tensor_reduce(sel[:, two], eq[:], AX.X, ALU.add).then_inc(dve_chain, 1)
                    dve.wait_ge(dve_chain, seen.upto(dve_chain))
                dve.wait_ge(cand_exp, seen.upto(cand_exp))
                V.tensor_reduce(small[:, 136:144], best[:], AX.X, ALU.add).then_inc(dve_chain, 1)
                dve.wait_ge(dve_chain, seen.upto(dve_chain))
                V.reciprocal(small[:, 136:144], small[:, 136:144]).then_inc(dve_chain, 1)
                dve.wait_ge(dve_chain, seen.upto(dve_chain))
                V.tensor_tensor(sel[:, 2].rearrange("p (h k) -> p h k", h=PH), best[:],
                                small[:, 136:144].unsqueeze(2).broadcast_to([P, PH, TOPK]), ALU.mult).then_inc(sel_ready, 1)
                dve.wait_ge(sel_ready, seen.upto(sel_ready))
            dve.wait_ge(sel_copied, seen.upto(sel_copied))

        def build_gates(l):
            tb0 = 0 if l < DEPTH - 1 else NCTX // TB
            base = 3 + (0 if l == 0 else NTB * GROUPS * l)
            with dve.Fori(0, (NTB - tb0) // 2) as i:
                seen.enter(i, {oh_passed: 2 * GROUPS, oh_ready: 2 * GROUPS})
                for g in range(2 * GROUPS):
                    dve.wait_ge(oh_passed, seen.at(oh_passed, base + g - 2))
                    for j in range(4):
                        t = i * (2 * TB) + (tb0 * TB + 4 * g + j)
                        V.tensor_scalar(onehot[:, g % 4, 0, j], iota, idxT[:, 0, bass.ds(t, 1)], None, ALU.is_equal)
                        ins = V.tensor_scalar(onehot[:, g % 4, 1, j], iota, idxT[:, 1, bass.ds(t, 1)],
                                              idxT[:, 2, bass.ds(t, 1)], ALU.is_equal, ALU.mult)
                    ins.then_inc(oh_ready, 1)
                    dve.wait_ge(oh_ready, seen.upto(oh_ready))
            seen.leave((NTB - tb0) // 2)

        def experts(l):
            segs = segs_of(l, False)
            t0 = segs[-1][0]
            banks = len(segs)

            def weight(c, par_):
                dve.wait_ge(gelu_ready, seen.upto(gelu_ready))
                if c == 0:
                    dve.wait_ge(g_landed[par_], seen.upto(g_landed[par_], 16))
                g = gel[:, c, t0:T]
                g3 = g.rearrange("p (b t) -> p b t", t=TB)
                V.tensor_tensor(g3, g3, g_in[:, par_, t0 // TB:, c * TB:(c + 1) * TB], ALU.mult).then_inc(dve_chain, 1)
                dve.wait_ge(dve_chain, seen.upto(dve_chain))
                V.tensor_copy(W_hi[:, par_, c, t0:T], g).then_inc(dve_chain, 1)
                dve.wait_ge(dve_chain, seen.upto(dve_chain))
                V.tensor_tensor(W_lo[:, par_, c, t0:T], g, W_hi[:, par_, c, t0:T].bitcast(F32), ALU.subtract).then_inc(w_ready, 1)
                dve.wait_ge(w_ready, seen.upto(w_ready))

            def add_chunk(k):
                f = seen.bank(psum_V_full)
                dve.wait_ge(psum_V_full, seen.upto(psum_V_full, banks))
                add_gated(l, 5, k, f, segs, banks)

            def body(now):
                base = splits[0]
                weight(1, now)
                split_to(base + 2)
                weight(0, 1 - now)
                for k in range(KD):
                    if k in (2, 5):
                        split_to(splits[0] + 1)
                    add_chunk(k)

            weight(0, 0)
            split_to(EX0[l] + 4)
            body(0)
            rate = {raw_landed[0]: 64, raw_landed[1]: 64, tile_passed: 8, hi_done: 8, lo_done: 8, w_ready: 4, gelu_ready: 4,
                    g_landed[0]: 16, g_landed[1]: 16, psum_V_full: 16 * banks, psum_V_free: 16 * banks, dve_chain: 8}
            first = splits[0]
            with dve.Fori(0, (NSUPER - 2) // 2) as i:
                seen.enter(i, rate)
                body(1)
                body(0)
            seen.leave((NSUPER - 2) // 2)
            splits[0] = first + 4 * (NSUPER - 2)
            weight(1, 1)
            split_to(min(EX0[l] + EXPERT_TILES + 2, N_TILES))
            for k in range(KD):
                add_chunk(k)

        dve.wait_ge(inputs_landed, seen.upto(inputs_landed, 16 * 13))
        V.memset(small[:, 150:151], EPS)
        V.memset(small[:, 151:152], BQK * EPS).then_inc(dve_chain, 1)
        dve.wait_ge(dve_chain, seen.upto(dve_chain))
        dve.wait_ge(cond_hi, seen.upto(cond_hi))
        V.tensor_tensor(c_lo[:], c_raw[:], c_hi[:].bitcast(F32), ALU.subtract).then_inc(cond_split, 1)
        dve.wait_ge(cond_split, seen.upto(cond_split))

        def modulation(n):
            f = seen.bank(psum_V_full)
            dve.wait_ge(psum_V_full, seen.upto(psum_V_full, 4))
            V.tensor_tensor(mod[:, n, :], psV[:, f, 0:16].rearrange("p (n j) -> p n j", j=2),
                                          bm[:, n].unsqueeze(2).broadcast_to([P, 8, 2]), ALU.add).then_inc(psum_V_free, 4)
            dve.wait_ge(psum_V_free, seen.upto(psum_V_free, 4))

        split_to(10)
        modulation(slice(0, 8))
        first = splits[0]
        with dve.Fori(0, MOD_TILES // 8 - 1) as i:
            seen.enter(i, {raw_landed[0]: 64, raw_landed[1]: 64, tile_passed: 8,
                           hi_done: 8, lo_done: 8, psum_V_full: 4, psum_V_free: 4})
            split_to(splits[0] + 8)
            modulation(bass.ds(i * 8 + 8, 8))
        seen.leave(MOD_TILES // 8 - 1)
        splits[0] = first + MOD_TILES - 8
        for l in range(DEPTH):
            for w in range(2):
                name = ("ln1", "ln2")[w]
                scale = mod[:, l * 48 + w * 24 + 8:l * 48 + w * 24 + 16, :]
                ins = V.scalar_tensor_tensor(modA[:, l, w], scale, 1.0,
                                             par[:, l, PAR[name]:PAR[name] + 8].unsqueeze(2).broadcast_to([P, KD, 2]),
                                             ALU.add, ALU.mult)
        ins.then_inc(dve_chain, 1)
        dve.wait_ge(dve_chain, seen.upto(dve_chain))
        V.tensor_tensor(lb[:, 2, :], lb[:, 0, :], lb[:, 1, :], ALU.max).then_inc(dve_chain, 1)
        dve.wait_ge(dve_chain, seen.upto(dve_chain))
        V.tensor_tensor(lb[:, 3, :], lb[:, 0, :], lb[:, 2, :], ALU.subtract)
        V.tensor_tensor(lb[:, 4, :], lb[:, 1, :], lb[:, 2, :], ALU.subtract).then_inc(dve_chain, 1)
        dve.wait_ge(dve_chain, seen.upto(dve_chain))
        dve.sem_inc(mod_ready, 1)
        dve.wait_ge(cond_hi, seen.upto(cond_hi))
        V.tensor_tensor(lb[:, 2, :], lb[:, 3, :], lb[:, 4, :], ALU.add).then_inc(dve_chain, 1)
        dve.wait_ge(dve_chain, seen.upto(dve_chain))
        V.reciprocal(lb[:, 2, :], lb[:, 2, :]).then_inc(dve_chain, 1)
        dve.wait_ge(dve_chain, seen.upto(dve_chain))
        V.tensor_tensor(lb[:, 5, :], lb[:, 4, :], lb[:, 2, :], ALU.mult)
        V.tensor_tensor(lb[:, 6, :], lb[:, 3, :], lb[:, 2, :], ALU.mult).then_inc(dve_chain, 1)
        dve.wait_ge(dve_chain, seen.upto(dve_chain))
        x_signal()
        for l in range(DEPTH):
            norm(l, 0)
            for t in range(IN_TILES):
                split_to(IN0[l] + t + 3)
            dve.wait_ge(proj_ready, seen.upto(proj_ready))
            gated_mlp(l)
            hgrn(l)
            attention(l)
            mix_split(l)
            segs = segs_of(l, False)
            for t in range(OUT_TILES):
                split_to(OUT0[l] + t + 3)
                f = seen.bank(psum_V_full)
                dve.wait_ge(psum_V_full, seen.upto(psum_V_full, 2))
                add_gated(l, 2, t, f, segs)
            x_signal()
            norm(l, 1)
            route(l)
            build_gates(l)
            experts(l)
            x_signal()


def shape_constants():
    p = np.arange(P)
    ident = np.eye(P)
    ones = np.ones((P, P))
    bones = (p[:, None] // 64 == p[None, :] // 64).astype(float)
    iota = np.broadcast_to(p[None, :], (P, P))
    iota16 = np.broadcast_to(np.arange(TOPK)[None, :], (P, TOPK))
    s, t = np.arange(64)[:, None], np.arange(64)[None, :]
    masks = np.zeros((P, 2, NLB, 64))
    for li, m in enumerate(LEVELS[1:]):
        same = s // (2 * m) == t // (2 * m)
        left, right = s // m % 2 == 0, t // m % 2 == 1
        masks[:, 0, li] = np.tile(same & left & right, (2, 1))
        masks[:, 1, li] = np.tile(same & ~left & ~right, (2, 1))
    masks[:, :, NLB - 1] = np.tile(s == t, (2, 1))[:, None, :]
    resets = np.broadcast_to((np.arange(T + 1) % P != 0)[None, :], (P, T + 1))
    f32 = np.float32
    n = np.arange(NLAT)
    inv = (f32(10000.0) ** (-np.arange(BR // 4, dtype=f32) / f32(BR // 4))).astype(f32)
    r = np.arange(BR)
    where = np.where(r[:, None] // 16 == 0, n[None, :] // 64, n[None, :] % 64).astype(f32)
    ang = (where * inv[r % 8][:, None]).astype(f32)
    sign = np.where(r % 16 < 8, -1.0, 1.0)[:, None]
    rope = np.zeros((P, 2, T))
    rope[64:96, 0, :NCTX] = 1.0
    rope[64:96, 0, NCTX:] = np.cos(ang)
    rope[64:96, 1, NCTX:] = np.sin(ang) * sign
    parts = [ident, ones, bones, iota, iota16, masks.reshape(P, -1), resets, rope.reshape(P, -1)]
    return np.ascontiguousarray(np.concatenate(parts, axis=1).astype(f32))


def tiles_of(w):
    d_in, n = w.shape
    return w.reshape(d_in // P, P, n // P, P).transpose(2, 1, 0, 3).reshape(n // P, P, d_in)


def columns(v):
    return np.moveaxis(v.reshape(v.shape[:-1] + (-1, P)), -1, 0)


def kernel(x, c, ctx, c_ctx, ln1_w, ln2_w, w_mod, b_mod, w_in, w_out, a_norm_w, a_w_s, a_b_s,
           b_q_norm_w, b_w_uq, b_kv_norm_w, b_w_ukv, b_q_head_norm_w, b_k_head_norm_w,
           c_lb_logits, c_out_norm_w, p_w_q, p_sub_keys, p_u, p_v):
    import concourse.bacc as bacc
    from concourse.bass_utils import run_bass_kernel_spmd

    A = np.asarray
    (x, c, ctx, c_ctx, ln1_w, ln2_w, w_mod, b_mod, w_in, w_out, a_norm_w, a_w_s, a_b_s, b_q_norm_w, b_w_uq,
     b_kv_norm_w, b_w_ukv, b_q_head_norm_w, b_k_head_norm_w, c_lb_logits, c_out_norm_w, p_w_q, p_sub_keys,
     p_u, p_v) = map(A, (x, c, ctx, c_ctx, ln1_w, ln2_w, w_mod, b_mod, w_in, w_out, a_norm_w, a_w_s, a_b_s,
                         b_q_norm_w, b_w_uq, b_kv_norm_w, b_w_ukv, b_q_head_norm_w, b_k_head_norm_w,
                         c_lb_logits, c_out_norm_w, p_w_q, p_sub_keys, p_u, p_v))

    partner = np.arange(BR) ^ 8
    offs = np.cumsum([0, 256, 256, 256, 128, 32, 256, 256, 256, 256, 256])
    a_u, a_v, b_q, b_kv, b_kr, c_q, c_f, c_b, c_i, c_g = [np.arange(offs[i], offs[i + 1]) for i in range(10)]
    kr_tile = np.concatenate([b_kr, b_kr, b_kr, b_kr[partner]])
    in_cols = np.concatenate([a_u, b_q, b_kv, kr_tile, c_q, c_f, c_b, c_g, a_v, c_i])
    tiles = np.empty((N_TILES, P, D), np.float32)
    at = 0

    def put(block):
        nonlocal at
        tiles[at:at + len(block)] = block
        at += len(block)

    for l in range(DEPTH):
        put(tiles_of(w_mod[l]))
    for l in range(DEPTH):
        put(tiles_of(w_in[l][:, in_cols]))
        put(tiles_of(w_out[l]))
        put(tiles_of(p_w_q[l]))
        u = p_u[l].reshape(NK, P, KD, P).transpose(0, 3, 2, 1).reshape(NK, P, D)
        v = p_v[l].reshape(NK, P, D)
        block = tiles[at:at + EXPERT_TILES]
        block[0:2] = u[0:2]
        rest = block[2:EXPERT_TILES - 2].reshape(NSUPER - 1, 4, P, D)
        rest[:, 0:2] = u[2:].reshape(NSUPER - 1, 2, P, D)
        rest[:, 2:4] = v[:-2].reshape(NSUPER - 1, 2, P, D)
        block[EXPERT_TILES - 2:] = v[-2:]
        at += EXPERT_TILES
    assert at == N_TILES

    x_in = np.concatenate([ctx[0].T, x[0].T], axis=1).reshape(KD, P, T).transpose(1, 0, 2)
    cond = np.stack([c[0].reshape(KD, P).T, c_ctx.reshape(KD, P).T], axis=2)
    params = np.zeros((P, DEPTH, NPAR), np.float32)
    for l in range(DEPTH):
        params[:, l, 0:8] = columns(ln1_w[l])
        params[:, l, 8:16] = columns(ln2_w[l])
        params[:, l, 16:18] = columns(b_q_norm_w[l])
        params[:, l, 18:19] = columns(b_kv_norm_w[l])
        params[0:BQK, l, 19] = b_q_head_norm_w[l]
        params[0:BQK, l, 20] = b_k_head_norm_w[l]
        params[64:96, l, 21] = b_q_head_norm_w[l][64:][partner]
        params[64:96, l, 22] = b_k_head_norm_w[l][64:][partner]
        params[:, l, 23] = np.tile(c_out_norm_w[l], 2)
    bmod = columns(b_mod.reshape(-1))
    lblog = columns(c_lb_logits).reshape(P, DEPTH, 4)
    bias = np.repeat(a_b_s.reshape(DEPTH, 2, 2, 1, P), 64, axis=3).reshape(DEPTH, 2, P, P).transpose(0, 2, 1, 3)
    arow = np.concatenate([bias.reshape(DEPTH, P, 256), np.broadcast_to(a_norm_w[:, None, :], (DEPTH, P, 256))], axis=2)
    aws = a_w_s.transpose(0, 3, 1, 2)
    uq = b_w_uq.reshape(DEPTH, 2, P, BH, BQK).transpose(0, 2, 1, 3, 4)
    uq_rot = uq[..., 64:][..., partner]
    ukv = b_w_ukv.reshape(DEPTH, P, BH, BN + BV)
    bw = np.concatenate([uq.reshape(DEPTH, P, 1536), uq_rot.reshape(DEPTH, P, 512),
                         ukv[..., :BN].reshape(DEPTH, P, 512), ukv[..., BN:].reshape(DEPTH, P, 512)], axis=2)
    keys = p_sub_keys.reshape(DEPTH, WQ_TILES, NK, P).transpose(0, 3, 1, 2)

    inputs = dict(tiles=tiles, x_in=x_in, consts=shape_constants(), params=params, bmod=bmod, cond=cond, arow=arow,
                  aws=aws, bw=bw, keys=keys, lblog=lblog)
    inputs = {k: np.ascontiguousarray(v) for k, v in inputs.items()}
    nc = bacc.Bacc("TRN2", target_bir_lowering=False, num_devices=1)
    args = {k: nc.dram_tensor(k, v.shape, F32, kind="ExternalInput").ap() for k, v in inputs.items()}
    args["gates"] = nc.dram_tensor("gates", (NTB, P, NK, TB), F32, kind="Internal").ap()
    args["out"] = nc.dram_tensor("out", (P, KD, NLAT), F32, kind="ExternalOutput").ap()
    build_program(nc, **args)
    r = run_bass_kernel_spmd(nc, [inputs], core_ids=[0])
    y = r.results[0]["out"]
    return y.transpose(1, 0, 2).reshape(1, D, NLAT).transpose(0, 2, 1)
```

```python
from collections import defaultdict
from contextlib import ExitStack

import numpy as np

import concourse.bass as bass
from concourse import mybir

P = 128
DEPTH = 2
D = 1024
KD = D // P
NCTX, NLAT = 256, 512
T = NCTX + NLAT
NTT = T // P
EPS = 1e-6
F32 = mybir.dt.float32
F32R = mybir.dt.float32r
U32 = mybir.dt.uint32
ALU = mybir.AluOpType
ACT = mybir.ActivationFunctionType
AX = mybir.AxisListType

LAT, CTX = (NCTX, NLAT, 0), (0, NCTX, 1)
BH, BN, BR, BV = 8, 64, 32, 64
BQK = BN + BR
PH, NK, TOPK = 8, 128, 16
LEVELS = (64, 32, 16, 8, 4, 2, 1)
NLB = 7
TB = 32
NTB = T // TB

MOD_TILES = 6 * KD
MOD_FIRST = 2 * KD
MOD_LATER = DEPTH * MOD_TILES - MOD_FIRST
IN_TILES, OUT_TILES, WQ_TILES, EXPERT_TILES = 18, 8, 16, 256
LAYER_TILES = IN_TILES + OUT_TILES + WQ_TILES + EXPERT_TILES
N_TILES = DEPTH * LAYER_TILES
MOD_SLOTS = MOD_FIRST // 2
NSUPER = NK // 2
RAW, SPLIT = 2, 4
GROUPS = TB // 4

PAR = {"ln1": 0, "ln2": 8, "bqn": 16, "bkvn": 18, "qhw": 19, "khw": 20, "qrw": 21, "krw": 22, "conorm": 23}
NPAR = 24


def segs_of(layer, context_too):
    return (LAT, CTX) if context_too or layer < DEPTH - 1 else (LAT,)


class Counts:

    def __init__(self):
        self.n = defaultdict(int)
        self.i, self.rate, self.entry = None, {}, {}

    def at(self, sem, count):
        return count if self.i is None else self.i * self.rate[sem] + count

    def upto(self, sem, k=1):
        self.n[sem] += k
        return self.at(sem, self.n[sem])

    def bank(self, sem):
        return self.n[sem] % 4

    def enter(self, i, rate):
        self.i, self.rate, self.entry = i, rate, dict(self.n)

    def leave(self, count):
        for sem in list(self.n):
            gained = self.n[sem] - self.entry.get(sem, 0)
            assert not gained or gained == self.rate.get(sem), (sem, gained, self.rate.get(sem))
            self.n[sem] = self.entry.get(sem, 0) + count * gained
        self.i = None


def build_program(nc, mod_pairs, mod_tiles, tiles, x_in, consts, params, bmod, cond, arow, aws, bw, keys, lblog, gates, out):
    sem_ctx = ExitStack()

    def semaphore(name):
        return sem_ctx.enter_context(nc.semaphore(name))

    raw_landed = (semaphore("raw_landed0"), semaphore("raw_landed1"))
    g_stored = (semaphore("g_stored0"), semaphore("g_stored1"))
    g_landed = (semaphore("g_landed0"), semaphore("g_landed1"))
    hi_done = semaphore("hi_done")
    lo_done = semaphore("lo_done")
    tile_passed = semaphore("tile_passed")
    psum_V_full = semaphore("psum_V_full")
    psum_V_free = semaphore("psum_V_free")
    psum_A_full = semaphore("psum_A_full")
    psum_A_free = semaphore("psum_A_free")
    inputs_landed = semaphore("inputs_landed")
    act_chain = semaphore("act_chain")
    pool_chain = semaphore("pool_chain")
    dve_chain = semaphore("dve_chain")
    cond_ready = semaphore("cond_ready")
    lb_exp = semaphore("lb_exp")
    mod_landed = [semaphore("mod_landed%d" % m) for m in range(MOD_SLOTS)]
    mod_passed = semaphore("mod_passed")
    mod_ready = semaphore("mod_ready")
    sq_ready = semaphore("sq_ready")
    sq_used = semaphore("sq_used")
    root_ready = semaphore("root_ready")
    tmp_ready = semaphore("tmp_ready")
    hhi_ready = semaphore("hhi_ready")
    h_ready = semaphore("h_ready")
    proj_ready = semaphore("proj_ready")
    aw_landed = semaphore("aw_landed")
    av_squared = semaphore("av_squared")
    a_sums = semaphore("a_sums")
    vn_ready = semaphore("vn_ready")
    a_root = semaphore("a_root")
    f_ready = semaphore("f_ready")
    logf_ready = semaphore("logf_ready")
    e_raw = semaphore("e_raw")
    e_exp = semaphore("e_exp")
    khat_ready = semaphore("khat_ready")
    gx_exp = semaphore("gx_exp")
    khT_ready = semaphore("khT_ready")
    states_zero = semaphore("states_zero")
    state_ready = semaphore("state_ready")
    qexp_ready = semaphore("qexp_ready")
    lvl_raw = semaphore("lvl_raw")
    lvl_exp = semaphore("lvl_exp")
    qk_ready = semaphore("qk_ready")
    att_ready = semaphore("att_ready")
    att_used = semaphore("att_used")
    unit_passed = semaphore("unit_passed")
    o_raw = semaphore("o_raw")
    osq_ready = semaphore("osq_ready")
    o_root = semaphore("o_root")
    a_done = semaphore("a_done")
    c_done = semaphore("c_done")
    bw_landed = semaphore("bw_landed")
    bsq_ready = semaphore("bsq_ready")
    b_root = semaphore("b_root")
    bn_ready = semaphore("bn_ready")
    v_ready = semaphore("v_ready")
    kr_squared = semaphore("kr_squared")
    headsq = semaphore("headsq")
    head_root = semaphore("head_root")
    head_ready = semaphore("head_ready")
    scores_ready = semaphore("scores_ready")
    negmax_ready = semaphore("negmax_ready")
    exp_done = semaphore("exp_done")
    probs_ready = semaphore("probs_ready")
    pt_ready = semaphore("pt_ready")
    mix_lo = semaphore("mix_lo")
    mix_ready = semaphore("mix_ready")
    x_ready = semaphore("x_ready")
    keys_landed = semaphore("keys_landed")
    q_ready = semaphore("q_ready")
    cand_raw = semaphore("cand_raw")
    cand_exp = semaphore("cand_exp")
    sel_ready = semaphore("sel_ready")
    sel_copied = semaphore("sel_copied")
    oh_ready = semaphore("oh_ready")
    oh_first = semaphore("oh_first")
    oh_passed = semaphore("oh_passed")
    gates_full = semaphore("gates_full")
    gelu_ready = semaphore("gelu_ready")
    w_ready = semaphore("w_ready")
    out_stored = semaphore("out_stored")

    at = [((nc.sbuf_base + 31) // 32) * 32]

    def place(name, shape, dt=F32, offset=None):
        size = int(np.prod(shape[1:])) * 4
        if offset is None:
            offset = at[0]
            at[0] += (size + 31) // 32 * 32
        return nc.alloc_sbuf_tensor_at(name, shape, dt, offset=offset)

    xT = place("xT", [P, KD, T])
    raw = place("raw", [P, RAW, D])
    SH = at[0]
    split_hi = place("split_hi", [P, SPLIT, KD, P], F32R)
    split_lo = place("split_lo", [P, SPLIT, KD, P], F32R)
    HB = at[0]
    h_hi = place("h_hi", [P, KD, T], F32R)
    h_lo = place("h_lo", [P, KD, T], F32R)
    CW = consts.shape[1]
    cst = place("cst", [P, CW])
    mod = place("mod", [P, DEPTH * MOD_TILES, 2])
    modA = place("modA", [P, DEPTH, 2, KD, 2])
    par = place("par", [P, DEPTH, NPAR])
    bm = place("bm", [P, DEPTH * MOD_TILES])
    lb = place("lb", [P, 8, 4])
    c_raw = place("c_raw", [P, KD, 2])
    a_wsT = place("a_wsT", [P, 4, P])
    a_bias = place("a_bias", [P, 2, P])
    a_norm = place("a_norm", [P, 256])
    small = place("small", [P, 160])
    first_key = place("first_key", [P, 4, 2])
    RB = at[0]
    assert RB + 75520 <= nc.sbuf_usable_end, (RB + 75520, nc.sbuf_usable_end)

    def in_r(name, offset, shape, dt=F32):
        assert offset + int(np.prod(shape[1:])) * 4 <= nc.sbuf_usable_end - RB, name
        return place(name, shape, dt, RB + offset)

    o = [0]

    def const(w):
        o[0] += w
        return cst[:, o[0] - w:o[0]]

    ident, ones, bones, iota = const(P), const(P), const(P), const(P)
    iota16 = const(TOPK)
    masks = const(2 * NLB * 64).rearrange("p (d l t) -> p d l t", d=2, l=NLB)
    resets = const(T + 1)
    rope_c, rope_s = const(T), const(T)
    assert o[0] == CW

    mod_w = in_r("mod_w", 0, [P, MOD_SLOTS, 2, KD, P])
    sq = in_r("sq", 0, [P, 2, T])
    root = in_r("root", 6144, [P, T])
    tmp = in_r("tmp", 9216, [P, 2, T])
    au = in_r("au", 0, [P, 2, T])
    av = in_r("av", 6144, [P, NTT, 256])
    bq = in_r("bq", 12288, [P, 2, T])
    bkv = in_r("bkv", 18432, [P, T])
    krx = in_r("krx", 21504, [P, 2, T])
    ci = in_r("ci", 27648, [P, NTT, 256])
    cq = in_r("cq", 33792, [P, 2, T])
    lf = in_r("lf", 39936, [P, 4, T])
    kk = in_r("kk", 52224, [P, 4, T])
    cg = in_r("cg", 64512, [P, 2, T])
    attm = in_r("attm", 70656, [P, 2, NLB, 64])
    attF = in_r("attF", 74240, [P, 2, P])
    attR = in_r("attR", 75264, [P, 64])
    mixF = place("mixF", [P, KD, T], F32, HB)
    HL = HB + KD * T * 4
    av_sq = place("av_sq", [P, NTT, 256], F32, HL)
    vn = place("vn", [P, NTT, 256], F32, HL + 6144)
    cb = place("cb", [P, 4, T], F32, HB + 6144)
    states = place("states", [P, 4, NTT, P], F32, HL)
    khT = place("khT", [P, NTT, 4, P], F32, HL + 12288)
    lvl_qs = (place("lvl_q0", [P, 7, 2, P], F32, HL + 12288), place("lvl_q1", [P, 7, 2, P], F32, SH),
              place("lvl_q2", [P, 7, 2, P], F32, SH + 8192))
    lvl_ks = (in_r("lvl_k0", 0, [P, 7, 2, P]), place("lvl_k1", [P, 7, 2, P], F32, SH + 16384),
              place("lvl_k2", [P, 7, 2, P], F32, SH + 16384 + 8192))
    o_sq = in_r("o_sq", 0, [P, T])
    o_rt = in_r("o_rt", 3072, [P, T])
    w_uq = in_r("w_uq", 0, [P, 2048 + 1024])
    bc = in_r("bc", 27648, [P, 4, T])
    vt = in_r("vt", 39936, [P, NTT, BH * BV])
    qn = in_r("qn", 52224, [P, 2, T])
    kn = in_r("kn", 58368, [P, 2, T])
    q_sq = in_r("q_sq", 64512, [P, T])
    k_sq = in_r("k_sq", 67584, [P, 2, T])
    b_sq = in_r("b_sq", 64512, [P, 3, T])
    q_raw = place("q_raw", [P, T], F32, HL)
    q_rot = place("q_rot", [P, T], F32, HL + 3072)
    k_raw = place("k_raw", [P, T], F32, HL + 6144)
    h_rt = place("h_rt", [P, 2, T], F32, HL + 9216)
    b_rt = place("b_rt", [P, 2, T], F32, HL + 9216)
    probs = place("probs", [P, 2, T], F32, HL + 15360)
    ptA = place("ptA", [P, T], F32, HL + 21504)
    ptB = in_r("ptB", 24576, [P, T])
    pts = (ptA, ptB)
    mix_r = in_r("mix_r", 0, [P, 2, T], F32R)
    keysT = in_r("keysT", 67328, [P, WQ_TILES, P])
    q_hp = in_r("q_hp", 8192, [P, 2, T])
    s_work = in_r("s_work", 14336, [P, NTT, P])
    sv = in_r("sv", 17408, [P, NTT, WQ_TILES, TOPK])
    si = in_r("si", 23552, [P, NTT, WQ_TILES, TOPK], U32)
    si_f = in_r("si_f", 29696, [P, NTT, WQ_TILES, TOPK])
    cand = in_r("cand", 35840, [P, PH, TOPK * TOPK])
    eq = in_r("eq", 44032, [P, P, TOPK])
    cand2 = in_r("cand2", 0, [P, PH, TOPK * TOPK])
    best = in_r("best", 53248, [P, PH, TOPK])
    best_i = in_r("best_i", 53760, [P, PH, TOPK], U32)
    ab_i = in_r("ab_i", 54272, [P, 2, PH * TOPK], U32)
    ab_f = in_r("ab_f", 55296, [P, 2, PH * TOPK])
    sel = in_r("sel", 56320, [P, 3, P])
    idxT = in_r("idxT", 58112, [P, 3, T])
    onehot = in_r("onehot", 0, [P, 4, 2, 4, P])
    g_buf = in_r("g_buf", 16384, [P, 2, P, TB])
    W_hi = in_r("W_hi", 0, [P, 2, 2, T], F32R)
    W_lo = in_r("W_lo", 12288, [P, 2, 2, T], F32R)
    gel = in_r("gel", 24576, [P, 2, T])
    g_in = in_r("g_in", 30720, [P, 2, NTB, 2 * TB])

    psV = nc.alloc_psum_tensor("psV", [P, 4, 512], F32)
    psA = nc.alloc_psum_tensor("psA", [P, 4, 512], F32)

    IN0 = [l * LAYER_TILES for l in range(DEPTH)]
    OUT0 = [n + IN_TILES for n in IN0]
    WQ0 = [n + OUT_TILES for n in OUT0]
    EX0 = [n + WQ_TILES for n in WQ0]
    uq = w_uq[:, 0:1536].rearrange("p (k n) -> p k n", k=2)
    uqr = w_uq[:, 1536:2048].rearrange("p (k n) -> p k n", k=2)
    ukv = w_uq[:, 2048:3072]
    chunk_f = list(range(NTT))
    chunk_b = [1, 0] + list(range(NTT - 1, 1, -1))


    def recurrence_units(l):
        return [(hp, s, tt, tt == (s + n) // P - 1) for hp in range(2) for s, n, _ in segs_of(l, False)
                for tt in range(s // P, (s + n) // P)]

    block = sem_ctx.enter_context(nc.Block())

    score_bank = [[] for _ in range(DEPTH)]

    @block.tensor
    def _(pe):
        seen = Counts()
        tile_n = [0]
        passed = [0]

        def mm(out_, lhsT, rhs, start, stop, last=False):
            ins = nc.tensor.matmul(out_, lhsT, rhs, start=start, stop=stop)
            if passed[0] and not last:
                ins.then_inc(tile_passed, passed[0])
                passed[0] = 0
            return ins

        def next_tile():
            n = tile_n[0]
            tile_n[0] += 1
            pe.wait_ge(hi_done, seen.upto(hi_done))
            pe.wait_ge(lo_done, seen.upto(lo_done))
            return n % SPLIT

        def three(out_, a_hi, a_lo, b_hi, b_lo, start, stop):
            mm(out_, a_hi, b_hi, start, False)
            mm(out_, a_hi, b_lo, False, False)
            return mm(out_, a_lo, b_hi, False, stop, last=stop)

        def feature_tile(ring, segs, banks=2):
            w = next_tile()
            ps, full, free = (psA, psum_A_full, psum_A_free) if ring == "A" else (psV, psum_V_full, psum_V_free)
            f = seen.bank(free)
            pe.wait_ge(free, seen.upto(free, banks))
            for b, (s, n, _) in enumerate(segs):
                for c in range(KD):
                    ins = three(ps[:, f + b, 0:n], split_hi[:, w, c], split_lo[:, w, c],
                                h_hi[:, c, s:s + n], h_lo[:, c, s:s + n], c == 0, c == KD - 1)
            ins.then_inc(full, banks)
            passed[0] += 1

        def token_tile(segs):
            w = next_tile()
            f = seen.bank(psum_A_free)
            pe.wait_ge(psum_A_free, seen.upto(psum_A_free, 2))
            for b, (s, n, _) in enumerate(segs):
                for t in range(n // P):
                    tok = slice(s + t * P, s + (t + 1) * P)
                    for c in range(KD):
                        ins = three(psA[:, f + b, t * P:(t + 1) * P], h_hi[:, c, tok], h_lo[:, c, tok],
                                    split_hi[:, w, c], split_lo[:, w, c], c == 0, c == KD - 1)
            ins.then_inc(psum_A_full, 2)
            passed[0] += 1

        def sum_rows(segs, matrix, src, steps=1, rows=P):
            f = seen.bank(psum_A_free)
            pe.wait_ge(psum_A_free, seen.upto(psum_A_free, 2))
            for b, (s, n, _) in enumerate(segs):
                for k in range(steps):
                    ins = mm(psA[0:rows, f + b, 0:n], matrix, src(k)[:, s:s + n], k == 0, k == steps - 1,
                             last=k == steps - 1)
            ins.then_inc(psum_A_full, 2)

        def modulation():
            f = seen.bank(psum_V_free)
            pe.wait_ge(psum_V_free, seen.upto(psum_V_free, 4))
            for m in range(MOD_SLOTS):
                pe.wait_ge(mod_landed[m], seen.upto(mod_landed[m], 16))
                for j in range(2):
                    for c in range(KD):
                        ins = nc.tensor.matmul(psV[:, f, 4 * m + 2 * j:4 * m + 2 * j + 2], mod_w[:, m, j, c], c_raw[:, c],
                                               start=c == 0, stop=c == KD - 1)
            ins.then_inc(psum_V_full, 4)

        def norm(l, which):
            segs = segs_of(l, which == 0)
            f = seen.bank(psum_A_free)
            pe.wait_ge(psum_A_free, seen.upto(psum_A_free, 2))
            for k in range(KD):
                pe.wait_ge(sq_ready, seen.upto(sq_ready))
                for b, (s, n, _) in enumerate(segs):
                    ins = mm(psA[:, f + b, 0:n], ones, sq[:, k % 2, s:s + n], k == 0, k == KD - 1,
                             last=b == len(segs) - 1)
                if k < KD - 2:
                    ins.then_inc(sq_used, 1)
            ins.then_inc(psum_A_full, 2)
            pe.wait_ge(h_ready, seen.upto(h_ready, KD))

        def in_projection(l):
            own, both = segs_of(l, False), segs_of(l, True)
            for t in range(IN_TILES):
                if t < 14:
                    feature_tile("A", both if t in (4, 5) or 8 <= t < 12 else own)
                else:
                    token_tile(own if t < 16 else both)

        def gated_mlp(l):
            segs = segs_of(l, False)
            pe.wait_ge(vn_ready, seen.upto(vn_ready))
            pe.wait_ge(aw_landed, seen.upto(aw_landed, 48))
            for hp in range(2):
                f = seen.bank(psum_V_free)
                pe.wait_ge(psum_V_free, seen.upto(psum_V_free, 2))
                for b, (s, n, _) in enumerate(segs):
                    for t in range(n // P):
                        tt = s // P + t
                        for hd in range(2):
                            h = 2 * hp + hd
                            ins = mm(psV[64 * hd:64 * hd + 64, f + b, t * P:(t + 1) * P], vn[:, tt, 64 * h:64 * h + 64],
                                     a_wsT[:, h], True, True, last=hd == 1)
                ins.then_inc(psum_V_full, 2)

        def hgrn(l):
            own = segs_of(l, False)
            pe.wait_ge(khat_ready, seen.upto(khat_ready))
            for tt in range(NTT):
                f = seen.bank(psum_A_free)
                pe.wait_ge(psum_A_free, seen.upto(psum_A_free, 2))
                for dt in range(4):
                    ins = nc.tensor.transpose(psA[:, f, dt * P:(dt + 1) * P], lf[:, dt, tt * P:(tt + 1) * P], ident)
                ins.then_inc(psum_A_full, 2)
            pe.wait_ge(khT_ready, seen.upto(khT_ready))
            for i in range(NTT - 1):
                f = seen.bank(psum_V_free)
                pe.wait_ge(psum_V_free, seen.upto(psum_V_free, 2))
                for d in range(2):
                    c = (chunk_f, chunk_b)[d][i]
                    for t in range(2):
                        dt = 2 * d + t
                        ins = mm(psV[:, f, dt * P:(dt + 1) * P], khT[:, c, dt], ci[:, c, t * P:(t + 1) * P],
                                 True, True, last=dt == 3)
                ins.then_inc(psum_V_full, 2)
            pe.wait_ge(qexp_ready, seen.upto(qexp_ready))
            pe.wait_ge(state_ready, seen.upto(state_ready))

            def scores(u):
                hp, _, tt, _ = units[u]
                lvl_q, lvl_k = lvl_qs[u % 3], lvl_ks[u % 3]
                pe.wait_ge(qk_ready, seen.upto(qk_ready))
                for hd in range(2):
                    r = slice(64 * hd, 64 * hd + 64)
                    f = seen.bank(psum_V_free)
                    pe.wait_ge(psum_V_free, seen.upto(psum_V_free, 2))
                    for d in range(2):
                        for half in range(2):
                            hs = slice(64 * half, 64 * half + 64)
                            cs = slice(tt * P + 64 * half, tt * P + 64 * half + 64)
                            for li in range(1, NLB):
                                mm(psV[hs, f + d, (li - 1) * 64:li * 64], lvl_k[r, li, d, hs],
                                   lvl_q[r, li, d, hs], True, True)
                            mm(psV[hs, f + d, 384:448], kk[r, 2 * d + hp, cs], cq[r, hp, cs], True, True)
                        a, b = (slice(0, 64), slice(64, 128)) if d == 0 else (slice(64, 128), slice(0, 64))
                        ins = mm(psV[a, f + d, 448:512], lvl_k[r, 0, d, a], lvl_q[r, 0, d, b], True, True,
                                 last=d == 1)
                    ins.then_inc(psum_V_full, 2)

            def output(u, fo):
                hp, s, tt, end = units[u]
                t = tt - s // P
                own_tokens = slice(tt * P, (tt + 1) * P)
                o_ = psA[:, fo, t * P:(t + 1) * P]
                ins = mm(o_, states[:, hp, tt], lf[:, hp, own_tokens], True, False, last=True)
                if u + 1 < len(units):
                    ins.then_inc(unit_passed, 1)
                mm(o_, states[:, 2 + hp, tt], lf[:, 2 + hp, own_tokens], False, False)
                for hd in range(2):
                    pe.wait_ge(att_ready, seen.upto(att_ready))
                    h = 2 * hp + hd
                    ins = mm(psA[64 * hd:64 * hd + 64, fo, t * P:(t + 1) * P], ci[:, tt, h * 64:(h + 1) * 64],
                             attF[:, hd], False, True, last=True)
                    if hd == 1 and end:
                        ins.then_inc(psum_A_full, 2)
                        pe.wait_ge(psum_A_full, seen.n[psum_A_free])
                        pe.sem_inc(att_used, 1)
                    else:
                        ins.then_inc(att_used, 1)

            units = recurrence_units(l)
            scores(0)
            pe.wait_ge(psum_V_full, seen.n[psum_V_free])
            pe.sem_inc(unit_passed, 1)
            for u, (_, s, tt, _) in enumerate(units):
                if u + 1 < len(units):
                    scores(u + 1)
                if tt == s // P:
                    fo = seen.bank(psum_A_free)
                    pe.wait_ge(psum_A_free, seen.upto(psum_A_free, 2))
                output(u, fo)
            for hp in range(2):
                pe.wait_ge(osq_ready, seen.upto(osq_ready))
                sum_rows(own, bones, lambda k: o_sq)

        def attention(l):
            own, both = segs_of(l, False), segs_of(l, True)
            pe.wait_ge(c_done, seen.upto(c_done))
            pe.wait_ge(bw_landed, seen.upto(bw_landed, 16))
            pe.wait_ge(bsq_ready, seen.upto(bsq_ready, 2))
            sum_rows(own, ones, lambda k: b_sq[:, k], 2)
            sum_rows(both, ones, lambda k: b_sq[:, 2])
            pe.wait_ge(bn_ready, seen.upto(bn_ready))
            for tt in range(NTT):
                f = seen.bank(psum_A_free)
                pe.wait_ge(psum_A_free, seen.upto(psum_A_free, 1))
                mm(psA[:, f, :], bkv[:, tt * P:(tt + 1) * P], ukv[:, 512:1024], True, True, last=True)\
                    .then_inc(psum_A_full, 1)
            pe.wait_ge(v_ready, seen.upto(v_ready))

            def project(h, part):
                for s, n, _ in own[0:1] if part == 0 else own[1:] if part == 1 else ():
                    f = seen.bank(psum_A_free)
                    pe.wait_ge(psum_A_free, seen.upto(psum_A_free, 2))
                    for k in range(2):
                        mm(psA[0:BQK, f, 0:n], uq[:, k, h * BQK:(h + 1) * BQK], bq[:, k, s:s + n], k == 0, k == 1)
                    for k in range(2):
                        ins = mm(psA[64:96, f + 1, 0:n], uqr[:, k, h * BR:(h + 1) * BR], bq[:, k, s:s + n],
                                 k == 0, k == 1, last=k == 1)
                    ins.then_inc(psum_A_full, 2)
                if part == 1:
                    f = seen.bank(psum_A_free)
                    pe.wait_ge(psum_A_free, seen.upto(psum_A_free, 2))
                    for b, (s, n, _) in enumerate(both):
                        ins = mm(psA[0:BN, f + b, 0:n], ukv[:, h * BN:(h + 1) * BN], bkv[:, s:s + n], True, True, last=b == 1)
                    ins.then_inc(psum_A_full, 2)
                if part == 2:
                    pe.wait_ge(headsq, seen.upto(headsq))
                    sum_rows(own, ones[0:BQK, 0:BQK], lambda k: q_sq[0:BQK], rows=BQK)
                    sum_rows(both, ones[0:BQK, 0:BQK], lambda k: k_sq[0:BQK, h % 2], rows=BQK)

            def scores(h, s, q):
                f = seen.bank(psum_A_free)
                pe.wait_ge(psum_A_free, seen.upto(psum_A_free, 2))
                score_bank[l].append(f)
                lhsT = qn[0:BQK, h % 2, s + q * P:s + (q + 1) * P]
                cuts = ((0, 512), (512, T)) if s else ((0, P), (P, NCTX))
                for b, (a, e) in enumerate(cuts):
                    ins = mm(psA[:, f + b, 0:e - a], lhsT, kn[0:BQK, h % 2, a:e], True, True, last=True)
                    if b == 0:
                        ins.then_inc(psum_A_full, 2)
                    else:
                        ins.then_inc(scores_ready, 1)

            def transpose(u, s):
                pe.wait_ge(probs_ready, seen.upto(probs_ready))
                f = seen.bank(psum_A_free)
                pe.wait_ge(psum_A_free, seen.upto(psum_A_free, 2))
                for j in range(NTT if s else NCTX // P):
                    ins = nc.tensor.transpose(psA[:, f + j // 4, (j % 4) * P:(j % 4 + 1) * P],
                                              probs[:, u % 2, j * P:(j + 1) * P], ident)
                ins.then_inc(psum_A_full, 2)

            def values(h, u, s, n, q, fo):
                pe.wait_ge(pt_ready, seen.upto(pt_ready))
                nt = NTT if s else NCTX // P
                end = (q + 1) * P == n
                for j in range(nt):
                    ins = mm(psV[64 * (h % 2):64 * (h % 2) + 64, fo, q * P:(q + 1) * P], vt[:, j, h * BV:(h + 1) * BV],
                             pts[u % 2][:, j * P:(j + 1) * P], j == 0, j == nt - 1, last=end and j == nt - 1)
                if end:
                    ins.then_inc(psum_V_full, 1)

            units = [(s, n, q) for s, n, _ in own for q in range(n // P)]
            u = [0]
            mod_bank = [0]

            def modulate(h, tiles_of_head):
                for i in tiles_of_head:
                    slot = (h * per_head + i) % RAW
                    if i == 0:
                        mod_bank[0] = seen.bank(psum_V_free)
                        pe.wait_ge(psum_V_free, seen.upto(psum_V_free, 1))
                    pe.wait_ge(raw_landed[slot], seen.upto(raw_landed[slot], 16))
                    for c in range(KD):
                        ins = nc.tensor.matmul(psV[:, mod_bank[0], 2 * i:2 * i + 2], raw[:, slot, c * P:(c + 1) * P],
                                               c_raw[:, c], start=c == 0, stop=c == KD - 1)
                    ins.then_inc(mod_passed, 1)

            if l == 0:
                per_head = MOD_LATER // BH
                for b in range(RAW):
                    seen.n[raw_landed[b]] = 16 * OUT0[l] // RAW

            def attend(h):
                fo = {}
                for s, n, _ in own:
                    fo[s] = seen.bank(psum_V_free)
                    pe.wait_ge(psum_V_free, seen.upto(psum_V_free, 1))
                scores(h, units[0][0], units[0][2])
                for i, (s, n, q) in enumerate(units):
                    if i + 1 < len(units):
                        scores(h, units[i + 1][0], units[i + 1][2])
                    if i:
                        s1, n1, q1 = units[i - 1]
                        values(h, u[0] - 1, s1, n1, q1, fo[s1])
                    if l == 0 and i < len(units) - 1:
                        modulate(h, range(2 * i, min(2 * i + 2, per_head - 1)))
                    transpose(u[0], s)
                    u[0] += 1
                    if i < 3 and h + 1 < BH:
                        project(h + 1, i)
                values(h, u[0] - 1, s, n, q, fo[s])
                if l == 0:
                    modulate(h, [per_head - 1])
                    pe.wait_ge(mod_passed, (h + 1) * per_head)
                    pe.sem_inc(psum_V_full, 1)

            for part in range(3):
                project(0, part)
            for h in range(BH):
                pe.wait_ge(head_ready, seen.upto(head_ready))
                attend(h)

        def out_projection(l):
            pe.wait_ge(mix_ready, seen.upto(mix_ready))
            for t in range(OUT_TILES):
                feature_tile("V", segs_of(l, False))

        def route(l):
            segs = segs_of(l, False)
            pe.wait_ge(keys_landed, seen.upto(keys_landed, 16))

            def score(t):
                pe.wait_ge(q_ready, seen.upto(q_ready))
                f = seen.bank(psum_V_free)
                pe.wait_ge(psum_V_free, seen.upto(psum_V_free, 2))
                for b, (s, n, _) in enumerate(segs):
                    for j in range(n // P):
                        ins = mm(psV[:, f + b, j * P:(j + 1) * P], q_hp[:, t % 2, s + j * P:s + (j + 1) * P],
                                 keysT[:, t], True, True, last=(j + 1) * P == n)
                ins.then_inc(psum_V_full, 2)

            for t in range(WQ_TILES):
                feature_tile("A", segs)
                if t:
                    score(t - 1)
            score(WQ_TILES - 1)
            for tt in range(segs[-1][0] // P, NTT):
                pe.wait_ge(sel_ready, seen.upto(sel_ready))
                f = seen.bank(psum_A_free)
                pe.wait_ge(psum_A_free, seen.upto(psum_A_free, 1))
                for j in range(3):
                    ins = nc.tensor.transpose(psA[:, f, j * P:(j + 1) * P], sel[:, j], ident)
                ins.then_inc(psum_A_full, 1)

        def build_gates(l):
            tb0 = 0 if l < DEPTH - 1 else NCTX // TB
            assert not passed[0]
            with pe.Fori(0, (NTB - tb0) // 2) as i:
                seen.enter(i, {oh_ready: 2 * GROUPS, oh_first: 2 * GROUPS, psum_A_free: 2 * GROUPS})
                for g in range(2 * GROUPS):
                    pe.wait_ge(oh_first, seen.upto(oh_first))
                    pe.wait_ge(oh_ready, seen.upto(oh_ready))
                    f = seen.bank(psum_A_free)
                    pe.wait_ge(psum_A_free, seen.upto(psum_A_free, 1))
                    for j in range(4):
                        ins = mm(psA[:, f, j * P:(j + 1) * P], onehot[:, g % 4, 1, j], onehot[:, g % 4, 0, j], True, True,
                                 last=True)
                        if j == 1:
                            ins.then_inc(oh_passed, 1)
                    ins.then_inc(psum_A_full, 1)
            seen.leave((NTB - tb0) // 2)

        def experts(l):
            segs = segs_of(l, False)
            banks = len(segs)

            def apply_u():
                for c in range(2):
                    feature_tile("A", segs, banks)

            def apply_v(parity):
                w = [next_tile(), next_tile()]
                for k in range(KD):
                    f = seen.bank(psum_V_free)
                    pe.wait_ge(psum_V_free, seen.upto(psum_V_free, banks))
                    for b, (s, n, _) in enumerate(segs):
                        for c in range(2):
                            ins = three(psV[:, f + b, 0:n], split_hi[:, w[c], k], split_lo[:, w[c], k],
                                        W_hi[:, parity, c, s:s + n], W_lo[:, parity, c, s:s + n], c == 0, c == 1)
                    ins.then_inc(psum_V_full, banks)
                passed[0] += 2

            apply_u()
            apply_u()
            pe.wait_ge(w_ready, seen.upto(w_ready, 2))
            apply_v(0)
            rate = {hi_done: 8, lo_done: 8, psum_A_free: 4 * banks, psum_V_free: 16 * banks, w_ready: 4}
            with pe.Fori(0, (NSUPER - 2) // 2) as i:
                seen.enter(i, rate)
                for parity in (1, 0):
                    apply_u()
                    pe.wait_ge(w_ready, seen.upto(w_ready, 2))
                    apply_v(parity)
            seen.leave((NSUPER - 2) // 2)
            tile_n[0] = EX0[l] + EXPERT_TILES - 2
            pe.wait_ge(w_ready, seen.upto(w_ready, 2))
            apply_v(1)

        pe.wait_ge(inputs_landed, seen.upto(inputs_landed, 16 * 13))
        pe.wait_ge(cond_ready, seen.upto(cond_ready))
        pe.sem_inc(oh_passed, 3)
        pe.sem_inc(psum_V_free, 4)
        pe.sem_inc(psum_A_free, 4)
        modulation()
        for l in range(DEPTH):
            norm(l, 0)
            in_projection(l)
            pe.wait_ge(proj_ready, seen.upto(proj_ready))
            gated_mlp(l)
            hgrn(l)
            attention(l)
            out_projection(l)
            norm(l, 1)
            route(l)
            build_gates(l)
            experts(l)
        pe.wait_ge(psum_V_full, seen.n[psum_V_free])

    @block.sync
    def _(sp):
        seen = Counts()

        def load(n, where=None):
            if n >= RAW:
                sp.wait_ge(hi_done, seen.at(hi_done, n - RAW + 1))
                sp.wait_ge(lo_done, seen.at(lo_done, n - RAW + 1))
            sp.dma_start(raw[:, n % RAW, :], tiles[n if where is None else where])\
               .then_inc(raw_landed[n % RAW], 16)

        def load_many(n, end):
            while n % 2 or n < RAW:
                load(n)
                n += 1
            pairs = (end - n) // 2
            with sp.Fori(0, pairs) as i:
                seen.enter(i, {hi_done: 2, lo_done: 2})
                load(n, i * 2 + n)
                load(n + 1, i * 2 + (n + 1))
            seen.leave(pairs)
            for m in range(n + 2 * pairs, end):
                load(m)

        def later_modulation(l):
            for n in range(RAW):
                sp.wait_ge(hi_done, OUT0[l] - RAW + n + 1)
                sp.wait_ge(lo_done, OUT0[l] - RAW + n + 1)
                sp.dma_start(raw[:, n, :], mod_tiles[n]).then_inc(raw_landed[n], 16)
            with sp.Fori(0, MOD_LATER // RAW - 1) as i:
                seen.enter(i, {mod_passed: RAW})
                for n in range(RAW):
                    sp.wait_ge(mod_passed, seen.upto(mod_passed))
                    sp.dma_start(raw[:, n, :], mod_tiles[i * RAW + (RAW + n)]).then_inc(raw_landed[n], 16)
            seen.leave(MOD_LATER // RAW - 1)
            for n in range(RAW):
                sp.wait_ge(mod_passed, seen.upto(mod_passed))
                sp.dma_start(raw[:, n, :], tiles[OUT0[l] + n]).then_inc(raw_landed[n], 16)

        for m in range(MOD_SLOTS):
            sp.dma_start(mod_w[:, m], mod_pairs[m]).then_inc(mod_landed[m], 16)
        done = 0
        for l in range(DEPTH):
            if l == 0:
                load_many(done, OUT0[l])
                later_modulation(l)
                done = OUT0[l] + RAW
            load_many(done, EX0[l] + 2 + RAW)
            done = EX0[l] + 2 + RAW
            tb0 = 0 if l < DEPTH - 1 else NCTX // TB
            with sp.Fori(0, (NTB - tb0) // 2) as i:
                seen.enter(i, {gates_full: 2})
                for b in range(2):
                    sp.wait_ge(gates_full, seen.upto(gates_full))
                    sp.dma_start(gates[i * 2 + (tb0 + b)], g_buf[:, b]).then_inc(g_stored[b], 16)
            seen.leave((NTB - tb0) // 2)
        load_many(done, N_TILES)

    @block.gpsimd
    def _(pool):
        seen = Counts()
        for k in range(KD):
            pool.dma_start(xT[:, k, :], x_in[:, k, :]).then_inc(inputs_landed, 16)
        for dst, src in ((cst[:], consts), (par[:], params), (bm[:], bmod), (c_raw[:], cond), (lb[:, 0:2, :], lblog)):
            pool.dma_start(dst, src).then_inc(inputs_landed, 16)

        def a_weights(l):
            pool.dma_start(a_wsT[:], aws[l]).then_inc(aw_landed, 16)
            pool.dma_start(a_bias[:], arow[l, :, 0:256]).then_inc(aw_landed, 16)
            pool.dma_start(a_norm[:], arow[l, :, 256:512]).then_inc(aw_landed, 16)

        a_weights(0)
        for b in range(2):
            seen.n[g_stored[b]] = 16
        for l in range(DEPTH):
            pool.wait_ge(a_done, seen.upto(a_done))
            pool.memset(states[:], 0.0).then_inc(states_zero, 1)
            if l + 1 < DEPTH:
                a_weights(l + 1)
            pool.wait_ge(c_done, seen.upto(c_done))
            pool.dma_start(w_uq[:], bw[l]).then_inc(bw_landed, 16)
            pool.wait_ge(mix_ready, seen.upto(mix_ready))
            pool.dma_start(keysT[:], keys[l]).then_inc(keys_landed, 16)
            tb0 = 0 if l < DEPTH - 1 else NCTX // TB
            pool.wait_ge(sel_copied, seen.upto(sel_copied, NTT - tb0 * TB // P))
            base = 3 + (0 if l == 0 else NTB * GROUPS * l)
            steps = (NTB - tb0) // 2 - 1
            nc.gpsimd.tensor_copy(first_key[:, 0], idxT[:, 0, tb0 * TB + 2:tb0 * TB + 4]).then_inc(pool_chain, 1)

            def first_one_hots(i, last):
                for g in range(2 * GROUPS):
                    pool.wait_ge(oh_passed, seen.at(oh_passed, base + g - 2 + (2 * GROUPS * steps if last else 0)))
                    pool.wait_ge(pool_chain, seen.upto(pool_chain))
                    if not last:
                        t = i * (2 * TB) + (tb0 * TB + 4 * (g + 1) + 2)
                        nc.gpsimd.tensor_copy(first_key[:, (g + 1) % 4], idxT[:, 0, bass.ds(t, 2)]).then_inc(pool_chain, 1)
                    elif g < 2 * GROUPS - 1:
                        t = T - 2 * TB + 4 * (g + 1) + 2
                        nc.gpsimd.tensor_copy(first_key[:, (g + 1) % 4], idxT[:, 0, t:t + 2]).then_inc(pool_chain, 1)
                    for j in range(2):
                        ins = nc.gpsimd.tensor_scalar(onehot[:, g % 4, 0, 2 + j], iota, first_key[:, g % 4, j:j + 1], None,
                                                      ALU.is_equal)
                    ins.then_inc(oh_first, 1)

            with pool.Fori(0, steps) as i:
                seen.enter(i, {oh_passed: 2 * GROUPS, pool_chain: 2 * GROUPS})
                first_one_hots(i, False)
            seen.leave(steps)
            first_one_hots(None, True)
            for b in range(2):
                pool.wait_ge(g_stored[b], seen.upto(g_stored[b], 16 * (NTB - tb0) // 2))

            def load_gates(s, slot):
                return pool.dma_start(g_in[:, slot, tb0:NTB, :].rearrange("p b (i t) -> p b i t", i=2),
                                     gates[tb0:NTB].rearrange("b p (s i) t -> s p b i t", i=2)[s])\
                    .then_inc(g_landed[slot], 16)

            load_gates(0, 0)
            load_gates(1, 1)
            with pool.Fori(0, NSUPER // 2 - 1) as i:
                seen.enter(i, {w_ready: 4})
                for b in range(2):
                    pool.wait_ge(w_ready, seen.upto(w_ready, 2))
                    load_gates(i * 2 + (2 + b), b)
            seen.leave(NSUPER // 2 - 1)
            pool.wait_ge(w_ready, seen.upto(w_ready, 4))
        pool.wait_ge(x_ready, seen.upto(x_ready, 1 + 2 * DEPTH))
        pool.dma_start(out, xT[:, :, NCTX:T]).then_inc(out_stored, 16)
        pool.wait_ge(out_stored, 16)

    @block.scalar
    def _(act):
        seen = Counts()
        seen.n[psum_A_free] = 4
        A = nc.scalar.activation
        splits = [0]

        def split_to(end):
            while splits[0] < end:
                n = splits[0]
                splits[0] += 1
                act.wait_ge(raw_landed[n % RAW], seen.upto(raw_landed[n % RAW], 16))
                if n >= SPLIT:
                    act.wait_ge(tile_passed, seen.at(tile_passed, n - SPLIT + 1))
                A(split_hi[:, n % SPLIT].rearrange("p k n -> p (k n)"), raw[:, n % RAW, :], ACT.Copy).then_inc(hi_done, 1)
                act.wait_ge(hi_done, seen.upto(hi_done))

        def pair(f):
            return psA[:, f:f + 2, :].rearrange("p b n -> p (b n)")

        def norm(l, which):
            segs = segs_of(l, which == 0)
            t0 = segs[-1][0]
            for k in range(KD):
                if k >= 2:
                    act.wait_ge(sq_used, seen.upto(sq_used))
                A(sq[:, k % 2, t0:T], xT[:, k, t0:T], ACT.Square).then_inc(sq_ready, 1)
                act.wait_ge(sq_ready, seen.upto(sq_ready))
            f = seen.bank(psum_A_full)
            act.wait_ge(psum_A_full, seen.upto(psum_A_full, 2))
            for b, (s, n, _) in enumerate(segs):
                ins = A(root[:, s:s + n], psA[:, f + b, 0:n], ACT.Ln, bias=EPS_COL, scale=1.0 / D)
            ins.then_inc(psum_A_free, 2)
            act.wait_ge(psum_A_free, seen.upto(psum_A_free, 2))
            A(root[:, t0:T], root[:, t0:T], ACT.Exp, scale=-0.5).then_inc(root_ready, 1)
            act.wait_ge(root_ready, seen.upto(root_ready))
            for k in range(KD):
                act.wait_ge(tmp_ready, seen.upto(tmp_ready))
                for s, n, j in segs:
                    shift = mod[:, l * 48 + which * 24 + k, j:j + 1]
                    ins = A(h_hi[:, k, s:s + n], tmp[:, k % 2, s:s + n], ACT.Identity, bias=shift)
                ins.then_inc(hhi_ready, 1)
                act.wait_ge(hhi_ready, seen.upto(hhi_ready))

        def copy_pair(f, segs, fn, dst, rows=slice(0, P), src_rows=None, **kw):
            src_rows = src_rows or rows
            for b, (s, n, _) in enumerate(segs):
                ins = A(dst[rows, s:s + n], psA[src_rows, f + b, 0:n], fn, **kw)
            return ins

        def in_projection(l):
            own = segs_of(l, False)
            both = segs_of(l, True)
            for t in range(IN_TILES):
                split_to(min(IN0[l] + t + 3, OUT0[l]))
                f = seen.bank(psum_A_full)
                act.wait_ge(psum_A_full, seen.upto(psum_A_full, 2))
                if t < 2:
                    ins = copy_pair(f, own, ACT.Copy, au[:, t])
                elif t < 4:
                    ins = copy_pair(f, own, ACT.Copy, bq[:, t - 2])
                elif t == 4:
                    ins = copy_pair(f, both, ACT.Copy, bkv[:])
                elif t == 5:
                    copy_pair(f, both, ACT.Copy, krx[:, 0], slice(64, 96))
                    ins = copy_pair(f, both, ACT.Copy, krx[:, 1], slice(64, 96), slice(96, 128))
                elif t < 8:
                    ins = copy_pair(f, own, ACT.Copy, cq[:, t - 6], scale=0.125)
                elif t < 12:
                    copy_pair(f, both, ACT.Sigmoid, lf[:, t - 8])
                    ins = copy_pair(f, both, ACT.Sigmoid, kk[:, t - 8], scale=-1.0)
                elif t < 14:
                    ins = copy_pair(f, own, ACT.Silu, cg[:, t - 12])
                else:
                    dst = (av, ci)[(t - 14) // 2]
                    c0 = (t % 2) * P
                    segs = own if t < 16 else both
                    for b, (s, n, _) in enumerate(segs):
                        ins = A(dst[:, s // P:(s + n) // P, c0:c0 + P],
                                psA[:, f + b, 0:n].rearrange("p (t c) -> p t c", c=P), ACT.Copy)
                ins.then_inc(psum_A_free, 2)
                act.wait_ge(psum_A_free, seen.upto(psum_A_free, 2))
            act.sem_inc(proj_ready, 1)

        def gated_mlp(l):
            t0 = 0 if l < DEPTH - 1 else NCTX // P
            A(av_sq[:, t0:], av[:, t0:], ACT.Square).then_inc(av_squared, 1)
            act.wait_ge(av_squared, seen.upto(av_squared))
            act.wait_ge(a_sums, seen.upto(a_sums))
            A(small[:, 24:48], small[:, 0:24], ACT.Ln, bias=EPS_COL, scale=1.0 / 64).then_inc(act_chain, 1)
            act.wait_ge(act_chain, seen.upto(act_chain))
            A(small[:, 24:48], small[:, 24:48], ACT.Exp, scale=-0.5).then_inc(a_root, 1)
            act.wait_ge(a_root, seen.upto(a_root))

        def hgrn(l):
            own = segs_of(l, False)
            act.wait_ge(f_ready, seen.upto(f_ready))
            A(lf[:], lf[:], ACT.Ln).then_inc(logf_ready, 1)
            act.wait_ge(logf_ready, seen.upto(logf_ready))
            act.wait_ge(e_raw, seen.upto(e_raw))
            A(lf[:], lf[:], ACT.Exp, scale=-1.0).then_inc(e_exp, 1)
            act.wait_ge(e_exp, seen.upto(e_exp))
            for tt in range(NTT):
                f = seen.bank(psum_A_full)
                act.wait_ge(psum_A_full, seen.upto(psum_A_full, 2))
                A(khT[:, tt].rearrange("p d n -> p (d n)"), psA[:, f, :], ACT.Copy).then_inc(psum_A_free, 2)
                act.wait_ge(psum_A_free, seen.upto(psum_A_free, 2))
            act.sem_inc(khT_ready, 1)
            A(lf[:], cb[:], ACT.Exp).then_inc(gx_exp, 1)
            act.wait_ge(gx_exp, seen.upto(gx_exp))

            def decays(u):
                lvl_q = lvl_qs[u % 3]
                act.wait_ge(lvl_raw, seen.upto(lvl_raw))
                A(lvl_q[:], lvl_q[:], ACT.Abs).then_inc(act_chain, 1)
                act.wait_ge(act_chain, seen.upto(act_chain))
                A(lvl_q[:], lvl_q[:], ACT.Exp, scale=-1.0).then_inc(lvl_exp, 1)
                act.wait_ge(lvl_exp, seen.upto(lvl_exp))

            units = recurrence_units(l)
            decays(0)
            for u, (hp, s, tt, end) in enumerate(units):
                if u + 1 < len(units):
                    decays(u + 1)
                if end:
                    f = seen.bank(psum_A_full)
                    act.wait_ge(psum_A_full, seen.upto(psum_A_full, 2))
                    n = (tt + 1) * P - s
                    A(mixF[:, 6 + hp, s:s + n], psA[:, f, 0:n], ACT.Copy).then_inc(psum_A_free, 2)
                    act.wait_ge(psum_A_free, seen.upto(psum_A_free, 2))
            t0 = own[-1][0]
            for hp in range(2):
                if hp:
                    act.wait_ge(o_raw, seen.upto(o_raw))
                A(o_sq[:, t0:T], mixF[:, 6 + hp, t0:T], ACT.Square).then_inc(osq_ready, 1)
                act.wait_ge(osq_ready, seen.upto(osq_ready))
                f = seen.bank(psum_A_full)
                act.wait_ge(psum_A_full, seen.upto(psum_A_full, 2))
                for b, (s, n, _) in enumerate(own):
                    ins = A(o_rt[:, s:s + n], psA[:, f + b, 0:n], ACT.Ln, bias=EPS_COL, scale=1.0 / 64)
                ins.then_inc(psum_A_free, 2)
                act.wait_ge(psum_A_free, seen.upto(psum_A_free, 2))
                A(o_rt[:, t0:T], o_rt[:, t0:T], ACT.Exp, scale=-0.5).then_inc(o_root, 1)
                act.wait_ge(o_root, seen.upto(o_root))

        def attention(l):
            own, both = segs_of(l, False), segs_of(l, True)
            t0 = own[-1][0]
            act.wait_ge(c_done, seen.upto(c_done))
            A(b_sq[:, 0:2, t0:T], bq[:, :, t0:T], ACT.Square).then_inc(bsq_ready, 1)
            act.wait_ge(bsq_ready, seen.upto(bsq_ready))
            A(b_sq[:, 2, :], bkv[:], ACT.Square).then_inc(bsq_ready, 1)
            act.wait_ge(bsq_ready, seen.upto(bsq_ready))
            for j, (segs, width) in enumerate(((own, 256), (both, 128))):
                f = seen.bank(psum_A_full)
                act.wait_ge(psum_A_full, seen.upto(psum_A_full, 2))
                for b, (s, n, _) in enumerate(segs):
                    ins = A(b_rt[:, j, s:s + n], psA[:, f + b, 0:n], ACT.Ln, bias=EPS_COL, scale=1.0 / width)
                ins.then_inc(psum_A_free, 2)
                act.wait_ge(psum_A_free, seen.upto(psum_A_free, 2))
            A(b_rt[:, 0, t0:T], b_rt[:, 0, t0:T], ACT.Exp, scale=-0.5)
            A(b_rt[:, 1], b_rt[:, 1], ACT.Exp, scale=-0.5).then_inc(b_root, 1)
            act.wait_ge(b_root, seen.upto(b_root))
            for tt in range(NTT):
                f = seen.bank(psum_A_full)
                act.wait_ge(psum_A_full, seen.upto(psum_A_full, 1))
                A(vt[:, tt, :], psA[:, f, :], ACT.Copy).then_inc(psum_A_free, 1)
                act.wait_ge(psum_A_free, seen.upto(psum_A_free, 1))
            act.sem_inc(v_ready, 1)
            for j in range(2):
                ins = A(k_sq[64:96, j, :], krx[64:96, 0, :], ACT.Square)
            ins.then_inc(kr_squared, 1)
            act.wait_ge(kr_squared, seen.upto(kr_squared))

            def project(h, part):
                if part == 0 and h:
                    act.wait_ge(head_ready, seen.upto(head_ready))
                for s, n, _ in own[0:1] if part == 0 else own[1:] if part == 1 else ():
                    f = seen.bank(psum_A_full)
                    act.wait_ge(psum_A_full, seen.upto(psum_A_full, 2))
                    A(q_raw[0:BQK, s:s + n], psA[0:BQK, f, 0:n], ACT.Copy)
                    A(q_sq[0:BQK, s:s + n], psA[0:BQK, f, 0:n], ACT.Square)
                    A(q_rot[64:96, s:s + n], psA[64:96, f + 1, 0:n], ACT.Copy).then_inc(psum_A_free, 2)
                    act.wait_ge(psum_A_free, seen.upto(psum_A_free, 2))
                if part == 1:
                    f = seen.bank(psum_A_full)
                    act.wait_ge(psum_A_full, seen.upto(psum_A_full, 2))
                    for b, (s, n, _) in enumerate(both):
                        A(k_raw[0:BN, s:s + n], psA[0:BN, f + b, 0:n], ACT.Copy)
                        ins = A(k_sq[0:BN, h % 2, s:s + n], psA[0:BN, f + b, 0:n], ACT.Square)
                    ins.then_inc(psum_A_free, 2)
                    act.wait_ge(psum_A_free, seen.upto(psum_A_free, 2))
                    act.sem_inc(headsq, 1)
                if part == 2:
                    f = seen.bank(psum_A_full)
                    act.wait_ge(psum_A_full, seen.upto(psum_A_full, 2))
                    for b, (s, n, _) in enumerate(own):
                        ins = A(h_rt[0:BQK, 0, s:s + n], psA[0:BQK, f + b, 0:n], ACT.Ln, bias=EPS96_COL[0:BQK], scale=1.0)
                    ins.then_inc(psum_A_free, 2)
                    act.wait_ge(psum_A_free, seen.upto(psum_A_free, 2))
                    f = seen.bank(psum_A_full)
                    act.wait_ge(psum_A_full, seen.upto(psum_A_full, 2))
                    for b, (s, n, _) in enumerate(both):
                        ins = A(h_rt[0:BQK, 1, s:s + n], psA[0:BQK, f + b, 0:n], ACT.Ln, bias=EPS_COL[0:BQK], scale=1.0 / BQK)
                    ins.then_inc(psum_A_free, 2)
                    act.wait_ge(psum_A_free, seen.upto(psum_A_free, 2))
                    A(h_rt[0:BQK, 0, t0:T], h_rt[0:BQK, 0, t0:T], ACT.Exp, scale=-0.5)
                    A(h_rt[0:BQK, 1], h_rt[0:BQK, 1], ACT.Exp, scale=-0.5).then_inc(head_root, 1)
                    act.wait_ge(head_root, seen.upto(head_root))

            units = [(s, n, q) for s, n, _ in own for q in range(n // P)]

            def evacuate(u, nkeys):
                f = seen.bank(psum_A_full)
                act.wait_ge(psum_A_full, seen.upto(psum_A_full, 2))
                A(pts[u % 2][:, 0:nkeys], pair(f)[:, 0:nkeys], ACT.Copy).then_inc(psum_A_free, 2)
                act.wait_ge(psum_A_free, seen.upto(psum_A_free, 2))
                act.sem_inc(pt_ready, 1)

            u = [0]

            def exponent(i):
                s, n, q = units[i]
                f = seen.bank(psum_A_full)
                act.wait_ge(psum_A_full, seen.upto(psum_A_full, 2))
                act.wait_ge(negmax_ready, seen.upto(negmax_ready))
                b = (u[0] + i) % 2
                if s:
                    src, dst = pair(f)[:, 0:T], probs[:, b, :]
                else:
                    src, dst = psA[:, f:f + 2, 0:P], probs[:, b, 0:NCTX].rearrange("p (b n) -> p b n", b=2)
                A(dst, src, ACT.Exp, bias=small[:, 48 + b:49 + b], accum_out=small[:, 50 + b:51 + b]).then_inc(psum_A_free, 2)
                act.wait_ge(psum_A_free, seen.upto(psum_A_free, 2))
                act.sem_inc(exp_done, 1)

            def attend(h):
                exponent(0)
                for i, (s, n, q) in enumerate(units):
                    if i + 1 < len(units):
                        exponent(i + 1)
                    evacuate(u[0] + i, T if s else NCTX)
                    if i < 3 and h + 1 < BH:
                        project(h + 1, i)
                u[0] += len(units)

            for part in range(3):
                project(0, part)
            for h in range(BH):
                attend(h)
            act.wait_ge(head_ready, seen.upto(head_ready))
            if l == 0:
                for b in range(RAW):
                    seen.n[raw_landed[b]] += 16 * MOD_LATER // RAW

        def mix_split():
            for k in range(KD):
                act.wait_ge(mix_lo, seen.upto(mix_lo))
                ins = A(h_hi[:, k, T0[0]:T], mixF[:, k, T0[0]:T], ACT.Copy)
            ins.then_inc(mix_ready, 1)
            act.wait_ge(mix_ready, seen.upto(mix_ready))

        def route(l):
            segs = segs_of(l, False)
            for t in range(WQ_TILES):
                split_to(min(WQ0[l] + t + 3, EX0[l] + 2))
                f = seen.bank(psum_A_full)
                act.wait_ge(psum_A_full, seen.upto(psum_A_full, 2))
                copy_pair(f, segs, ACT.Copy, q_hp[:, t % 2]).then_inc(psum_A_free, 2)
                act.wait_ge(psum_A_free, seen.upto(psum_A_free, 2))
                act.sem_inc(q_ready, 1)
            for tt in range(segs[-1][0] // P, NTT):
                act.wait_ge(cand_raw, seen.upto(cand_raw))
                A(best[:], best[:], ACT.Exp).then_inc(cand_exp, 1)
                act.wait_ge(cand_exp, seen.upto(cand_exp))
                f = seen.bank(psum_A_full)
                act.wait_ge(psum_A_full, seen.upto(psum_A_full, 1))
                A(idxT[:, :, tt * P:(tt + 1) * P],
                                psA[:, f, 0:384].rearrange("p (j t) -> p j t", j=3), ACT.Copy).then_inc(psum_A_free, 1)
                act.wait_ge(psum_A_free, seen.upto(psum_A_free, 1))
                act.sem_inc(sel_copied, 1)

        def build_gates(l):
            tb0 = 0 if l < DEPTH - 1 else NCTX // TB
            with act.Fori(0, (NTB - tb0) // 2) as i:
                seen.enter(i, {psum_A_full: 2 * GROUPS, psum_A_free: 2 * GROUPS, g_stored[0]: 16, g_stored[1]: 16})
                for b in range(2):
                    act.wait_ge(g_stored[b], seen.at(g_stored[b], seen.n[g_stored[b]]))
                    seen.n[g_stored[b]] += 16
                    for g in range(GROUPS):
                        f = seen.bank(psum_A_full)
                        act.wait_ge(psum_A_full, seen.upto(psum_A_full, 1))
                        A(g_buf[:, b, :, 4 * g:4 * g + 4],
                                        psA[:, f, :].rearrange("p (t i) -> p i t", t=4), ACT.Copy).then_inc(psum_A_free, 1)
                        act.wait_ge(psum_A_free, seen.upto(psum_A_free, 1))
                    act.sem_inc(gates_full, 1)
            seen.leave((NTB - tb0) // 2)

        def experts(l):
            segs = segs_of(l, False)
            banks = len(segs)

            def gelus():
                for c in range(2):
                    f = seen.bank(psum_A_full)
                    act.wait_ge(psum_A_full, seen.upto(psum_A_full, banks))
                    act.wait_ge(w_ready, seen.at(w_ready, seen.n[w_ready]))
                    seen.n[w_ready] += 1
                    copy_pair(f, segs, ACT.Gelu, gel[:, c]).then_inc(psum_A_free, banks)
                    act.wait_ge(psum_A_free, seen.upto(psum_A_free, banks))
                    act.sem_inc(gelu_ready, 1)

            def body(gelu=True):
                base = splits[0]
                split_to(base + 2)
                if gelu:
                    gelus()
                split_to(base + 4 if gelu else base + 2)

            for b in range(2):
                act.wait_ge(g_stored[b], seen.at(g_stored[b], seen.n[g_stored[b]]))
            for c in range(2):
                f = seen.bank(psum_A_full)
                act.wait_ge(psum_A_full, seen.upto(psum_A_full, banks))
                copy_pair(f, segs, ACT.Gelu, gel[:, c]).then_inc(psum_A_free, banks)
                act.wait_ge(psum_A_free, seen.upto(psum_A_free, banks))
                act.sem_inc(gelu_ready, 1)
            seen.n[w_ready] = l * 2 * NSUPER + 1
            split_to(EX0[l] + 4)
            body()
            rate = {raw_landed[0]: 64, raw_landed[1]: 64, tile_passed: 8, hi_done: 8, psum_A_full: 4 * banks,
                    psum_A_free: 4 * banks, w_ready: 4}
            first = splits[0]
            with act.Fori(0, (NSUPER - 2) // 2) as i:
                seen.enter(i, rate)
                body()
                body()
            seen.leave((NSUPER - 2) // 2)
            splits[0] = first + 4 * (NSUPER - 2)
            split_to(min(EX0[l] + EXPERT_TILES + 2, N_TILES))

        for b in range(2):
            act.sem_inc(g_stored[b], 16)
            seen.n[g_stored[b]] = 16
        EPS_COL, EPS96_COL = small[:, 150:151], small[:, 151:152]
        act.wait_ge(inputs_landed, seen.upto(inputs_landed, 16 * 13))
        A(c_raw[:], c_raw[:], ACT.Silu).then_inc(cond_ready, 1)
        act.wait_ge(cond_ready, seen.upto(cond_ready))
        act.wait_ge(mod_ready, seen.upto(mod_ready))
        A(lb[:, 3:5, :], lb[:, 3:5, :], ACT.Exp).then_inc(lb_exp, 1)
        act.wait_ge(lb_exp, seen.upto(lb_exp))
        T0 = [0]
        for l in range(DEPTH):
            T0[0] = segs_of(l, False)[-1][0]
            act.wait_ge(x_ready, seen.upto(x_ready))
            norm(l, 0)
            in_projection(l)
            gated_mlp(l)
            hgrn(l)
            attention(l)
            mix_split()
            for t in range(OUT_TILES):
                split_to(OUT0[l] + t + 3)
            act.wait_ge(x_ready, seen.upto(x_ready))
            norm(l, 1)
            route(l)
            build_gates(l)
            experts(l)

    @block.vector
    def _(dve):
        seen = Counts()
        seen.n[psum_V_free] = 4
        V = nc.vector
        splits = [0]

        def split_one():
            n = splits[0]
            splits[0] += 1
            dve.wait_ge(raw_landed[n % RAW], seen.upto(raw_landed[n % RAW], 16))
            if n >= SPLIT:
                dve.wait_ge(tile_passed, seen.at(tile_passed, n - SPLIT + 1))
            dve.wait_ge(hi_done, seen.upto(hi_done))
            V.tensor_tensor(split_lo[:, n % SPLIT].rearrange("p k n -> p (k n)"), raw[:, n % RAW, :],
                            split_hi[:, n % SPLIT].rearrange("p k n -> p (k n)").bitcast(F32), ALU.subtract).then_inc(lo_done, 1)
            dve.wait_ge(lo_done, seen.upto(lo_done))

        def split_to(end):
            while splits[0] < end:
                split_one()

        def norm(l, which):
            segs = segs_of(l, which == 0)
            t0 = segs[-1][0]
            dve.wait_ge(root_ready, seen.upto(root_ready))

            def lo(k):
                dve.wait_ge(hhi_ready, seen.upto(hhi_ready))
                for s, n, j in segs:
                    shift = mod[:, l * 48 + which * 24 + k, j:j + 1]
                    ins = V.scalar_tensor_tensor(h_lo[:, k, s:s + n], tmp[:, k % 2, s:s + n], shift,
                                                 h_hi[:, k, s:s + n].bitcast(F32), ALU.add, ALU.subtract)
                ins.then_inc(h_ready, 1)
                dve.wait_ge(h_ready, seen.upto(h_ready))

            for k in range(KD):
                for s, n, j in segs:
                    ins = V.scalar_tensor_tensor(tmp[:, k % 2, s:s + n], xT[:, k, s:s + n],
                                                 modA[:, l, which, k, j:j + 1], root[:, s:s + n], ALU.mult, ALU.mult)
                ins.then_inc(tmp_ready, 1)
                dve.wait_ge(tmp_ready, seen.upto(tmp_ready))
                if k:
                    lo(k - 1)
            lo(KD - 1)

        def gated_mlp(l):
            t0 = 0 if l < DEPTH - 1 else NCTX // P
            dve.wait_ge(av_squared, seen.upto(av_squared))
            V.tensor_reduce(small[:, 4 * t0:24], av_sq[:, t0:].rearrange("p t (h c) -> p (t h) c", c=64), AX.X, ALU.add).then_inc(a_sums, 1)
            dve.wait_ge(a_sums, seen.upto(a_sums))
            dve.wait_ge(a_root, seen.upto(a_root))
            v4 = vn[:, t0:].rearrange("p t (h c) -> p (t h) c", c=64)
            V.tensor_tensor(v4, av[:, t0:].rearrange("p t (h c) -> p (t h) c", c=64),
                                     small[:, 24 + 4 * t0:48].unsqueeze(2).broadcast_to([P, 24 - 4 * t0, 64]), ALU.mult).then_inc(dve_chain, 1)
            dve.wait_ge(dve_chain, seen.upto(dve_chain))
            dve.wait_ge(aw_landed, seen.upto(aw_landed, 48))
            V.tensor_tensor(vn[:, t0:], vn[:, t0:], a_norm[:].unsqueeze(1).broadcast_to([P, NTT - t0, 256]), ALU.mult).then_inc(vn_ready, 1)
            dve.wait_ge(vn_ready, seen.upto(vn_ready))
            segs = segs_of(l, False)
            for hp in range(2):
                f = seen.bank(psum_V_full)
                dve.wait_ge(psum_V_full, seen.upto(psum_V_full, 2))
                for b, (s, n, _) in enumerate(segs):
                    ins = V.tensor_tensor(mixF[:, hp, s:s + n].rearrange("p (t c) -> p t c", c=P),
                                          psV[:, f + b, 0:n].rearrange("p (t c) -> p t c", c=P),
                                          a_bias[:, hp].unsqueeze(1).broadcast_to([P, n // P, P]), ALU.add)
                ins.then_inc(psum_V_free, 2)
                dve.wait_ge(psum_V_free, seen.upto(psum_V_free, 2))
            t0 = t0 * P
            V.tensor_tensor(mixF[:, 0:2, t0:T], mixF[:, 0:2, t0:T], au[:, :, t0:T], ALU.mult).then_inc(dve_chain, 1)
            dve.wait_ge(dve_chain, seen.upto(dve_chain))
            dve.sem_inc(a_done, 1)

        def hgrn(l):
            own = segs_of(l, False)
            if l == DEPTH - 1:
                for dt in range(4):
                    V.tensor_scalar(lf[:, dt], lf[:, dt], lb[:, 6, dt:dt + 1], lb[:, 5, dt:dt + 1], ALU.mult, ALU.add)
                    ins = V.tensor_scalar(kk[:, dt], kk[:, dt], lb[:, 6, dt:dt + 1], None, ALU.mult)
                ins.then_inc(dve_chain, 1)
                dve.wait_ge(dve_chain, seen.upto(dve_chain))
            V.tensor_scalar(lf[:], lf[:], 2.0 ** -64, None, ALU.max).then_inc(f_ready, 1)
            dve.wait_ge(f_ready, seen.upto(f_ready))
            dve.wait_ge(logf_ready, seen.upto(logf_ready))
            for dt in range(4):
                if dt < 2:
                    ins = V.tensor_tensor_scan(cb[:, dt], resets[:, 0:T], lf[:, dt], 0.0, ALU.mult, ALU.add)
                else:
                    ins = V.tensor_tensor_scan(cb[:, dt, ::-1], resets[:, 1:T + 1][:, ::-1], lf[:, dt, ::-1], 0.0,
                                               ALU.mult, ALU.add)
            ins.then_inc(dve_chain, 1)
            dve.wait_ge(dve_chain, seen.upto(dve_chain))
            for dt in range(4):
                b4 = cb[:, dt].rearrange("p (c t) -> p c t", t=P)
                end = b4[:, :, P - 1:P] if dt < 2 else b4[:, :, 0:1]
                ins = V.tensor_tensor(lf[:, dt].rearrange("p (c t) -> p c t", t=P), b4,
                                      end.broadcast_to([P, NTT, P]), ALU.subtract)
            ins.then_inc(e_raw, 1)
            dve.wait_ge(e_raw, seen.upto(e_raw))
            dve.wait_ge(e_exp, seen.upto(e_exp))
            V.tensor_tensor(lf[:], lf[:], kk[:], ALU.mult).then_inc(khat_ready, 1)
            dve.wait_ge(khat_ready, seen.upto(khat_ready))
            dve.wait_ge(khT_ready, seen.upto(khT_ready))
            dve.wait_ge(gx_exp, seen.upto(gx_exp))
            for d in range(2):
                col = P - 1 if d == 0 else 0
                ins = V.tensor_copy(small[:, 52 + 12 * d:64 + 12 * d].rearrange("p (a c) -> p a c", a=2),
                                    lf[:, 2 * d:2 * d + 2, col::P])
            ins.then_inc(dve_chain, 1)
            dve.wait_ge(dve_chain, seen.upto(dve_chain))
            t0 = own[-1][0]
            for d in range(2):
                ins = V.tensor_tensor(lf[:, 2 * d:2 * d + 2, t0:T], lf[:, 2 * d:2 * d + 2, t0:T], cq[:, :, t0:T], ALU.mult)
            ins.then_inc(qexp_ready, 1)
            dve.wait_ge(qexp_ready, seen.upto(qexp_ready))
            dve.wait_ge(states_zero, seen.upto(states_zero))
            for i in range(NTT - 1):
                f = seen.bank(psum_V_full)
                dve.wait_ge(psum_V_full, seen.upto(psum_V_full, 2))
                for d in range(2):
                    order = chunk_f if d == 0 else chunk_b
                    c, nxt = order[i], order[i + 1]
                    for t in range(2):
                        dt = 2 * d + t
                        for r in (slice(0, 64), slice(64, 128)):
                            ins = V.scalar_tensor_tensor(
                                states[r, dt, nxt, r], states[r, dt, c, r], small[r, 52 + 6 * dt + c:53 + 6 * dt + c],
                                psV[r, f, dt * P + r.start:dt * P + r.stop], ALU.mult, ALU.add)
                ins.then_inc(psum_V_free, 2)
                dve.wait_ge(psum_V_free, seen.upto(psum_V_free, 2))
            dve.sem_inc(state_ready, 1)
            units = recurrence_units(l)

            def log_decays(u):
                hp, _, tt, _ = units[u]
                lvl_q = lvl_qs[u % 3]
                if u >= 3:
                    dve.wait_ge(unit_passed, seen.upto(unit_passed))
                for li, m in enumerate(LEVELS):
                    for d in range(2):
                        b3 = cb[:, 2 * d + hp, tt * P:(tt + 1) * P].rearrange("p (b t) -> p b t", t=2 * m)
                        ref = b3[:, :, m - 1:m] if d == 0 else b3[:, :, m:m + 1]
                        ins = V.tensor_tensor(lvl_q[:, li, d].rearrange("p (b t) -> p b t", t=2 * m), b3,
                                              ref.broadcast_to([P, P // (2 * m), 2 * m]), ALU.subtract)
                ins.then_inc(lvl_raw, 1)
                dve.wait_ge(lvl_raw, seen.upto(lvl_raw))

            def decayed(u):
                hp, _, tt, _ = units[u]
                lvl_q, lvl_k = lvl_qs[u % 3], lvl_ks[u % 3]
                c0 = tt * P
                dve.wait_ge(lvl_exp, seen.upto(lvl_exp))
                V.tensor_tensor(lvl_k[:], lvl_q[:],
                                kk[:, hp:4:2, c0:c0 + P].unsqueeze(1).broadcast_to([P, 7, 2, P]), ALU.mult)
                flat = lvl_q[:].rearrange("p l d t -> p (l d) t")
                V.tensor_tensor(flat, flat, cq[:, hp, c0:c0 + P].unsqueeze(1).broadcast_to([P, 14, P]),
                                ALU.mult).then_inc(qk_ready, 1)
                dve.wait_ge(qk_ready, seen.upto(qk_ready))

            def scores(u):
                for hd in range(2):
                    f = seen.bank(psum_V_full)
                    dve.wait_ge(psum_V_full, seen.upto(psum_V_full, 2))
                    if u:
                        dve.wait_ge(att_used, seen.upto(att_used))
                    V.tensor_tensor(attm[:], psV[:, f:f + 2, 0:448].rearrange("p d (l t) -> p d l t", l=NLB),
                                    masks, ALU.mult).then_inc(dve_chain, 1)
                    dve.wait_ge(dve_chain, seen.upto(dve_chain))
                    V.tensor_reduce(attR[:], attm[:].rearrange("p d l t -> p t (d l)"), AX.X, ALU.add).then_inc(dve_chain, 1)
                    dve.wait_ge(dve_chain, seen.upto(dve_chain))
                    F = attF[:, hd]
                    V.tensor_copy(F[0:64, 0:64], attR[0:64, :])
                    V.tensor_copy(F[64:128, 64:128], attR[64:128, :])
                    V.tensor_copy(F[0:64, 64:128], psV[0:64, f, 448:512])
                    V.tensor_copy(F[64:128, 0:64], psV[64:128, f + 1, 448:512]).then_inc(psum_V_free, 2)
                    dve.wait_ge(psum_V_free, seen.upto(psum_V_free, 2))
                    dve.sem_inc(att_ready, 1)

            log_decays(0)
            log_decays(1)
            decayed(0)
            for u in range(1, len(units)):
                if u + 1 < len(units):
                    log_decays(u + 1)
                decayed(u)
                scores(u - 1)
            scores(len(units) - 1)
            dve.wait_ge(att_used, seen.upto(att_used, 2))
            dve.wait_ge(unit_passed, seen.upto(unit_passed, 3))
            for hp in range(2):
                dve.wait_ge(o_root, seen.upto(o_root))
                V.scalar_tensor_tensor(mixF[:, 6 + hp, t0:T], mixF[:, 6 + hp, t0:T],
                                                par[:, l, PAR["conorm"]:PAR["conorm"] + 1], o_rt[:, t0:T], ALU.mult, ALU.mult).then_inc(dve_chain, 1)
                dve.wait_ge(dve_chain, seen.upto(dve_chain))
                V.tensor_tensor(mixF[:, 6 + hp, t0:T], mixF[:, 6 + hp, t0:T], cg[:, hp, t0:T], ALU.mult).then_inc(dve_chain, 1)
                dve.wait_ge(dve_chain, seen.upto(dve_chain))
                if hp == 0:
                    dve.sem_inc(o_raw, 1)
            dve.sem_inc(c_done, 1)

        def attention(l):
            own, both = segs_of(l, False), segs_of(l, True)
            t0 = own[-1][0]

            def pcol(name, rows=slice(0, P), i=0):
                return par[rows, l, PAR[name] + i:PAR[name] + i + 1]

            R = slice(64, 96)
            for j, (tab, w) in enumerate(((rope_c, "qhw"), (rope_s, "qrw"), (rope_c, "khw"), (rope_s, "krw"))):
                ins = V.tensor_scalar(bc[R, j], tab[R, :], pcol(w, R), None, ALU.mult)
            dve.wait_ge(b_root, seen.upto(b_root))
            for k in range(2):
                V.scalar_tensor_tensor(bq[:, k, t0:T], bq[:, k, t0:T], pcol("bqn", i=k), b_rt[:, 0, t0:T], ALU.mult, ALU.mult)
            V.scalar_tensor_tensor(bkv[:], bkv[:], pcol("bkvn"), b_rt[:, 1], ALU.mult, ALU.mult).then_inc(bn_ready, 1)
            dve.wait_ge(bn_ready, seen.upto(bn_ready))
            dve.wait_ge(kr_squared, seen.upto(kr_squared))
            V.tensor_tensor(krx[R, 0], krx[R, 0], bc[R, 2], ALU.mult)
            V.tensor_tensor(krx[R, 1], krx[R, 1], bc[R, 3], ALU.mult).then_inc(dve_chain, 1)
            dve.wait_ge(dve_chain, seen.upto(dve_chain))
            V.tensor_tensor(krx[R, 0], krx[R, 0], krx[R, 1], ALU.add).then_inc(dve_chain, 1)
            dve.wait_ge(dve_chain, seen.upto(dve_chain))
            N = slice(0, 64)

            def project(h, part):
                q, k = qn[:, h % 2], kn[:, h % 2]
                if part == 0:
                    dve.wait_ge(head_root, seen.upto(head_root))
                    V.scalar_tensor_tensor(q[N, t0:T], q_raw[N, t0:T], pcol("qhw", N), h_rt[N, 0, t0:T], ALU.mult, ALU.mult)
                    V.scalar_tensor_tensor(k[N, :], k_raw[N, :], pcol("khw", N), h_rt[N, 1], ALU.mult, ALU.mult)
                    V.tensor_tensor(q_raw[R, t0:T], q_raw[R, t0:T], bc[R, 0, t0:T], ALU.mult).then_inc(dve_chain, 1)
                    dve.wait_ge(dve_chain, seen.upto(dve_chain))
                else:
                    V.tensor_tensor(q_rot[R, t0:T], q_rot[R, t0:T], bc[R, 1, t0:T], ALU.mult).then_inc(dve_chain, 1)
                    dve.wait_ge(dve_chain, seen.upto(dve_chain))
                    V.tensor_tensor(k[R, :], krx[R, 0], h_rt[R, 1], ALU.mult)
                    V.tensor_tensor(q_raw[R, t0:T], q_raw[R, t0:T], q_rot[R, t0:T], ALU.add).then_inc(dve_chain, 1)
                    dve.wait_ge(dve_chain, seen.upto(dve_chain))
                    V.tensor_tensor(q[R, t0:T], q_raw[R, t0:T], h_rt[R, 0, t0:T], ALU.mult).then_inc(dve_chain, 1)
                    dve.wait_ge(dve_chain, seen.upto(dve_chain))
                    dve.sem_inc(head_ready, 1)

            units = [(s, n, q) for s, n, _ in own for q in range(n // P)]
            u = [0]

            def row_max(i):
                dve.wait_ge(scores_ready, seen.upto(scores_ready))
                s, f, b = units[i][0], score_bank[l][u[0] + i], (u[0] + i) % 2
                src = psA[:, f:f + 2, :].rearrange("p b n -> p (b n)")[:, 0:T] if s else psA[:, f:f + 2, 0:P]
                V.tensor_reduce(small[:, 48 + b:49 + b], src, AX.X if s else AX.XY, ALU.max, negate=True).then_inc(negmax_ready, 1)
                dve.wait_ge(negmax_ready, seen.upto(negmax_ready))

            def normalise(i, nkeys):
                dve.wait_ge(exp_done, seen.upto(exp_done))
                r = small[:, 50 + i % 2:51 + i % 2]
                V.reciprocal(r, r).then_inc(dve_chain, 1)
                dve.wait_ge(dve_chain, seen.upto(dve_chain))
                V.tensor_scalar(probs[:, i % 2, 0:nkeys], probs[:, i % 2, 0:nkeys], r, None, ALU.mult).then_inc(probs_ready, 1)
                dve.wait_ge(probs_ready, seen.upto(probs_ready))

            def attend(h):
                row_max(0)
                for i, (s, n, q) in enumerate(units):
                    normalise(u[0] + i, T if s else NCTX)
                    if i + 1 < len(units):
                        row_max(i + 1)
                    if i == 3 and h + 1 < BH:
                        project(h + 1, 0)
                    if i == min(4, len(units) - 1) and h + 1 < BH:
                        project(h + 1, 1)
                u[0] += len(units)
                for s, n, _ in own:
                    f = seen.bank(psum_V_full)
                    dve.wait_ge(psum_V_full, seen.upto(psum_V_full, 1))
                    r = slice(64 * (h % 2), 64 * (h % 2) + 64)
                    V.tensor_copy(mixF[r, 2 + h // 2, s:s + n], psV[r, f, 0:n]).then_inc(psum_V_free, 1)
                    dve.wait_ge(psum_V_free, seen.upto(psum_V_free, 1))

            project(0, 0)
            project(0, 1)
            for h in range(BH):
                attend(h)
                if l == 0:
                    f = seen.bank(psum_V_full)
                    dve.wait_ge(psum_V_full, seen.upto(psum_V_full, 1))
                    k = MOD_LATER // BH
                    n = slice(MOD_FIRST + h * k, MOD_FIRST + (h + 1) * k)
                    V.tensor_tensor(mod[:, n, :], psV[:, f, 0:2 * k].rearrange("p (n j) -> p n j", j=2),
                                    bm[:, n].unsqueeze(2).broadcast_to([P, k, 2]), ALU.add).then_inc(psum_V_free, 1)
                    dve.wait_ge(psum_V_free, seen.upto(psum_V_free, 1))
            if l == 0:
                for b in range(RAW):
                    seen.n[raw_landed[b]] += 16 * MOD_LATER // RAW

        def mix_split(l):
            t0 = segs_of(l, False)[-1][0]
            for k in range(KD):
                V.tensor_copy(mix_r[:, k % 2, t0:T], mixF[:, k, t0:T]).then_inc(dve_chain, 1)
                dve.wait_ge(dve_chain, seen.upto(dve_chain))
                V.tensor_tensor(h_lo[:, k, t0:T], mixF[:, k, t0:T], mix_r[:, k % 2, t0:T].bitcast(F32), ALU.subtract).then_inc(mix_lo, 1)
                dve.wait_ge(mix_lo, seen.upto(mix_lo))

        def add_gated(l, part, k, f, segs, banks=2):
            for b, (s, n, j) in enumerate(segs):
                ins = V.scalar_tensor_tensor(xT[:, k, s:s + n], psV[:, f + b, 0:n], mod[:, l * 48 + part * 8 + k, j:j + 1],
                                             xT[:, k, s:s + n], ALU.mult, ALU.add)
            ins.then_inc(psum_V_free, banks)
            dve.wait_ge(psum_V_free, seen.upto(psum_V_free, banks))

        def x_signal():
            dve.sem_inc(x_ready, 1)

        def route(l):
            segs = segs_of(l, False)
            tts = [(b, tt, tt - s // P) for b, (s, n, _) in enumerate(segs) for tt in range(s // P, (s + n) // P)]
            for t in range(WQ_TILES):
                split_to(min(WQ0[l] + t + 3, EX0[l] + 2))
                f = seen.bank(psum_V_full)
                dve.wait_ge(psum_V_full, seen.upto(psum_V_full, 2))

                def s_of(b, j):
                    return psV[:, f + b, j * P:(j + 1) * P]

                for b, tt, j in tts:
                    ins = V.max(sv[:, tt, t, 0:8], s_of(b, j))
                ins.then_inc(dve_chain, 1)
                dve.wait_ge(dve_chain, seen.upto(dve_chain))
                for b, tt, j in tts:
                    V.max_index(si[:, tt, t, 0:8], sv[:, tt, t, 0:8], s_of(b, j))
                    ins = V.match_replace(s_work[:, tt], sv[:, tt, t, 0:8], s_of(b, j), -3.0e38)
                ins.then_inc(psum_V_free, 2)
                dve.wait_ge(psum_V_free, seen.upto(psum_V_free, 2))
                for b, tt, j in tts:
                    ins = V.max(sv[:, tt, t, 8:16], s_work[:, tt])
                ins.then_inc(dve_chain, 1)
                dve.wait_ge(dve_chain, seen.upto(dve_chain))
                for b, tt, j in tts:
                    ins = V.max_index(si[:, tt, t, 8:16], sv[:, tt, t, 8:16], s_work[:, tt])
            ins.then_inc(dve_chain, 1)
            dve.wait_ge(dve_chain, seen.upto(dve_chain))
            tt0 = segs[-1][0] // P
            V.tensor_copy(si_f[:, tt0:], si[:, tt0:]).then_inc(dve_chain, 1)
            dve.wait_ge(dve_chain, seen.upto(dve_chain))
            for tt in range(tt0, NTT):
                svt = sv[:, tt].rearrange("p (h two) a -> p h two a", two=2)
                sit = si_f[:, tt].rearrange("p (h two) a -> p h two a", two=2)
                V.tensor_tensor(cand[:].rearrange("p h (a b) -> p h a b", b=TOPK),
                                         svt[:, :, 0, :].unsqueeze(3).broadcast_to([P, PH, TOPK, TOPK]),
                                         svt[:, :, 1, :].unsqueeze(2).broadcast_to([P, PH, TOPK, TOPK]), ALU.add).then_inc(dve_chain, 1)
                dve.wait_ge(dve_chain, seen.upto(dve_chain))
                for h in range(PH):
                    ins = V.max(best[:, h, 0:8], cand[:, h])
                ins.then_inc(dve_chain, 1)
                dve.wait_ge(dve_chain, seen.upto(dve_chain))
                for h in range(PH):
                    V.max_index(best_i[:, h, 0:8], best[:, h, 0:8], cand[:, h])
                    ins = V.match_replace(cand2[:, h], best[:, h, 0:8], cand[:, h], -3.0e38)
                ins.then_inc(dve_chain, 1)
                dve.wait_ge(dve_chain, seen.upto(dve_chain))
                for h in range(PH):
                    ins = V.max(best[:, h, 8:16], cand2[:, h])
                ins.then_inc(dve_chain, 1)
                dve.wait_ge(dve_chain, seen.upto(dve_chain))
                for h in range(PH):
                    ins = V.max_index(best_i[:, h, 8:16], best[:, h, 8:16], cand2[:, h])
                ins.then_inc(dve_chain, 1)
                dve.wait_ge(dve_chain, seen.upto(dve_chain))
                if tt > tt0:
                    dve.wait_ge(sel_copied, seen.upto(sel_copied))
                bi = best_i[:].rearrange("p h k -> p (h k)")
                V.tensor_scalar(ab_i[:, 0], bi, 4, None, ALU.logical_shift_right)
                V.tensor_scalar(ab_i[:, 1], bi, 15, None, ALU.bitwise_and).then_inc(dve_chain, 1)
                dve.wait_ge(dve_chain, seen.upto(dve_chain))
                V.tensor_copy(ab_f[:], ab_i[:]).then_inc(dve_chain, 1)
                dve.wait_ge(dve_chain, seen.upto(dve_chain))
                V.tensor_copy(small[:, 128:136], best[:, :, 0]).then_inc(dve_chain, 1)
                dve.wait_ge(dve_chain, seen.upto(dve_chain))
                V.tensor_tensor(best[:], best[:], small[:, 128:136].unsqueeze(2).broadcast_to([P, PH, TOPK]), ALU.subtract).then_inc(cand_raw, 1)
                dve.wait_ge(cand_raw, seen.upto(cand_raw))
                for two in range(2):
                    V.tensor_tensor(eq[:], ab_f[:, two].unsqueeze(2).broadcast_to([P, P, TOPK]),
                                             iota16.unsqueeze(1).broadcast_to([P, P, TOPK]), ALU.is_equal).then_inc(dve_chain, 1)
                    dve.wait_ge(dve_chain, seen.upto(dve_chain))
                    e4 = eq[:].rearrange("p (h k) a -> p h k a", h=PH)
                    V.tensor_tensor(e4, e4, sit[:, :, two, :].unsqueeze(2).broadcast_to([P, PH, TOPK, TOPK]), ALU.mult).then_inc(dve_chain, 1)
                    dve.wait_ge(dve_chain, seen.upto(dve_chain))
                    V.tensor_reduce(sel[:, two], eq[:], AX.X, ALU.add).then_inc(dve_chain, 1)
                    dve.wait_ge(dve_chain, seen.upto(dve_chain))
                dve.wait_ge(cand_exp, seen.upto(cand_exp))
                V.tensor_reduce(small[:, 136:144], best[:], AX.X, ALU.add).then_inc(dve_chain, 1)
                dve.wait_ge(dve_chain, seen.upto(dve_chain))
                V.reciprocal(small[:, 136:144], small[:, 136:144]).then_inc(dve_chain, 1)
                dve.wait_ge(dve_chain, seen.upto(dve_chain))
                V.tensor_tensor(sel[:, 2].rearrange("p (h k) -> p h k", h=PH), best[:],
                                small[:, 136:144].unsqueeze(2).broadcast_to([P, PH, TOPK]), ALU.mult).then_inc(sel_ready, 1)
                dve.wait_ge(sel_ready, seen.upto(sel_ready))
            dve.wait_ge(sel_copied, seen.upto(sel_copied))

        def build_gates(l):
            tb0 = 0 if l < DEPTH - 1 else NCTX // TB
            base = 3 + (0 if l == 0 else NTB * GROUPS * l)
            with dve.Fori(0, (NTB - tb0) // 2) as i:
                seen.enter(i, {oh_passed: 2 * GROUPS})
                for g in range(2 * GROUPS):
                    dve.wait_ge(oh_passed, seen.at(oh_passed, base + g - 2))
                    t = i * (2 * TB) + (tb0 * TB + 4 * g)
                    V.tensor_tensor(onehot[:, g % 4, 0, 0:2], iota.unsqueeze(1).broadcast_to([P, 2, P]),
                                    idxT[:, 0, bass.ds(t, 2)].unsqueeze(2).broadcast_to([P, 2, P]), ALU.is_equal)
                    for j in range(4):
                        ins = V.tensor_scalar(onehot[:, g % 4, 1, j], iota, idxT[:, 1, bass.ds(t + j, 1)],
                                              idxT[:, 2, bass.ds(t + j, 1)], ALU.is_equal, ALU.mult)
                    ins.then_inc(oh_ready, 1)
            seen.leave((NTB - tb0) // 2)

        def experts(l):
            segs = segs_of(l, False)
            t0 = segs[-1][0]
            banks = len(segs)

            def weight(c, par_):
                dve.wait_ge(gelu_ready, seen.upto(gelu_ready))
                if c == 0:
                    dve.wait_ge(g_landed[par_], seen.upto(g_landed[par_], 16))
                g = gel[:, c, t0:T]
                g3 = g.rearrange("p (b t) -> p b t", t=TB)
                V.tensor_tensor(g3, g3, g_in[:, par_, t0 // TB:, c * TB:(c + 1) * TB], ALU.mult).then_inc(dve_chain, 1)
                dve.wait_ge(dve_chain, seen.upto(dve_chain))
                V.tensor_copy(W_hi[:, par_, c, t0:T], g).then_inc(dve_chain, 1)
                dve.wait_ge(dve_chain, seen.upto(dve_chain))
                V.tensor_tensor(W_lo[:, par_, c, t0:T], g, W_hi[:, par_, c, t0:T].bitcast(F32), ALU.subtract).then_inc(w_ready, 1)
                dve.wait_ge(w_ready, seen.upto(w_ready))

            def add_chunk(k):
                f = seen.bank(psum_V_full)
                dve.wait_ge(psum_V_full, seen.upto(psum_V_full, banks))
                add_gated(l, 5, k, f, segs, banks)

            def body(now):
                base = splits[0]
                weight(1, now)
                split_to(base + 2)
                weight(0, 1 - now)
                for k in range(KD):
                    if k in (2, 5):
                        split_to(splits[0] + 1)
                    add_chunk(k)

            weight(0, 0)
            split_to(EX0[l] + 4)
            body(0)
            rate = {raw_landed[0]: 64, raw_landed[1]: 64, tile_passed: 8, hi_done: 8, lo_done: 8, w_ready: 4, gelu_ready: 4,
                    g_landed[0]: 16, g_landed[1]: 16, psum_V_full: 16 * banks, psum_V_free: 16 * banks, dve_chain: 8}
            first = splits[0]
            with dve.Fori(0, (NSUPER - 2) // 2) as i:
                seen.enter(i, rate)
                body(1)
                body(0)
            seen.leave((NSUPER - 2) // 2)
            splits[0] = first + 4 * (NSUPER - 2)
            weight(1, 1)
            split_to(min(EX0[l] + EXPERT_TILES + 2, N_TILES))
            for k in range(KD):
                add_chunk(k)

        dve.wait_ge(inputs_landed, seen.upto(inputs_landed, 16 * 13))
        V.memset(small[:, 150:151], EPS)
        V.memset(small[:, 151:152], BQK * EPS).then_inc(dve_chain, 1)
        dve.wait_ge(dve_chain, seen.upto(dve_chain))

        f = seen.bank(psum_V_full)
        dve.wait_ge(psum_V_full, seen.upto(psum_V_full, 4))
        V.tensor_tensor(mod[:, 0:MOD_FIRST, :], psV[:, f, 0:2 * MOD_FIRST].rearrange("p (n j) -> p n j", j=2),
                        bm[:, 0:MOD_FIRST].unsqueeze(2).broadcast_to([P, MOD_FIRST, 2]), ALU.add).then_inc(psum_V_free, 4)
        dve.wait_ge(psum_V_free, seen.upto(psum_V_free, 4))

        def norm_scales(l, w):
            name = ("ln1", "ln2")[w]
            scale = mod[:, l * MOD_TILES + w * 24 + 8:l * MOD_TILES + w * 24 + 16, :]
            V.scalar_tensor_tensor(modA[:, l, w], scale, 1.0,
                                   par[:, l, PAR[name]:PAR[name] + 8].unsqueeze(2).broadcast_to([P, KD, 2]),
                                   ALU.add, ALU.mult).then_inc(dve_chain, 1)
            dve.wait_ge(dve_chain, seen.upto(dve_chain))

        V.tensor_tensor(lb[:, 2, :], lb[:, 0, :], lb[:, 1, :], ALU.max).then_inc(dve_chain, 1)
        dve.wait_ge(dve_chain, seen.upto(dve_chain))
        V.tensor_tensor(lb[:, 3, :], lb[:, 0, :], lb[:, 2, :], ALU.subtract)
        V.tensor_tensor(lb[:, 4, :], lb[:, 1, :], lb[:, 2, :], ALU.subtract).then_inc(dve_chain, 1)
        dve.wait_ge(dve_chain, seen.upto(dve_chain))
        dve.sem_inc(mod_ready, 1)
        dve.wait_ge(lb_exp, seen.upto(lb_exp))
        V.tensor_tensor(lb[:, 2, :], lb[:, 3, :], lb[:, 4, :], ALU.add).then_inc(dve_chain, 1)
        dve.wait_ge(dve_chain, seen.upto(dve_chain))
        V.reciprocal(lb[:, 2, :], lb[:, 2, :]).then_inc(dve_chain, 1)
        dve.wait_ge(dve_chain, seen.upto(dve_chain))
        V.tensor_tensor(lb[:, 5, :], lb[:, 4, :], lb[:, 2, :], ALU.mult)
        V.tensor_tensor(lb[:, 6, :], lb[:, 3, :], lb[:, 2, :], ALU.mult).then_inc(dve_chain, 1)
        dve.wait_ge(dve_chain, seen.upto(dve_chain))
        x_signal()
        for l in range(DEPTH):
            norm_scales(l, 0)
            norm(l, 0)
            for t in range(IN_TILES):
                split_to(min(IN0[l] + t + 3, OUT0[l]))
            dve.wait_ge(proj_ready, seen.upto(proj_ready))
            gated_mlp(l)
            hgrn(l)
            attention(l)
            mix_split(l)
            segs = segs_of(l, False)
            for t in range(OUT_TILES):
                split_to(OUT0[l] + t + 3)
                f = seen.bank(psum_V_full)
                dve.wait_ge(psum_V_full, seen.upto(psum_V_full, 2))
                add_gated(l, 2, t, f, segs)
            x_signal()
            norm_scales(l, 1)
            norm(l, 1)
            route(l)
            build_gates(l)
            experts(l)
            x_signal()


def shape_constants():
    p = np.arange(P)
    ident = np.eye(P)
    ones = np.ones((P, P))
    bones = (p[:, None] // 64 == p[None, :] // 64).astype(float)
    iota = np.broadcast_to(p[None, :], (P, P))
    iota16 = np.broadcast_to(np.arange(TOPK)[None, :], (P, TOPK))
    s, t = np.arange(64)[:, None], np.arange(64)[None, :]
    masks = np.zeros((P, 2, NLB, 64))
    for li, m in enumerate(LEVELS[1:]):
        same = s // (2 * m) == t // (2 * m)
        left, right = s // m % 2 == 0, t // m % 2 == 1
        masks[:, 0, li] = np.tile(same & left & right, (2, 1))
        masks[:, 1, li] = np.tile(same & ~left & ~right, (2, 1))
    masks[:, :, NLB - 1] = np.tile(s == t, (2, 1))[:, None, :]
    resets = np.broadcast_to((np.arange(T + 1) % P != 0)[None, :], (P, T + 1))
    f32 = np.float32
    n = np.arange(NLAT)
    inv = (f32(10000.0) ** (-np.arange(BR // 4, dtype=f32) / f32(BR // 4))).astype(f32)
    r = np.arange(BR)
    where = np.where(r[:, None] // 16 == 0, n[None, :] // 64, n[None, :] % 64).astype(f32)
    ang = (where * inv[r % 8][:, None]).astype(f32)
    sign = np.where(r % 16 < 8, -1.0, 1.0)[:, None]
    rope = np.zeros((P, 2, T))
    rope[64:96, 0, :NCTX] = 1.0
    rope[64:96, 0, NCTX:] = np.cos(ang)
    rope[64:96, 1, NCTX:] = np.sin(ang) * sign
    parts = [ident, ones, bones, iota, iota16, masks.reshape(P, -1), resets, rope.reshape(P, -1)]
    return np.ascontiguousarray(np.concatenate(parts, axis=1).astype(f32))


def tiles_of(w):
    d_in, n = w.shape
    return w.reshape(d_in // P, P, n // P, P).transpose(2, 1, 0, 3).reshape(n // P, P, d_in)


def columns(v):
    return np.moveaxis(v.reshape(v.shape[:-1] + (-1, P)), -1, 0)


def kernel(x, c, ctx, c_ctx, ln1_w, ln2_w, w_mod, b_mod, w_in, w_out, a_norm_w, a_w_s, a_b_s,
           b_q_norm_w, b_w_uq, b_kv_norm_w, b_w_ukv, b_q_head_norm_w, b_k_head_norm_w,
           c_lb_logits, c_out_norm_w, p_w_q, p_sub_keys, p_u, p_v):
    import concourse.bacc as bacc
    from concourse.bass_utils import run_bass_kernel_spmd

    A = np.asarray
    (x, c, ctx, c_ctx, ln1_w, ln2_w, w_mod, b_mod, w_in, w_out, a_norm_w, a_w_s, a_b_s, b_q_norm_w, b_w_uq,
     b_kv_norm_w, b_w_ukv, b_q_head_norm_w, b_k_head_norm_w, c_lb_logits, c_out_norm_w, p_w_q, p_sub_keys,
     p_u, p_v) = map(A, (x, c, ctx, c_ctx, ln1_w, ln2_w, w_mod, b_mod, w_in, w_out, a_norm_w, a_w_s, a_b_s,
                         b_q_norm_w, b_w_uq, b_kv_norm_w, b_w_ukv, b_q_head_norm_w, b_k_head_norm_w,
                         c_lb_logits, c_out_norm_w, p_w_q, p_sub_keys, p_u, p_v))

    partner = np.arange(BR) ^ 8
    offs = np.cumsum([0, 256, 256, 256, 128, 32, 256, 256, 256, 256, 256])
    a_u, a_v, b_q, b_kv, b_kr, c_q, c_f, c_b, c_i, c_g = [np.arange(offs[i], offs[i + 1]) for i in range(10)]
    kr_tile = np.concatenate([b_kr, b_kr, b_kr, b_kr[partner]])
    in_cols = np.concatenate([a_u, b_q, b_kv, kr_tile, c_q, c_f, c_b, c_g, a_v, c_i])
    tiles = np.empty((N_TILES, P, D), np.float32)
    at = 0

    def put(block):
        nonlocal at
        tiles[at:at + len(block)] = block
        at += len(block)

    for l in range(DEPTH):
        put(tiles_of(w_in[l][:, in_cols]))
        put(tiles_of(w_out[l]))
        put(tiles_of(p_w_q[l]))
        u = p_u[l].reshape(NK, P, KD, P).transpose(0, 3, 2, 1).reshape(NK, P, D)
        v = p_v[l].reshape(NK, P, D)
        block = tiles[at:at + EXPERT_TILES]
        block[0:2] = u[0:2]
        rest = block[2:EXPERT_TILES - 2].reshape(NSUPER - 1, 4, P, D)
        rest[:, 0:2] = u[2:].reshape(NSUPER - 1, 2, P, D)
        rest[:, 2:4] = v[:-2].reshape(NSUPER - 1, 2, P, D)
        block[EXPERT_TILES - 2:] = v[-2:]
        at += EXPERT_TILES
    assert at == N_TILES
    mods = np.concatenate([tiles_of(w_mod[l]) for l in range(DEPTH)])
    mod_tiles = mods[MOD_FIRST:]
    mod_pairs = mods[:MOD_FIRST].reshape(MOD_FIRST // 2, 2, P, KD, P).transpose(0, 2, 1, 3, 4)

    x_in = np.concatenate([ctx[0].T, x[0].T], axis=1).reshape(KD, P, T).transpose(1, 0, 2)
    cond = np.stack([c[0].reshape(KD, P).T, c_ctx.reshape(KD, P).T], axis=2)
    params = np.zeros((P, DEPTH, NPAR), np.float32)
    for l in range(DEPTH):
        params[:, l, 0:8] = columns(ln1_w[l])
        params[:, l, 8:16] = columns(ln2_w[l])
        params[:, l, 16:18] = columns(b_q_norm_w[l])
        params[:, l, 18:19] = columns(b_kv_norm_w[l])
        params[0:BQK, l, 19] = b_q_head_norm_w[l]
        params[0:BQK, l, 20] = b_k_head_norm_w[l]
        params[64:96, l, 21] = b_q_head_norm_w[l][64:][partner]
        params[64:96, l, 22] = b_k_head_norm_w[l][64:][partner]
        params[:, l, 23] = np.tile(c_out_norm_w[l], 2)
    bmod = columns(b_mod.reshape(-1))
    lblog = columns(c_lb_logits).reshape(P, DEPTH, 4)
    bias = np.repeat(a_b_s.reshape(DEPTH, 2, 2, 1, P), 64, axis=3).reshape(DEPTH, 2, P, P).transpose(0, 2, 1, 3)
    arow = np.concatenate([bias.reshape(DEPTH, P, 256), np.broadcast_to(a_norm_w[:, None, :], (DEPTH, P, 256))], axis=2)
    aws = a_w_s.transpose(0, 3, 1, 2)
    uq = b_w_uq.reshape(DEPTH, 2, P, BH, BQK).transpose(0, 2, 1, 3, 4)
    uq_rot = uq[..., 64:][..., partner]
    ukv = b_w_ukv.reshape(DEPTH, P, BH, BN + BV)
    bw = np.concatenate([uq.reshape(DEPTH, P, 1536), uq_rot.reshape(DEPTH, P, 512),
                         ukv[..., :BN].reshape(DEPTH, P, 512), ukv[..., BN:].reshape(DEPTH, P, 512)], axis=2)
    keys = p_sub_keys.reshape(DEPTH, WQ_TILES, NK, P).transpose(0, 3, 1, 2)

    inputs = dict(mod_pairs=mod_pairs, mod_tiles=mod_tiles, tiles=tiles, x_in=x_in, consts=shape_constants(), params=params, bmod=bmod, cond=cond, arow=arow,
                  aws=aws, bw=bw, keys=keys, lblog=lblog)
    inputs = {k: np.ascontiguousarray(v) for k, v in inputs.items()}
    nc = bacc.Bacc("TRN2", target_bir_lowering=False, num_devices=1)
    args = {k: nc.dram_tensor(k, v.shape, F32, kind="ExternalInput").ap() for k, v in inputs.items()}
    args["gates"] = nc.dram_tensor("gates", (NTB, P, NK, TB), F32, kind="Internal").ap()
    args["out"] = nc.dram_tensor("out", (P, KD, NLAT), F32, kind="ExternalOutput").ap()
    build_program(nc, **args)
    r = run_bass_kernel_spmd(nc, [inputs], core_ids=[0])
    y = r.results[0]["out"]
    return y.transpose(1, 0, 2).reshape(1, D, NLAT).transpose(0, 2, 1)
```
